# Optimizing a Trainium2 kernel written in Bass

```python
import jax
import jax.numpy as jnp
from jax import lax
import numpy as np

D_MODEL = 1024
BATCH = 1
SEQ = 256
DEPTH = 2

POOL_WINDOWS = (2, 4, 8, 16)
POOL_GROUPS = 4
POOL_GROUP_W = D_MODEL // 16
POOL_W = POOL_GROUPS * POOL_GROUP_W
CONV_W = D_MODEL // 4
CONV_K = 31
RWKV_HEAD = 64
RWKV_W = D_MODEL // 2
RWKV_HEADS = RWKV_W // RWKV_HEAD
W_LORA = 32
A_LORA = 32
V_LORA = 16
G_LORA = 64
RWKV_COLS = 3 * RWKV_W + W_LORA + A_LORA + G_LORA
RWKV_SPLITS = (RWKV_W, 2 * RWKV_W, 3 * RWKV_W, 3 * RWKV_W + W_LORA, 3 * RWKV_W + W_LORA + A_LORA)
N_BRANCH = 3
OFF_CONV = POOL_W
OFF_RWKV = OFF_CONV + 2 * CONV_W
OFF_GATE = OFF_RWKV + RWKV_COLS
OFF_VRES = OFF_GATE + N_BRANCH * D_MODEL
IN_COLS = OFF_VRES
D_FF = 2816
N_EXPERTS = 8
TOP_K = 2
D_FF_EXPERT = 3584
N_DENSE = (DEPTH + 1) // 2
N_MOE = DEPTH // 2
RMS_EPS = 1e-6
LN_EPS = 1e-5
GN_EPS = 64e-5

kernel_name = 'hybrid_pool_conv_rwkv7_moe_adaln'

def _rms(x, g):
    xf = x.astype(jnp.float32)
    y = xf * lax.rsqrt(jnp.mean(xf * xf, axis=-1, keepdims=True) + RMS_EPS)
    return (y * g.astype(jnp.float32)).astype(x.dtype)

def _ada(x, c, w, b, g):
    mod = jax.nn.silu(c) @ w + b
    shift, scale, gate = jnp.split(mod, 3, axis=-1)
    h = _rms(x, g) * (1 + scale[:, None, :]) + shift[:, None, :]
    return h, gate[:, None, :]

def _shift(z):
    return jnp.pad(z, ((0, 0), (1, 0), (0, 0)))[:, :-1]

def _pool_mixer(u, pool_w, pool_scale, pool_proj):
    b_, s_, _ = u.shape
    uf = u.astype(jnp.float32).reshape(b_, s_, POOL_GROUPS, POOL_GROUP_W)
    cs = jnp.cumsum(uf, axis=1)
    pos = jnp.arange(1, s_ + 1, dtype=jnp.float32)
    outs = []
    for gi, win in enumerate(POOL_WINDOWS):
        csg = cs[:, :, gi]
        lag = jnp.pad(csg, ((0, 0), (win, 0), (0, 0)))[:, :s_]
        cnt = jnp.minimum(pos, float(win))[None, :, None]
        outs.append((csg - lag) / cnt - uf[:, :, gi])
    p = jnp.stack(outs, axis=2).astype(u.dtype)
    p = jnp.einsum('bsgc,gcd->bsgd', p, pool_w).reshape(b_, s_, POOL_W) * pool_scale
    return p @ pool_proj

def _conv_module(z, conv_w, conv_b, ln_g, ln_b, proj):
    a, b = jnp.split(z, 2, axis=-1)
    u = a * jax.nn.sigmoid(b)
    u = lax.conv_general_dilated(u, conv_w[:, None, :].astype(u.dtype), (1,), ((CONV_K - 1, 0),),
                                 dimension_numbers=('NWC', 'WIO', 'NWC'),
                                 feature_group_count=CONV_W) + conv_b
    uf = u.astype(jnp.float32)
    mean = jnp.mean(uf, axis=-1, keepdims=True)
    var = jnp.mean(jnp.square(uf - mean), axis=-1, keepdims=True)
    un = ((uf - mean) * lax.rsqrt(var + LN_EPS)).astype(u.dtype) * ln_g + ln_b
    return jax.nn.silu(un) @ proj

def _wkv7_scan(r, w, k, v, kk, a):
    def step(state, inp):
        r_t, w_t, k_t, v_t, kk_t, a_t = inp
        sa = jnp.einsum('bhij,bhj->bhi', state, -kk_t)
        state = (state * w_t[:, :, None, :]
                 + sa[..., None] * (kk_t * a_t)[:, :, None, :]
                 + v_t[..., None] * k_t[:, :, None, :])
        return state, jnp.einsum('bhij,bhj->bhi', state, r_t)
    b_, s_, h_, n_ = r.shape
    s0 = jnp.zeros((b_, h_, n_, n_), jnp.float32)
    xs = tuple(jnp.moveaxis(t, 1, 0) for t in (r, w, k, v, kk, a))
    _, out = lax.scan(step, s0, xs)
    return jnp.moveaxis(out, 0, 1)

def _rwkv7_branch(zr, mu, w0, w2, a0, a2, g2, k_scale, k_a, r_k, lnx_g, lnx_b, proj, vres):
    f32 = jnp.float32
    b_, s_, _ = zr.shape
    hd = lambda t: t.astype(f32).reshape(b_, s_, RWKV_HEADS, RWKV_HEAD)
    zr = zr + (_shift(zr) - zr) * mu
    r, k, v, wd, ad, gd = jnp.split(zr, RWKV_SPLITS, axis=-1)
    w = -jax.nn.softplus(-(w0 + jnp.tanh(wd) @ w2).astype(f32)) - 0.5
    decay = jnp.exp(-jnp.exp(w))
    a = jax.nn.sigmoid((a0 + ad @ a2).astype(f32))
    g = jax.nn.sigmoid(gd) @ g2
    if vres is not None:
        v_first, vd, v0, v2 = vres
        v = v + (v_first - v) * jax.nn.sigmoid(v0 + vd @ v2)
    kk = hd(k * k_scale)
    kk = kk / jnp.maximum(jnp.sqrt(jnp.sum(kk * kk, axis=-1, keepdims=True)), 1e-12)
    kh = hd(k * (1 + (a - 1) * k_a))
    rh = hd(r)
    vh = hd(v)
    o = _wkv7_scan(rh, hd(decay), kh, vh, kk, hd(a))
    mean = jnp.mean(o, axis=-1, keepdims=True)
    var = jnp.mean(jnp.square(o - mean), axis=-1, keepdims=True)
    o = ((o - mean) * lax.rsqrt(var + GN_EPS)).reshape(b_, s_, RWKV_W) * lnx_g + lnx_b
    bonus = jnp.sum(rh * kh * r_k.reshape(RWKV_HEADS, RWKV_HEAD), axis=-1, keepdims=True) * vh
    o = (o + bonus.reshape(b_, s_, RWKV_W)) * g
    return o.astype(zr.dtype) @ proj, v

def _swiglu(h, w1, w3, w2):
    return (jax.nn.silu(h @ w1) * (h @ w3)) @ w2

def _moe(h, router, w1, w3, w2):
    b_, s_, d_ = h.shape
    t = h.reshape(-1, d_)
    logits = (t @ router).astype(jnp.float32)
    vals, idx = lax.top_k(logits, TOP_K)
    wts = jax.nn.softmax(vals, axis=-1)
    gate = jnp.sum(jax.nn.one_hot(idx, N_EXPERTS, dtype=jnp.float32) * wts[..., None], axis=1).astype(h.dtype)
    y = jnp.zeros_like(t)
    for e in range(N_EXPERTS):
        y = y + gate[:, e:e + 1] * _swiglu(t, w1[e], w3[e], w2[e])
    return y.reshape(b_, s_, d_)

def setup_inputs(seed: int = 0) -> dict:
    key = jax.random.key(seed)
    ks = iter(jax.random.split(key, 64))
    nrm = lambda shape, s: jax.random.normal(next(ks), shape, jnp.float32) * s
    uni = lambda shape: jax.random.uniform(next(ks), shape, jnp.float32)
    D = D_MODEL
    L = DEPTH
    LV = DEPTH - 1
    w0 = jnp.broadcast_to(jnp.linspace(-6.0, 1.0, RWKV_W, dtype=jnp.float32), (L, RWKV_W)) + nrm((L, RWKV_W), 0.1)
    return {
        'x': nrm((BATCH, SEQ, D), 1.0),
        'c': nrm((BATCH, D), 1.0),
        'ada_w': nrm((L, 2, D, 3 * D), 0.5 * D ** -0.5),
        'ada_b': nrm((L, 2, 3 * D), 0.01),
        'norm_g': 1.0 + nrm((L, 2, D), 0.02),
        'w_in': nrm((L, D, IN_COLS), D ** -0.5),
        'pool_w': nrm((L, POOL_GROUPS, POOL_GROUP_W, POOL_GROUP_W), POOL_GROUP_W ** -0.5),
        'pool_scale': 1.0 + nrm((L, POOL_W), 0.1),
        'pool_proj': nrm((L, POOL_W, D), POOL_W ** -0.5),
        'conv_w': nrm((L, CONV_K, CONV_W), CONV_K ** -0.5),
        'conv_b': nrm((L, CONV_W), 0.01),
        'conv_ln_g': 1.0 + nrm((L, CONV_W), 0.02),
        'conv_ln_b': nrm((L, CONV_W), 0.01),
        'conv_proj': nrm((L, CONV_W, D), CONV_W ** -0.5),
        'rwkv_mu': uni((L, RWKV_COLS)),
        'rwkv_w0': w0,
        'rwkv_w2': nrm((L, W_LORA, RWKV_W), 0.5 * W_LORA ** -0.5),
        'rwkv_a0': nrm((L, RWKV_W), 0.1),
        'rwkv_a2': nrm((L, A_LORA, RWKV_W), 0.5 * A_LORA ** -0.5),
        'rwkv_g2': nrm((L, G_LORA, RWKV_W), G_LORA ** -0.5),
        'rwkv_kk_scale': 0.85 + nrm((L, RWKV_W), 0.05),
        'rwkv_ka': 1.0 + nrm((L, RWKV_W), 0.05),
        'rwkv_rk': nrm((L, RWKV_W), 0.1),
        'rwkv_lnx_g': 1.0 + nrm((L, RWKV_W), 0.02),
        'rwkv_lnx_b': nrm((L, RWKV_W), 0.01),
        'rwkv_proj': nrm((L, RWKV_W, D), RWKV_W ** -0.5),
        'vres_w_down': nrm((LV, D, V_LORA), D ** -0.5),
        'vres_mu': uni((LV, V_LORA)),
        'vres_v0': 1.0 + nrm((LV, RWKV_W), 0.1),
        'vres_v2': nrm((LV, V_LORA, RWKV_W), 0.5 * V_LORA ** -0.5),
        'w_o': nrm((L, D, D), D ** -0.5),
        'ffn_w1': nrm((N_DENSE, D, D_FF), D ** -0.5),
        'ffn_w3': nrm((N_DENSE, D, D_FF), D ** -0.5),
        'ffn_w2': nrm((N_DENSE, D_FF, D), D_FF ** -0.5),
        'moe_router': nrm((N_MOE, D, N_EXPERTS), D ** -0.5),
        'moe_w1': nrm((N_MOE, N_EXPERTS, D, D_FF_EXPERT), D ** -0.5),
        'moe_w3': nrm((N_MOE, N_EXPERTS, D, D_FF_EXPERT), D ** -0.5),
        'moe_w2': nrm((N_MOE, N_EXPERTS, D_FF_EXPERT, D), D_FF_EXPERT ** -0.5),
        'final_norm_g': 1.0 + nrm((D,), 0.02),
    }

def reference(x, c, ada_w, ada_b, norm_g, w_in, pool_w, pool_scale, pool_proj,
              conv_w, conv_b, conv_ln_g, conv_ln_b, conv_proj,
              rwkv_mu, rwkv_w0, rwkv_w2, rwkv_a0, rwkv_a2, rwkv_g2, rwkv_kk_scale, rwkv_ka,
              rwkv_rk, rwkv_lnx_g, rwkv_lnx_b, rwkv_proj,
              vres_w_down, vres_mu, vres_v0, vres_v2, w_o,
              ffn_w1, ffn_w3, ffn_w2, moe_router, moe_w1, moe_w3, moe_w2, final_norm_g):
    v_first = None
    for l in range(DEPTH):
        h, gate = _ada(x, c, ada_w[l, 0], ada_b[l, 0], norm_g[l, 0])
        if l == 0:
            w_cat = w_in[l]
        else:
            w_cat = jnp.concatenate([w_in[l], vres_w_down[l - 1]], axis=1)
        z = h @ w_cat
        y_pool = _pool_mixer(z[..., :OFF_CONV], pool_w[l], pool_scale[l], pool_proj[l])
        y_conv = _conv_module(z[..., OFF_CONV:OFF_RWKV], conv_w[l], conv_b[l],
                              conv_ln_g[l], conv_ln_b[l], conv_proj[l])
        vres = None
        if l > 0:
            zv = z[..., OFF_VRES:]
            zv = zv + (_shift(zv) - zv) * vres_mu[l - 1]
            vres = (v_first, zv, vres_v0[l - 1], vres_v2[l - 1])
        y_rwkv, v_l = _rwkv7_branch(z[..., OFF_RWKV:OFF_GATE], rwkv_mu[l], rwkv_w0[l], rwkv_w2[l],
                                    rwkv_a0[l], rwkv_a2[l], rwkv_g2[l], rwkv_kk_scale[l], rwkv_ka[l],
                                    rwkv_rk[l], rwkv_lnx_g[l], rwkv_lnx_b[l], rwkv_proj[l], vres)
        if l == 0:
            v_first = v_l
        g_p, g_c, g_r = jnp.split(jax.nn.sigmoid(z[..., OFF_GATE:OFF_VRES]), N_BRANCH, axis=-1)
        merged = g_p * y_pool + g_c * y_conv + g_r * y_rwkv
        x = x + gate * (merged @ w_o[l])
        h, gate = _ada(x, c, ada_w[l, 1], ada_b[l, 1], norm_g[l, 1])
        if l % 2 == 0:
            i = l // 2
            y = _swiglu(h, ffn_w1[i], ffn_w3[i], ffn_w2[i])
        else:
            i = l // 2
            y = _moe(h, moe_router[i], moe_w1[i], moe_w3[i], moe_w2[i])
        x = x + gate * y
    return _rms(x, final_norm_g)


_drawn_inputs = setup_inputs


def setup_inputs(seed=0):
    import zlib

    import numpy as np

    out = dict(_drawn_inputs(seed))
    spreads = {}
    factors = {'norm_g': 4.205,
     'conv_b': 8.0,
     'conv_ln_g': 25.274,
     'conv_ln_b': 50.26,
     'rwkv_w2': 4.633,
     'rwkv_a0': 6.136,
     'rwkv_kk_scale': 17.108,
     'rwkv_ka': 4.654,
     'rwkv_lnx_g': 27.901,
     'rwkv_lnx_b': 47.68,
     'vres_w_down': 3.096,
     'vres_mu': 8.0,
     'vres_v0': 23.855,
     'vres_v2': 3.052,
     'final_norm_g': 24.387}
    for name, (base, spread) in spreads.items():
        noise = np.random.default_rng([zlib.crc32(name.encode()), seed]).standard_normal(out[name].shape)
        drawn = base * np.exp(spread * noise) if base else spread * noise
        out[name] = jnp.asarray(drawn.astype(out[name].dtype))
    for name, factor in factors.items():
        out[name] = (out[name] * factor).astype(out[name].dtype)
    return out
```

```python
from contextlib import ExitStack

import numpy as np

import concourse.bass as bass
from concourse import mybir

P = 128
D = 1024
SEQ = 256
DEPTH = 2
KC = D // P
NT = SEQ // P
CONV_K = 31
NB_RKV = 12
COL_RWKV, COL_GATE = 768, 2432
GATE_R, GATE_P, GATE_C = COL_GATE + 2 * D, COL_GATE, COL_GATE + D
D_FF, D_FFE, NE = 2816, 3584, 8
FB = 256
EB = 512
N_FFB = D_FF // FB
N_EB = D_FFE // EB
N_JOBS = 12
CH = 64
VR = slice(64, 80)
N_RAW = 2
LEVELS = 6
DECAY = float(np.exp(-0.5))
PAD_P, PAD_C = 16, CONV_K - 1
MIX_FILLS = 16

C_ID, C_ONES, C_BONES, C_TRI_S, C_TRI_I, C_LOW0 = (P * i for i in range(6))
C_LVL = 6 * P
C_RANK = C_LVL + LEVELS * P
C_IOTA = C_RANK + P
C_CNT = C_IOTA + P
C_LOW8 = C_CNT + 2 * SEQ
C_EID = C_LOW8 + NE * NE
C_M256 = C_EID + NE
C_ZERO = C_M256 + P
C_END = C_ZERO + 256

PARAMS = [("norm_g", 16), ("ada_b", 48), ("pool_scale", 2), ("conv_w", 2 * CONV_K), ("conv_b", 2),
          ("ln_g", 2), ("ln_b", 2), ("mu", 13), ("a0", 4), ("kk_scale", 4), ("ka", 4),
          ("rk", 4), ("lnx_g", 4), ("lnx_b", 4), ("vmu", 1), ("v0", 4)]
P_OFF = {}
_at = 0
for _n, _w in PARAMS:
    P_OFF[_n] = _at
    _at += _w
P_W = _at
P_C = DEPTH * P_W
P_FG = P_C + KC
P_END = P_FG + KC


def shape_constants():
    i = np.arange(P)
    row, col = i[:, None], i[None, :]
    same = row // CH == col // CH
    c = np.zeros((P, C_END), np.float32)
    c[:, C_ID:C_ID + P] = row == col
    c[:, C_ONES:C_ONES + P] = 1
    c[:, C_BONES:C_BONES + P] = same
    c[:, C_TRI_S:C_TRI_S + P] = same & (row < col)
    c[:, C_TRI_I:C_TRI_I + P] = same & (row <= col)
    for m in range(LEVELS):
        n = 1 << m
        lvl = (row // (2 * n) == col // (2 * n)) & (row % (2 * n) < n) & (col % (2 * n) >= n)
        c[:, C_LVL + m * P:C_LVL + (m + 1) * P] = lvl
    c[:, C_LOW0:C_LOW0 + P] = c[:, C_LVL:C_LVL + P].T
    c[:, C_RANK:C_RANK + P] = row < col
    c[:, C_IOTA:C_IOTA + P] = col
    pos = np.arange(1, SEQ + 1)
    for b in range(2):
        for par in range(2):
            win = 2 ** (2 * b + par + 1)
            c[64 * par:64 * par + 64, C_CNT + b * SEQ:C_CNT + (b + 1) * SEQ] = \
                1.0 / np.minimum(pos, win).astype(np.float32)
    low = (np.arange(NE)[:, None] > np.arange(NE)[None, :]).astype(np.float32)
    c[:, C_LOW8:C_LOW8 + NE * NE] = low.reshape(1, -1)
    c[:, C_EID:C_EID + NE] = np.arange(NE)
    c[:, C_M256:C_M256 + P] = 1.0 / 256
    return c


def build_trunk(nc, x_in, consts, params, ada_w, w_in, pool_w, pool_proj, conv_proj, w0_row,
                w2, a2, g2, rwkv_proj, vres_down, vres_v2, w_o, ffn_w1, ffn_w3, ffn_w2,
                router, moe_w1, moe_w3, moe_w2, out):
    f32, i32 = mybir.dt.float32, mybir.dt.int32
    ALU, ACT, AX = mybir.AluOpType, mybir.ActivationFunctionType, mybir.AxisListType
    ds = bass.ds
    ctx = ExitStack()
    with ctx:
        def sb(name, cols, dt=f32):
            return ctx.enter_context(nc.sbuf_tensor(name, [P, cols], dt))

        def sem(name):
            return ctx.enter_context(nc.semaphore(name))

        def v3(t, a, n, w):
            return t[:, a:a + n * w].rearrange("p (n w) -> p n w", w=w)

        ring = sb("ring", 3 * 4096)
        scr = sb("scr", 3 * 4096)
        e1, e2, a_b, kk_a, gg, bon = (v3(scr, 1024 * i, 4, SEQ) for i in range(6))
        ltm, lvl_l, tinv, tinv_t, p_sb, ak_t = (v3(scr, 6144 + 1024 * i, 8, P) for i in range(6))
        sig_tok = v3(scr, 6144, NT, 512)
        o_state, o_all = e1, e2
        inv4_t = scr[:, 8192:9216]
        inv4 = v3(scr, 8192, 4, SEQ)
        rkv_t = sb("rkv", NB_RKV * SEQ)
        rkv = v3(rkv_t, 0, NB_RKV, SEQ)
        rr, kkv, vv = rkv[:, 0:4, :], rkv[:, 4:8, :], rkv[:, 8:12, :]
        lora_in = sb("lora_in", SEQ)
        vres_in = sb("vres_in", SEQ)
        raw_t = sb("raw", N_RAW * (SEQ + 1))
        raw = v3(raw_t, 0, N_RAW, SEQ + 1)
        v_first = sb("v_first", 4 * SEQ)
        state_t = sb("state", 256)
        state = v3(state_t, 0, 4, 64)
        chunk_decay = sb("chunk_decay", 16)
        x_t = sb("x", KC * SEQ)
        xT = v3(x_t, 0, KC, SEQ)
        h_t = sb("h", KC * SEQ)
        hT = v3(h_t, 0, KC, SEQ)
        merged_t = sb("merged", KC * SEQ)
        merged = v3(merged_t, 0, KC, SEQ)
        yT = merged
        gr_t = sb("gate_r", KC * SEQ)
        gate_r = v3(gr_t, 0, KC, SEQ)
        tokm = v3(gr_t, 0, NT, D)
        pu = sb("pool_u", 2 * (PAD_P + SEQ))
        pa = sb("pool_a", 2 * (PAD_P + SEQ))
        pbuf = sb("pool_b", 2 * (PAD_P + SEQ))
        pu3, pa3, pb3 = (v3(t, 0, 2, PAD_P + SEQ) for t in (pu, pa, pbuf))
        ca_t = sb("conv_a", 2 * (PAD_C + SEQ))
        ca = v3(ca_t, 0, 2, PAD_C + SEQ)
        cb_t = sb("conv_b_", 2 * SEQ)
        cb = v3(cb_t, 0, 2, SEQ)
        cy_t = sb("conv_y", 2 * SEQ)
        cy = v3(cy_t, 0, 2, SEQ)
        sg_t = sb("sg", 2 * SEQ)
        sg = v3(sg_t, 0, 2, SEQ)
        pl = sg
        tmp = sb("tmp", SEQ)
        rstd = sb("rstd", SEQ)
        wide = sb("wide", 6 * 1024)
        ada_ring = v3(wide, 0, 3, 1024)
        ada_acc = wide[:, 3072:6144]
        tok = v3(wide, 0, 4, 512)
        ht_sb = v3(wide, 2048, 4, P)
        akv, g_sb, u_sb = (v3(wide, 2560 + 512 * i, 8, 64) for i in range(3))
        act_sb = v3(wide, 0, 2, 512)
        act_t = v3(wide, 1024, 2, 512)
        sig_sb = v3(wide, 2048, 2, 512)
        y_slot = v3(wide, 3072, 2, D)
        sel = v3(wide, 5120, 4, P)
        sel_g = v3(wide, 5632, 4, P)
        h_sel = v3(rkv_t, 0, 2 * KC, P)
        lora_w = sb("lora_w", 512)
        w0_sb = sb("w0_sb", 512)
        pool_wsb = sb("pool_wsb", 2 * 64)
        sel_t_t = v_first[:, 0:2 * SEQ]
        sel_t = v3(v_first, 0, 2, SEQ)
        cst = sb("cst", C_END)
        par = sb("par", P_END)
        mods_t = sb("mods", 4 * 24)
        mods = v3(mods_t, 0, 4, 24)
        gain_t = sb("gain", 4 * 8)
        gain = v3(gain_t, 0, 4, 8)
        c_sig = sb("c_sig", KC)
        c_silu = sb("c_silu", KC)
        router_sb = sb("router_sb", KC * NE)
        widths = [NT * NE] * 6 + [NT, NT] + [NE] * 3 + [4 * NE] + [NT * N_JOBS] * 2
        starts = [sum(widths[:i]) for i in range(len(widths))]
        (lg, r_cnt, r_sel, r_exp, r_gate, r_rank, r_max, r_den, n_tok, over, prev, onehot, job_rank,
         job_gate) = (pbuf[:, o:o + w] for o, w in zip(starts, widths))
        cmp_t = pu[:, 0:NT * NE * NE]
        cmp2_t = pu[:, NT * NE * NE:2 * NT * NE * NE]
        job_f = sb("job_f", N_JOBS + 4)
        job_i = sb("job_i", N_JOBS + 4, i32)

        ps_t = ctx.enter_context(nc.psum_tensor("ps", [P, 8 * 512], f32))
        ps = ps_t[:, :].rearrange("p (b n) -> p b n", b=8)

        def bank(b, n=512, p0=0, p1=P):
            return ps_t[p0:p1, 512 * b:512 * b + n]

        def cc(col, n=P, p0=0, p1=P):
            return cst[p0:p1, col:col + n]

        def pcol(l, name, i=0, p0=0, p1=P):
            o = l * P_W + P_OFF[name] + i
            return par[p0:p1, o:o + 1]

        ident, ones, bones, mean256 = cc(C_ID), cc(C_ONES), cc(C_BONES), cc(C_M256)
        zeros16 = cst[:, C_ZERO:C_ZERO + 256].bitcast(mybir.dt.bfloat16)


        def places(groups):
            at, first = 0, {}
            for l in range(DEPTH):
                for name, n in groups(l):
                    first[l, name] = at
                    at += n
                first[l, "end"] = at
            return first

        ZA = places(lambda l: [("z", NB_RKV + 1 + l), ("pc", 6), ("a", 4), ("g", 4), ("vres", 4 * l),
                               ("gate_r", KC), ("gate_p", KC), ("gate_c", KC)])
        ZD = places(lambda l: [("kk", 4), ("bonus", 4), ("y_pool", KC), ("y_conv", KC), ("mean", 4),
                               ("var", 4), ("y_rwkv", KC), ("w_o", KC)])

        ZMIX = (0, NB_RKV + 1)
        T_INC = 4 * LEVELS
        SMALL = (16 * 10, 16 * 18)

        def head_col(h):
            return P * (h % 4) + 64 * (h // 4)

        cst_in, par_in, x_in_tok, small_in = sem("cst_in"), sem("par_in"), sem("x_in_tok"), sem("small_in")
        ada_full = [sem(f"ada_full{i}") for i in range(3)]
        ada_free, ada_sum, mod_ps, mods_ready = sem("ada_free"), sem("ada_sum"), sem("mod_ps"), sem("mods_ready")
        ring_full = [sem(f"ring_full{i}") for i in range(3)]
        za_ready, za_done, zd_ready, zd_free = sem("za_ready"), sem("za_done"), sem("zd_ready"), sem("zd_free")
        mix_done, pads_ready = sem("mix_done"), sem("pads_ready")
        x_ready, xsq_ready, ssum_ps, h_ready, xt_ps = sem("x_ready"), sem("xsq_ready"), sem("ssum_ps"), sem("h_ready"), sem("xt_ps")
        c_sig_ready = sem("c_sig_ready")
        pooled, pool_ps, pool_y = sem("pooled"), sem("pool_ps"), sem("pool_y")
        conv_dev, gather_d_ready = sem("conv_dev"), sem("gather_d_ready")
        conv_u, conv_mean, conv_sq, conv_var, conv_un, conv_sg, conv_y = (
            sem(n) for n in ("conv_u", "conv_mean", "conv_sq", "conv_var", "conv_un", "conv_sg", "conv_y"))
        lora_ready, sigt_ps, sigt_ready = sem("lora_ready"), sem("sigt_ps"), sem("sigt_ready")
        kk_ready, kksq_ready, rkk_ready, cum_ps = sem("kk_ready"), sem("kksq_ready"), sem("rkk_ready"), sem("cum_ps")
        decay_ready, decay_used, tilde_ready = sem("decay_ready"), sem("decay_used"), sem("tilde_ready")
        amat_ps, amat_ready, tok_ps, tok_a_ready, tok_d_ready = (
            sem(n) for n in ("amat_ps", "amat_ready", "tok_ps", "tok_a_ready", "tok_d_ready"))
        lvl_ready, p_ps, p_ready, dt_ps, t_ready = (sem(n) for n in ("lvl_ready", "p_ps", "p_ready", "dt_ps", "t_ready"))
        ht_ps, ht_ready, akv_ps, akv_ready, g_ps, g_ready = (
            sem(n) for n in ("ht_ps", "ht_ready", "akv_ps", "akv_ready", "g_ps", "g_ready"))
        rb_ps, rb_ready, u_ps, u_ready, o3_ps, o3_ready, s_ps, s_ready = (
            sem(n) for n in ("rb_ps", "rb_ready", "u_ps", "u_ready", "o3_ps", "o3_ready", "s_ps", "s_ready"))
        o_ps, o_ready, o_dev, o_sq, o_final, merged_ready = (
            sem(n) for n in ("o_ps", "o_ready", "o_dev", "o_sq", "o_final", "merged_ready"))
        up_full = [sem(f"up_full{i}") for i in range(2)]
        down_full = [sem(f"down_full{i}") for i in range(2)]
        up_g_ps = [sem(f"up_g_ps{i}") for i in range(2)]
        up_u_ps = [sem(f"up_u_ps{i}") for i in range(2)]
        down_ps = [sem(f"down_ps{i}") for i in range(2)]
        sig_ready = [sem(f"sig_ready{i}") for i in range(2)]
        silu_ready = [sem(f"silu_ready{i}") for i in range(2)]
        act_ready = [sem(f"act_ready{i}") for i in range(2)]
        actt_ps = [sem(f"actt_ps{i}") for i in range(2)]
        actt_ready = [sem(f"actt_ready{i}") for i in range(2)]
        f_ytok, f_tr = sem("f_ytok"), sem("f_tr")
        htok_ps, htok_ready = sem("htok_ps"), sem("htok_ready")
        logits_ps, r_maxed, r_exped, r_sel_ready, rank_ps, jobs_ready = (
            sem(n) for n in ("logits_ps", "r_maxed", "r_exped", "r_sel_ready", "rank_ps", "jobs_ready"))
        sel_ready, gather_ps, gather_ready, y_ready, comb_ps, comb_done = (
            sem(n) for n in ("sel_ready", "gather_ps", "gather_ready", "y_ready", "comb_ps", "comb_done"))
        out_ps, out_rows, out_done = sem("out_ps"), sem("out_rows"), sem("out_done")
        dve_chain, pool_chain = sem("dve_chain"), sem("pool_chain")
        inv_in, rstd_ready = sem("inv_in"), sem("rstd_ready")

        def cols_of(l, c0, n):
            return w_in[l, :, c0:c0 + n].rearrange("(k p) c -> p k c", p=P)

        def rows_of(w, k0, n):
            return w[k0 * P:(k0 + n) * P, :].rearrange("(k p) c -> p k c", p=P)

        def mixer_fills(l):
            z, zd = lambda name, n: (za_ready, ZA[l, name] + n), lambda name, n: (zd_ready, ZD[l, name] + n)
            fills = [([(0, cols_of(l, COL_RWKV + 512 * i, 512))], z("z", 4 * i + 4)) for i in range(3)]
            last = [(0, cols_of(l, COL_RWKV + 1536, P))]
            if l > 0:
                last.append((KC * P, rows_of(vres_down[l - 1], 0, KC)))
            fills.append((last, z("z", NB_RKV + 1 + l)))
            fills.append(([(0, cols_of(l, 0, 512))], z("pc", 4)))
            fills.append(([(0, cols_of(l, 512, 256))], z("pc", 6)))
            fills += [([(0, cols_of(l, GATE_R + 512 * i, 512))], z("gate_r", 4 * i + 4)) for i in range(2)]
            fills.append(([(0, cols_of(l, GATE_P, 512))], z("gate_p", 4)))
            fills.append(([(0, rows_of(pool_proj[l], 0, 2)), (2048, rows_of(conv_proj[l], 0, 2))],
                          zd("y_conv", KC)))
            fills.append(([(0, cols_of(l, GATE_P + 512, 512))], z("gate_p", 8)))
            fills += [([(0, cols_of(l, GATE_C + 512 * i, 512))], z("gate_c", 4 * i + 4)) for i in range(2)]
            fills.append(([(0, rows_of(rwkv_proj[l], 0, 4))], zd("y_rwkv", KC)))
            fills += [([(0, rows_of(w_o[l], 4 * i, 4))], zd("w_o", KC)) for i in range(2)]
            return fills

        SLOT = [0, 1, 2, 0, 1, 2, 0, 1, 2, 0, 1, 2, 1, 2, 0, 1]
        FILLS, FULL, AFTER = [], [], []
        last_in, landed = {}, {}
        for l in range(DEPTH):
            for i, (dmas, free) in enumerate(mixer_fills(l)):
                s = SLOT[i]
                FILLS.append((s, dmas))
                AFTER.append(last_in.get(s))
                landed[s] = landed.get(s, 0) + 16 * len(dmas)
                FULL.append(landed[s])
                last_in[s] = free
            last_in = {}

        def fill_at(n, width, off=0, k=None):
            base = 4096 * FILLS[n][0] + off
            k = k or 4096 // width
            return ring[:, base:base + k * width].rearrange("p (k c) -> p k c", c=width)

        def ffn_set(s, part):
            t = ring[:, 6144 * s + 2048 * part:6144 * s + 2048 * (part + 1)]
            return t.rearrange("p (k c) -> p k c", c=FB if part < 2 else D)

        def moe_set(s, part):
            t = (ring, scr)[s][:, 4096 * part:4096 * (part + 1)]
            return t.rearrange("p (k c) -> p k c", c=EB if part < 2 else D)

        block = ctx.enter_context(nc.Block())

        @block.sync
        def _(sp):
            sp.dma_start(tokm, x_in.rearrange("(t p) d -> p t d", p=P)).then_inc(x_in_tok, 16)
            sp.dma_start(cst[:, :], consts).then_inc(cst_in, 16)

            def mixer_weights(l):
                for i in range(MIX_FILLS):
                    n = MIX_FILLS * l + i
                    s, dmas = FILLS[n]
                    if AFTER[n] is not None:
                        sp.wait_ge(*AFTER[n])
                    for off, src in dmas:
                        k, w = src.shape[1], src.shape[2]
                        sp.dma_start(fill_at(n, w, off, k), src).then_inc(ring_full[s], 16)

            def ffn_weights(n, s):
                c = n * FB
                if not isinstance(n, int) or n >= 2:
                    sp.wait_ge(up_u_ps[1], n - 1)
                for part, w in enumerate((ffn_w1, ffn_w3)):
                    sp.dma_start(ffn_set(s, part), w[:, ds(c, FB)].rearrange("(k p) c -> p k c", p=P)
                                 ).then_inc(up_full[s], 16)
                if not isinstance(n, int) or n >= 2:
                    sp.wait_ge(down_ps[1], n - 1)
                sp.dma_start(ffn_set(s, 2), ffn_w2[ds(c, FB), :].rearrange("(k p) c -> p k c", p=P)
                             ).then_inc(down_full[s], 16)

            mixer_weights(0)
            sp.wait_ge(zd_ready, ZD[0, "end"])
            ffn_weights(0, 0)
            ffn_weights(1, 1)
            ffn_weights(2, 0)
            with sp.Fori(0, (N_FFB - 3) // 2) as it:
                ffn_weights(2 * it + 3, 1)
                ffn_weights(2 * it + 4, 0)
            sp.wait_ge(down_ps[1], N_FFB)
            mixer_weights(1)

            sp.wait_ge(zd_ready, ZD[1, "end"])
            sp.wait_ge(jobs_ready, 1)
            n_pairs = sp.value_load(job_i[0:1, N_JOBS:N_JOBS + 1], min_val=NE // 2, max_val=N_JOBS // 2)
            with sp.Fori(0, n_pairs) as pair:
                e = [sp.value_load(job_i[0:1, ds(2 * pair + s, 1)], min_val=0, max_val=NE - 1) for s in range(2)]
                with sp.Fori(0, N_EB) as b:
                    for s in range(2):
                        n = N_FFB + pair * N_EB + b
                        sp.wait_ge(up_u_ps[s], n)
                        for part, w in enumerate((moe_w1, moe_w3)):
                            sp.dma_start(moe_set(s, part),
                                         w[ds(e[s], 1), :, ds(b * EB, EB)].rearrange("o (k p) c -> p (o k) c", p=P)
                                         ).then_inc(up_full[s], 16)
                        sp.wait_ge(down_ps[s], n)
                        sp.dma_start(moe_set(s, 2),
                                     moe_w2[ds(e[s], 1), ds(b * EB, EB), :].rearrange("o (k p) c -> p (o k) c", p=P)
                                     ).then_inc(down_full[s], 16)
            for t in range(NT):
                sp.wait_ge(out_rows, t + 1)
                sp.dma_start(out.rearrange("(t p) d -> t p d", p=P)[t], tokm[:, t, :]).then_inc(out_done, 16)
            sp.wait_ge(out_done, 16 * NT)

        @block.gpsimd
        def _(pool):
            chain = [0]

            def link(ins):
                chain[0] += 1
                ins.then_inc(pool_chain, 1)
                pool.wait_ge(pool_chain, chain[0])
                return ins

            pool.dma_start(par[:, :], params).then_inc(par_in, 16)
            ada_rows = ada_w.rearrange("l i (k p) (t c) -> (l i k) t p c", p=P, c=1024)

            def ada_stream(first, last):
                with pool.Fori(first, last) as r:
                    for t in range(3):
                        pool.wait_ge(ada_free, 3 * r + t + 1)
                        pool.dma_start(ada_ring[:, t, :], ada_rows[ds(r, 1), t].rearrange("o p c -> (o p) c")
                                       ).then_inc(ada_full[t], 16)

            def small_weights(l):
                pool.dma_start(lora_w[0:32, :], w2[l]).then_inc(small_in, 16)
                pool.dma_start(lora_w[32:64, :], a2[l]).then_inc(small_in, 16)
                pool.dma_start(lora_w[64:P, :], g2[l]).then_inc(small_in, 16)
                pool.dma_start(w0_sb[0:1, :], w0_row[l:l + 1, :]).then_inc(small_in, 16)
                for g in range(4):
                    q = 64 * (g % 2)
                    pool.dma_start(pool_wsb[q:q + 64, 64 * (g // 2):64 * (g // 2) + 64],
                                   pool_w[l, g]).then_inc(small_in, 16)
                if l == 0:
                    pool.dma_start(w0_sb[VR, :], vres_v2[0]).then_inc(small_in, 16)
                    pool.dma_start(router_sb[:, :].rearrange("p (k e) -> p k e", e=NE),
                                   router.rearrange("(k p) e -> p k e", p=P)).then_inc(small_in, 16)

            def pooling(l):
                pool.wait_ge(za_done, ZA[l, "pc"] + 2)
                src = pu3
                for g, dst in enumerate((pa3, pb3, pa3, pb3)):
                    sh = 1 << g
                    lo = 2 * sh - 1
                    link(pool.tensor_tensor(dst[:, :, lo:], src[:, :, lo:],
                                            src[:, :, lo - sh:PAD_P + SEQ - sh], ALU.add))
                    q, b = slice(64 * (g % 2), 64 * (g % 2) + 64), g // 2
                    link(pool.tensor_tensor(pl[q, b, :], dst[q, b, PAD_P:],
                                            cst[q, C_CNT + b * SEQ:C_CNT + (b + 1) * SEQ], ALU.mult))
                    pool.tensor_tensor(pl[q, b, :], pl[q, b, :], pu3[q, b, PAD_P:], ALU.subtract
                                       ).then_inc(pooled, 1)
                    pool.wait_ge(pooled, 4 * l + g + 1)
                    src = dst

            def level_masks(l, hf):
                for m in range(1, LEVELS):
                    for g in range(2):
                        if m == 1:
                            pool.wait_ge(amat_ready, 2 * (2 * l + hf) + g + 1)
                        else:
                            pool.wait_ge(p_ps, ((2 * l + hf) * (LEVELS - 1) + m - 2) * 2 + g + 1)
                        pool.tensor_tensor(lvl_l[:, 4 * g:4 * g + 4, :], ltm[:, 4 * g:4 * g + 4, :],
                                           cc(C_LVL + m * P).unsqueeze(1).broadcast_to([P, 4, P]), ALU.mult
                                           ).then_inc(lvl_ready, 1)

            ada_stream(0, 8)
            small_weights(0)
            pool.wait_ge(cst_in, 16)
            pool.wait_ge(pads_ready, 1)
            ada_stream(8, 16)
            pooling(0)
            ada_stream(16, 32)
            level_masks(0, 0)
            level_masks(0, 1)
            pool.wait_ge(o_final, 1)
            small_weights(1)
            pooling(1)
            level_masks(1, 0)
            level_masks(1, 1)

        @block.scalar
        def _(act):
            za = [0]

            def evac(dst, func=ACT.Identity, rows=slice(0, P), **kw):
                n = za[0]
                za[0] += 1
                act.wait_ge(za_ready, n + 1)
                act.activation(dst, bank(n % 2, SEQ)[rows, :], func, **kw).then_inc(za_done, 1)

            roots = [0]

            def root(a):
                roots[0] += 1
                act.wait_ge(inv_in, roots[0])
                act.activation(a, a, ACT.Sqrt).then_inc(rstd_ready, 1)

            def square_x(li):
                act.wait_ge(x_ready, KC * (li + 1))
                act.activation(h_t[:, :], x_t[:, :], ACT.Square, scale=1.0 / 32).then_inc(xsq_ready, 1)
                root(rstd[:, :])

            def mixer(l):
                square_x(2 * l)
                for b in range(NB_RKV + 1 + l):
                    n = ZMIX[l] + b
                    if n >= N_RAW:
                        act.wait_ge(mix_done, n - N_RAW + 1)
                    rows = VR if b > NB_RKV else slice(0, P)
                    evac(raw[rows, n % N_RAW, 1:SEQ + 1], rows=rows)
                if l == 0:
                    act.wait_ge(pads_ready, 1)
                for b in range(2):
                    evac(pu3[:, b, PAD_P:])
                for b in range(2):
                    evac(ca[:, b, PAD_C:])
                for b in range(2):
                    evac(cb[:, b, :], ACT.Sigmoid)
                act.wait_ge(mix_done, ZMIX[l] + NB_RKV + 1)
                act.activation(lora_in[0:32, :], lora_in[0:32, :], ACT.Tanh).then_inc(lora_ready, 1)
                act.activation(lora_in[64:P, :], lora_in[64:P, :], ACT.Sigmoid).then_inc(lora_ready, 1)
                act.wait_ge(sigt_ps, l + 1)
                act.activation(scr[:, 6144:7168], ps_t[:, 5 * 512:7 * 512], ACT.Sigmoid).then_inc(sigt_ready, 1)
                for b in range(4):
                    evac(a_b[:, b, :], ACT.Sigmoid, bias=pcol(l, "a0", b))
                for b in range(4):
                    evac(gg[:, b, :])
                for b in range(4 * l):
                    evac(bon[:, b, :], ACT.Sigmoid, bias=pcol(l, "v0", b))
                act.wait_ge(kk_ready, 4 * (l + 1))
                act.activation(e1[:, :, :], kk_a[:, :, :], ACT.Square).then_inc(kksq_ready, 1)
                root(inv4_t)
                act.wait_ge(cum_ps, l + 1)
                act.wait_ge(zd_ready, ZD[l, "kk"] + 4)
                act.activation(scr[:, 0:1024], ps_t[:, 6 * 512:8 * 512], ACT.Exp, scale=-DECAY).then_inc(decay_ready, 1)
                act.wait_ge(zd_ready, ZD[l, "bonus"] + 4)
                act.activation(scr[:, 1024:2048], ps_t[:, 4 * 512:6 * 512], ACT.Exp, scale=DECAY).then_inc(decay_ready, 1)
                act.wait_ge(decay_used, l + 1)
                act.activation(scr[:, 0:1024], ps_t[:, 4 * 512:6 * 512], ACT.Exp, scale=-DECAY).then_inc(decay_ready, 1)
                for b in range(KC):
                    evac(gate_r[:, b, :], ACT.Sigmoid)
                act.wait_ge(pool_ps, l + 1)
                for b in range(2):
                    for q in range(2):
                        r = slice(64 * q, 64 * q + 64)
                        act.activation(pa3[r, b, PAD_P:], ps_t[r, 512 * (4 + q) + SEQ * b:512 * (4 + q) + SEQ * (b + 1)],
                                       ACT.Identity, scale=pcol(l, "pool_scale", b, 64 * q, 64 * q + 64)).then_inc(pool_y, 1)
                for b in range(KC):
                    if b >= 2:
                        act.wait_ge(zd_free, ZD[l, "y_pool"] + b - 1)
                    evac(sg[:, b % 2, :], ACT.Sigmoid)
                act.wait_ge(conv_dev, 2 * (l + 1))
                act.activation(cb_t[:, :], cy_t[:, :], ACT.Square).then_inc(conv_sq, 1)
                root(rstd[:, :])
                act.wait_ge(conv_un, 2 * (l + 1))
                act.activation(cb_t[:, :], cy_t[:, :], ACT.Sigmoid).then_inc(conv_sg, 1)
                for b in range(KC):
                    act.wait_ge(zd_free, ZD[l, "y_pool"] + KC + b - 1)
                    evac(sg[:, b % 2, :], ACT.Sigmoid)
                for hf in range(NT):
                    wkv_half(l, hf)
                for b in range(4):
                    act.wait_ge(o_dev, 4 * l + b + 1)
                    act.activation(e1[:, b, :], o_all[:, b, :], ACT.Square).then_inc(o_sq, 1)
                root(inv4_t)

            def wkv_half(l, hf):
                k = 2 * l + hf
                for i, kind in enumerate((0, 2)):
                    act.wait_ge(tok_ps, 4 * k + 2 * i + 1)
                    act.activation(tok[:, kind, :], bank(6), ACT.Identity).then_inc(tok_a_ready, 1)
                for m in range(1, LEVELS):
                    for g in range(2):
                        n = (k * (LEVELS - 1) + m - 1) * 2 + g
                        act.wait_ge(p_ps, n + 1)
                        act.activation(p_sb[:, 4 * g:4 * g + 4, :], bank(g), ACT.Identity).then_inc(p_ready, 1)
                    if m == 2:
                        act.wait_ge(akv_ps, k + 1)
                        act.activation(akv[:, :, :], bank(7), ACT.Identity).then_inc(akv_ready, 1)
                act.wait_ge(ht_ps, k + 1)
                act.activation(ht_sb[:, :, :], bank(6), ACT.Identity).then_inc(ht_ready, 1)
                act.wait_ge(g_ps, k + 1)
                act.activation(g_sb[:, :, :], bank(7), ACT.Identity).then_inc(g_ready, 1)
                for c in range(2):
                    act.wait_ge(o3_ps, 2 * k + c + 1)
                    for q in range(2):
                        r = slice(64 * q, 64 * q + 64)
                        act.activation(o_state[r, :, 128 * hf + 64 * c:128 * hf + 64 * c + 64],
                                       ps_t[r, 512 * (6 + q):512 * (6 + q) + 256], ACT.Identity).then_inc(o3_ready, 1)

            def activation_t(n, t, width):
                act.wait_ge(up_g_ps[t], n + 1)
                act.activation(sig_sb[:, t, 0:width], bank(2 * t, width), ACT.Sigmoid).then_inc(sig_ready[t], 1)

            def turned_t(n, t, width):
                act.wait_ge(actt_ps[t], n + 1)
                act.activation(act_t[:, t, 0:width], bank(2 * t, width), ACT.Identity).then_inc(actt_ready[t], 1)

            def ff_block(n, width):
                activation_t(n, 0, width)
                activation_t(n, 1, width)
                turned_t(n, 0, width)
                turned_t(n, 1, width)

            act.wait_ge(par_in, 16)
            act.activation(c_sig[:, :], par[:, P_C:P_C + KC], ACT.Sigmoid).then_inc(c_sig_ready, 1)
            mixer(0)
            square_x(1)
            with act.Fori(0, N_FFB) as n:
                ff_block(n, FB)
            act.wait_ge(down_ps[0], N_FFB)
            act.activation(tokm[:, 0, :], ps_t[:, 2048:3072], ACT.Identity).then_inc(f_ytok, 1)
            mixer(1)
            square_x(3)
            act.wait_ge(htok_ps, 1)
            act.activation(tokm[:, :, :], ps_t[:, 2048:4096], ACT.Identity).then_inc(htok_ready, 1)
            act.wait_ge(r_maxed, 2)
            act.activation(r_exp[:, :], r_exp[:, :], ACT.Exp).then_inc(r_exped, 1)
            act.wait_ge(jobs_ready, 1)
            n_pairs = act.value_load(job_i[0:1, N_JOBS:N_JOBS + 1], min_val=NE // 2, max_val=N_JOBS // 2)
            with act.Fori(0, n_pairs) as pair:
                act.wait_ge(gather_ps, 3 * pair + 2)
                act.activation(h_sel[:, 0:KC, :], ps_t[:, 0:1024], ACT.Identity).then_inc(gather_ready, 1)
                with act.Fori(0, N_EB) as b:
                    ff_block(N_FFB + pair * N_EB + b, EB)
                act.wait_ge(down_ps[0], N_FFB + (pair + 1) * N_EB)
                act.activation(y_slot[:, 0, :], ps_t[:, 2048:3072], ACT.Identity).then_inc(y_ready, 1)
            square_x(4)
            for t in range(NT):
                act.wait_ge(out_ps, t + 1)
                act.activation(tokm[:, t, :], ps_t[:, 1024 * t:1024 * (t + 1)], ACT.Identity).then_inc(out_rows, 1)

        @block.vector
        def _(dve):
            chain, zd, ada_n = [0], [0], [0]

            def link(ins):
                chain[0] += 1
                ins.then_inc(dve_chain, 1)
                dve.wait_ge(dve_chain, chain[0])

            def take():
                n = zd[0]
                zd[0] += 1
                dve.wait_ge(zd_ready, n + 1)
                return bank(2 + n % 2, SEQ)

            roots = [0]

            def inverse(a, last):
                if last is not None:
                    link(last)
                roots[0] += 1
                dve.reciprocal(a, a).then_inc(inv_in, 1)

            def ada_steps(count):
                for _ in range(count):
                    n = ada_n[0]
                    ada_n[0] += 1
                    k, t = n // 3 % KC, n % 3
                    acc = ada_acc[:, 1024 * t:1024 * (t + 1)]
                    dve.wait_ge(ada_full[t], 16 * (n // 3 + 1))
                    if n >= 3:
                        dve.wait_ge(ada_free, n + 1)
                    if k == 0:
                        if n >= 24:
                            dve.wait_ge(mod_ps, n // 24)
                        ins = dve.tensor_scalar(acc, ada_ring[:, t, :], c_silu[:, k:k + 1], None, ALU.mult)
                    else:
                        ins = dve.scalar_tensor_tensor(out=acc, in0=ada_ring[:, t, :], scalar=c_silu[:, k:k + 1],
                                                       in1=acc, op0=ALU.mult, op1=ALU.add)
                    ins.then_inc(ada_free, 1)

            def finish_mods(li):
                l, i = divmod(li, 2)
                dve.wait_ge(mod_ps, li + 1)
                o = l * P_W + P_OFF["ada_b"] + 24 * i
                link(dve.tensor_tensor(mods[:, li, :], bank(7, 24), par[:, o:o + 24], ALU.add))
                o = l * P_W + P_OFF["norm_g"] + 8 * i
                dve.scalar_tensor_tensor(out=gain[:, li, :], in0=mods[:, li, 8:16], scalar=1.0,
                                         in1=par[:, o:o + 8], op0=ALU.add, op1=ALU.mult).then_inc(mods_ready, 1)

            def normed(li):
                dve.wait_ge(ssum_ps, li + 1)
                inverse(rstd[:, :], dve.tensor_scalar(rstd[:, :], bank(4, SEQ), 1e-6, None, ALU.add))
                dve.wait_ge(rstd_ready, roots[0])
                link(dve.tensor_tensor(hT, xT, rstd[:, :].unsqueeze(1).broadcast_to([P, KC, SEQ]), ALU.mult))

            def norm_in(li):
                normed(li)
                dve.wait_ge(mods_ready, li + 1)
                for k in range(KC):
                    dve.tensor_scalar(hT[:, k, :], hT[:, k, :], gain[:, li, k:k + 1], mods[:, li, k:k + 1],
                                      ALU.mult, ALU.add).then_inc(h_ready, 1)

            def mix_shift(l):
                for b in range(NB_RKV + 1 + l):
                    n = ZMIX[l] + b
                    rows = VR if b > NB_RKV else slice(0, P)
                    dst = rkv[:, b, :] if b < NB_RKV else (lora_in, vres_in)[b - NB_RKV][rows, :]
                    mu = pcol(l, "mu", b) if b <= NB_RKV else pcol(l, "vmu", 0, 64, 80)
                    z = raw[rows, n % N_RAW, :]
                    dve.wait_ge(za_done, ZA[l, "z"] + b + 1)
                    link(dve.tensor_tensor(tmp[rows, :], z[:, 0:SEQ], z[:, 1:SEQ + 1], ALU.subtract))
                    dve.scalar_tensor_tensor(out=dst, in0=tmp[rows, :], scalar=mu, in1=z[:, 1:SEQ + 1],
                                             op0=ALU.mult, op1=ALU.add).then_inc(mix_done, 1)
                    dve.wait_ge(mix_done, n + 1)
                    if 4 <= b < 8:
                        dve.tensor_scalar(kk_a[:, b - 4, :], dst, pcol(l, "kk_scale", b - 4), None, ALU.mult
                                          ).then_inc(kk_ready, 1)
                    if l == 0 and b < NB_RKV:
                        ada_steps(2)

            def rwkv_inputs(l):
                dve.wait_ge(za_done, ZA[l, "a"] + 4)
                for b in range(4):
                    link(dve.tensor_scalar(tmp[:, :], a_b[:, b, :], 1.0, pcol(l, "ka", b), ALU.subtract, ALU.mult))
                    dve.wait_ge(kk_ready, 4 * (l + 1))
                    link(dve.scalar_tensor_tensor(out=kkv[:, b, :], in0=tmp[:, :], scalar=1.0, in1=kkv[:, b, :],
                                                  op0=ALU.add, op1=ALU.mult))
                for b in range(4):
                    link(dve.scalar_tensor_tensor(out=e2[:, b, :], in0=rr[:, b, :], scalar=pcol(l, "rk", b),
                                                  in1=kkv[:, b, :], op0=ALU.mult, op1=ALU.mult))
                dve.tensor_copy(tmp[:, 0:1], e2[:, 3, 0:1]).then_inc(rkk_ready, 1)
                if l == 0:
                    link(dve.tensor_copy(v_first[:, :], rkv_t[:, 8 * SEQ:12 * SEQ]))
                else:
                    dve.wait_ge(za_done, ZA[l, "vres"] + 4)
                    v1 = rkv_t[:, 8 * SEQ:12 * SEQ]
                    link(dve.tensor_tensor(v_first[:, :], v_first[:, :], v1, ALU.subtract))
                    link(dve.tensor_tensor(v_first[:, :], v_first[:, :], scr[:, 5120:6144], ALU.mult))
                    link(dve.tensor_tensor(v1, v1, v_first[:, :], ALU.add))
                for b in range(4):
                    dve.tensor_scalar(inv4[:, b, :], take(), 1e-24, None, ALU.max).then_inc(zd_free, 1)
                dve.wait_ge(zd_free, zd[0])
                inverse(inv4_t, None)
                for b in range(4):
                    dve.tensor_tensor(bon[:, b, :], take(), vv[:, b, :], ALU.mult).then_inc(zd_free, 1)
                dve.wait_ge(rstd_ready, roots[0])
                link(dve.tensor_tensor(kk_a, kk_a, inv4, ALU.mult))
                dve.wait_ge(decay_ready, 3 * l + 1)
                link(dve.tensor_tensor(a_b, a_b, kk_a, ALU.mult))
                dve.scalar_tensor_tensor(out=kk_a, in0=kk_a, scalar=-1.0, in1=e1, op0=ALU.mult, op1=ALU.mult
                                         ).then_inc(decay_used, 1)
                dve.wait_ge(decay_ready, 3 * l + 2)
                link(dve.tensor_tensor(a_b, a_b, e2, ALU.mult))
                link(dve.tensor_tensor(kkv, kkv, e2, ALU.mult))
                dve.wait_ge(decay_ready, 3 * l + 3)
                link(dve.tensor_copy(chunk_decay[:, :].rearrange("p (b c) -> p b c", b=4), e1[:, :, CH - 1:SEQ:CH]))
                dve.tensor_tensor(rr, rr, e1, ALU.mult).then_inc(tilde_ready, 1)

            def conv(l):
                dve.wait_ge(za_done, ZA[l, "pc"] + 6)
                link(dve.tensor_tensor(ca[:, :, PAD_C:], ca[:, :, PAD_C:], cb, ALU.mult))
                for b in range(2):
                    link(dve.tensor_scalar(cy[:, b, :], ca[:, b, 0:SEQ], pcol(l, "conv_w", b * CONV_K),
                                           pcol(l, "conv_b", b), ALU.mult, ALU.add))
                for j in range(1, CONV_K):
                    for b in range(2):
                        ins = dve.scalar_tensor_tensor(out=cy[:, b, :], in0=ca[:, b, j:j + SEQ],
                                                       scalar=pcol(l, "conv_w", b * CONV_K + j), in1=cy[:, b, :],
                                                       op0=ALU.mult, op1=ALU.add)
                        if j < CONV_K - 1:
                            link(ins)
                        else:
                            ins.then_inc(conv_u, 1)

            def conv_norm(l):
                dve.wait_ge(conv_mean, l + 1)
                dve.wait_ge(conv_u, 2 * (l + 1))
                for b in range(2):
                    dve.tensor_tensor(cy[:, b, :], cy[:, b, :], bank(4, SEQ), ALU.subtract).then_inc(conv_dev, 1)
                dve.wait_ge(conv_var, l + 1)
                inverse(rstd[:, :], dve.tensor_scalar(rstd[:, :], bank(5, SEQ), 1e-5, None, ALU.add))
                dve.wait_ge(rstd_ready, roots[0])
                dve.wait_ge(conv_dev, 2 * (l + 1))
                for b in range(2):
                    link(dve.tensor_tensor(cy[:, b, :], cy[:, b, :], rstd[:, :], ALU.mult))
                    dve.tensor_scalar(cy[:, b, :], cy[:, b, :], pcol(l, "ln_g", b), pcol(l, "ln_b", b),
                                      ALU.mult, ALU.add).then_inc(conv_un, 1)
                dve.wait_ge(conv_sg, l + 1)
                dve.wait_ge(conv_un, 2 * (l + 1))
                dve.tensor_tensor(cy, cy, cb, ALU.mult).then_inc(conv_y, 1)

            def wkv_half(l, hf):
                k = 2 * l + hf
                tri_s, tri_i = (cc(c).unsqueeze(1).broadcast_to([P, 4, P]) for c in (C_TRI_S, C_TRI_I))
                low0, lvl0, eye = (cc(c).unsqueeze(1).broadcast_to([P, 4, P]) for c in (C_LOW0, C_LVL, C_ID))

                def heads(b):
                    return bank(b).rearrange("p (n w) -> p n w", w=P)

                for g in range(2):
                    h4 = slice(4 * g, 4 * g + 4)
                    dve.wait_ge(amat_ps, 2 * k + g + 1)
                    link(dve.tensor_tensor(ltm[:, h4, :], heads(2 + g), tri_s, ALU.mult))
                    dve.tensor_tensor(ak_t[:, h4, :], heads(4 + g), tri_s, ALU.mult).then_inc(amat_ready, 1)
                    link(dve.tensor_tensor(tinv[:, h4, :], heads(g), low0, ALU.mult))
                    link(dve.tensor_tensor(tinv_t[:, h4, :], ltm[:, h4, :], lvl0, ALU.mult))
                    dve.tensor_tensor(tinv[:, h4, :], tinv[:, h4, :], eye, ALU.add).then_inc(t_ready, 1)
                    dve.tensor_tensor(tinv_t[:, h4, :], tinv_t[:, h4, :], eye, ALU.add).then_inc(t_ready, 1)
                base = k * T_INC
                for i, kind in enumerate((1, 3)):
                    dve.wait_ge(tok_ps, 4 * k + 2 * i + 2)
                    dve.tensor_copy(tok[:, kind, :], bank(7)).then_inc(tok_d_ready, 1)
                for m in range(1, LEVELS):
                    for g in range(2):
                        h4 = slice(4 * g, 4 * g + 4)
                        dve.wait_ge(dt_ps, (k * (LEVELS - 1) + m - 1) * 2 + g + 1)
                        dve.wait_ge(t_ready, base + 4 * m)
                        if m < LEVELS - 1:
                            dve.tensor_tensor(tinv[:, h4, :], tinv[:, h4, :], heads(2 + g), ALU.add).then_inc(t_ready, 1)
                        else:
                            dve.sem_inc(t_ready, 1)
                        dve.tensor_tensor(tinv_t[:, h4, :], tinv_t[:, h4, :], heads(4 + g), ALU.add).then_inc(t_ready, 1)
                for g in range(2):
                    h4 = slice(4 * g, 4 * g + 4)
                    dve.wait_ge(rb_ps, 2 * k + g + 1)
                    dve.tensor_tensor(lvl_l[:, h4, :], heads(g), tri_i, ALU.mult).then_inc(rb_ready, 1)
                    dve.tensor_tensor(ak_t[:, h4, :], heads(2 + g), tri_i, ALU.mult).then_inc(rb_ready, 1)
                for c in range(2):
                    n = 2 * k + c
                    r = slice(64 * c, 64 * c + 64)
                    dve.wait_ge(u_ps, n + 1)
                    dve.wait_ge(g_ready, k + 1)
                    for g in range(2):
                        dve.tensor_tensor(u_sb[r, 4 * g:4 * g + 4, :],
                                          ps_t[r, 512 * (4 + g):512 * (4 + g) + 256].rearrange("p (n w) -> p n w", w=64),
                                          g_sb[r, 4 * g:4 * g + 4, :], ALU.add).then_inc(u_ready, 1)
                    dve.wait_ge(s_ps, n + 1)
                    link(dve.tensor_tensor(state_t[:, :], state_t[:, :], bank(0, 256), ALU.add))
                    wc = chunk_decay[:, :].rearrange("p (b c) -> p b c", b=4)[:, :, 2 * hf + c:2 * hf + c + 1]
                    dve.tensor_tensor(state, state, wc.broadcast_to([P, 4, 64]), ALU.mult).then_inc(s_ready, 1)
                dve.wait_ge(o_ps, k + 1)
                dve.wait_ge(o3_ready, 4 * (k + 1))
                dve.tensor_tensor(o_all[:, :, P * hf:P * hf + P], bank(1).rearrange("p (n w) -> p n w", w=P),
                                  o_state[:, :, P * hf:P * hf + P], ALU.add).then_inc(o_ready, 1)

            def rwkv_out(l):
                dve.wait_ge(o_ready, 2 * (l + 1))
                for b in range(4):
                    dve.scalar_tensor_tensor(out=o_all[:, b, :], in0=take(), scalar=-1.0 / 64, in1=o_all[:, b, :],
                                             op0=ALU.mult, op1=ALU.add).then_inc(zd_free, 1)
                    dve.wait_ge(zd_free, zd[0])
                    dve.sem_inc(o_dev, 1)
                for b in range(4):
                    dve.tensor_scalar(inv4[:, b, :], take(), 1.0 / 64, 64e-5, ALU.mult, ALU.add).then_inc(zd_free, 1)
                dve.wait_ge(zd_free, zd[0])
                inverse(inv4_t, None)
                dve.wait_ge(rstd_ready, roots[0])
                link(dve.tensor_tensor(o_all, o_all, inv4, ALU.mult))
                for b in range(4):
                    link(dve.tensor_scalar(o_all[:, b, :], o_all[:, b, :], pcol(l, "lnx_g", b), pcol(l, "lnx_b", b),
                                           ALU.mult, ALU.add))
                link(dve.tensor_tensor(o_all, o_all, bon, ALU.add))
                dve.tensor_tensor(o_all, o_all, gg, ALU.mult).then_inc(o_final, 1)

            def mixer(l):
                norm_in(2 * l)
                mix_shift(l)
                if l == 0:
                    finish_mods(1)
                rwkv_inputs(l)
                conv(l)
                for b in range(KC):
                    src = take()
                    dve.wait_ge(za_done, ZA[l, "gate_p"] + b + 1)
                    dve.tensor_tensor(merged[:, b, :], src, sg[:, b % 2, :], ALU.mult).then_inc(zd_free, 1)
                    if l == 0:
                        ada_steps(3)
                if l == 0:
                    finish_mods(2)
                conv_norm(l)
                for b in range(KC):
                    src = take()
                    dve.wait_ge(za_done, ZA[l, "gate_c"] + b + 1)
                    dve.tensor_tensor(tmp[:, :], src, sg[:, b % 2, :], ALU.mult).then_inc(zd_free, 1)
                    dve.wait_ge(zd_free, zd[0])
                    link(dve.tensor_tensor(merged[:, b, :], merged[:, b, :], tmp[:, :], ALU.add))
                    if l == 0:
                        ada_steps(3)
                if l == 0:
                    finish_mods(3)
                dve.memset(state_t[:, :], 0.0).then_inc(s_ready, 1)
                dve.wait_ge(s_ready, 5 * l + 1)
                for hf in range(NT):
                    wkv_half(l, hf)
                rwkv_out(l)
                for b in range(KC):
                    if b >= 1:
                        dve.wait_ge(merged_ready, KC * l + b)
                    dve.tensor_tensor(tmp[:, :], take(), gate_r[:, b, :], ALU.mult).then_inc(zd_free, 1)
                    dve.wait_ge(zd_free, zd[0])
                    dve.tensor_tensor(merged[:, b, :], merged[:, b, :], tmp[:, :], ALU.add).then_inc(merged_ready, 1)
                for b in range(KC):
                    dve.scalar_tensor_tensor(out=xT[:, b, :], in0=take(), scalar=mods[:, 2 * l, 16 + b:17 + b],
                                             in1=xT[:, b, :], op0=ALU.mult, op1=ALU.add).then_inc(zd_free, 1)
                    dve.wait_ge(zd_free, zd[0])
                    dve.sem_inc(x_ready, 1)

            def ff_block(n, width):
                for t in range(2):
                    dve.wait_ge(sig_ready[t], n + 1)
                    dve.tensor_tensor(sig_sb[:, t, 0:width], sig_sb[:, t, 0:width], bank(2 * t, width), ALU.mult
                                      ).then_inc(silu_ready[t], 1)
                    dve.wait_ge(silu_ready[t], n + 1)
                    dve.wait_ge(up_u_ps[t], n + 1)
                    dve.tensor_tensor(act_sb[:, t, 0:width], sig_sb[:, t, 0:width], bank(2 * t + 1, width), ALU.mult
                                      ).then_inc(act_ready[t], 1)

            dve.memset(raw_t[:, :], 0.0)
            dve.memset(pu[:, :], 0.0)
            dve.memset(pa[:, :], 0.0)
            dve.memset(pbuf[:, :], 0.0)
            dve.memset(ca_t[:, :], 0.0).then_inc(pads_ready, 1)
            dve.sem_inc(ada_free, 3)
            ada_n_first = 0
            dve.wait_ge(c_sig_ready, 1)
            link(dve.tensor_tensor(c_silu[:, :], c_sig[:, :], par[:, P_C:P_C + KC], ALU.mult))
            for t in range(NT):
                dve.wait_ge(xt_ps, t + 1)
                src = ps_t[:, 1024 * t:1024 * (t + 1)].rearrange("p (k n) -> p k n", n=P)
                dve.tensor_copy(xT[:, :, P * t:P * t + P], src).then_inc(x_ready, KC // NT)
            ada_steps(3 * KC)
            finish_mods(0)
            mixer(0)
            norm_in(1)
            with dve.Fori(0, N_FFB) as n:
                ff_block(n, FB)
            dve.wait_ge(down_ps[1], N_FFB)
            dve.tensor_copy(tokm[:, 1, :], ps_t[:, 3072:4096]).then_inc(f_ytok, 1)
            for k in range(KC):
                dve.wait_ge(f_tr, 2 * (k // 2) + 2)
                dve.scalar_tensor_tensor(out=xT[:, k, :], in0=ps_t[:, SEQ * k:SEQ * (k + 1)],
                                         scalar=mods[:, 1, 16 + k:17 + k], in1=xT[:, k, :],
                                         op0=ALU.mult, op1=ALU.add).then_inc(x_ready, 1)
            mixer(1)
            norm_in(3)

            lg3, sel3, gate3, rank3 = (t[:, :].rearrange("p (t e) -> p t e", e=NE) for t in (lg, r_sel, r_gate, r_rank))
            cmp3, cmq3 = (t[:, :].rearrange("p (t e f) -> p t e f", e=NE, f=NE) for t in (cmp_t, cmp2_t))
            low8 = cst[:, C_LOW8:C_LOW8 + NE * NE].rearrange("p (e f) -> p e f", f=NE)
            dve.wait_ge(logits_ps, 1)
            link(dve.tensor_copy(lg[:, :], bank(0, NT * NE)))
            link(dve.tensor_reduce(r_max[:, :], lg3, AX.X, ALU.max))
            for t in range(NT):
                dve.tensor_scalar(r_exp[:, NE * t:NE * t + NE], lg3[:, t, :], r_max[:, t:t + 1], None, ALU.subtract
                                  ).then_inc(r_maxed, 1)
            for t in range(NT):
                other = lg3[:, t, :].unsqueeze(1).broadcast_to([P, NE, NE])
                own = lg3[:, t, :].unsqueeze(2).broadcast_to([P, NE, NE])
                link(dve.tensor_tensor(cmp3[:, t], other, own, ALU.is_gt))
                link(dve.tensor_tensor(cmq3[:, t], other, own, ALU.is_equal))
                link(dve.tensor_tensor(cmq3[:, t], cmq3[:, t], low8, ALU.mult))
                link(dve.tensor_tensor(cmp3[:, t], cmp3[:, t], cmq3[:, t], ALU.add))
                link(dve.tensor_reduce(r_cnt[:, NE * t:NE * t + NE], cmp3[:, t], AX.X, ALU.add))
            dve.tensor_scalar(r_sel[:, :], r_cnt[:, :], 2.0, None, ALU.is_lt).then_inc(r_sel_ready, 1)
            dve.wait_ge(r_sel_ready, 1)
            dve.wait_ge(r_exped, 1)
            link(dve.tensor_tensor(r_gate[:, :], r_exp[:, :], r_sel[:, :], ALU.mult))
            link(dve.tensor_reduce(r_den[:, :], gate3, AX.X, ALU.add))
            link(dve.reciprocal(r_den[:, :], r_den[:, :]))
            link(dve.tensor_tensor(gate3, gate3, r_den[:, :].unsqueeze(2).broadcast_to([P, NT, NE]), ALU.mult))

            far = 1024.0
            dve.wait_ge(rank_ps, 1)
            link(dve.scalar_tensor_tensor(out=r_rank[:, :], in0=bank(1, NT * NE), scalar=far, in1=r_sel[:, :],
                                          op0=ALU.add, op1=ALU.mult))
            link(dve.tensor_scalar(r_rank[:, :], r_rank[:, :], far, None, ALU.subtract))
            link(dve.tensor_scalar(over[:, :], ps_t[:, 512 + NT * NE:512 + (NT + 1) * NE], float(P), None, ALU.is_gt))
            link(dve.tensor_tensor(cmp3[:, 0], low8, over[:, :].unsqueeze(1).broadcast_to([P, NE, NE]), ALU.mult))
            link(dve.tensor_reduce(prev[:, :], cmp3[:, 0], AX.X, ALU.add))
            jr = job_rank[:, :].rearrange("p (t j) -> p t j", j=N_JOBS)
            jg = job_gate[:, :].rearrange("p (t j) -> p t j", j=N_JOBS)
            link(dve.memset(job_rank[:, :], -far))
            link(dve.memset(job_gate[:, :], 0.0))
            link(dve.memset(job_f[:, :], 0.0))
            link(dve.tensor_copy(jr[:, :, 0:NE], rank3))
            link(dve.tensor_copy(jg[:, :, 0:NE], gate3))
            link(dve.tensor_copy(job_f[:, 0:NE], cc(C_EID, NE)))
            for q in range(3):
                oh = onehot[:, NE * q:NE * q + NE]
                w8 = cmp_t[:, NE * q:NE * q + NE]
                link(dve.tensor_scalar(oh, prev[:, :], float(q), None, ALU.is_equal))
                link(dve.tensor_tensor(oh, oh, over[:, :], ALU.mult))
                for t in range(NT):
                    link(dve.tensor_tensor(w8, oh, rank3[:, t, :], ALU.mult))
                    link(dve.tensor_reduce(jr[:, t, NE + q:NE + q + 1], w8, AX.X, ALU.add))
                    link(dve.tensor_tensor(w8, oh, gate3[:, t, :], ALU.mult))
                    link(dve.tensor_reduce(jg[:, t, NE + q:NE + q + 1], w8, AX.X, ALU.add))
                link(dve.tensor_tensor(w8, oh, cc(C_EID, NE), ALU.mult))
                link(dve.tensor_reduce(job_f[:, NE + q:NE + q + 1], w8, AX.X, ALU.add))
            link(dve.tensor_scalar(jr[:, :, NE:NE + 3], jr[:, :, NE:NE + 3], float(P), None, ALU.subtract))
            n_over = job_f[:, N_JOBS + 1:N_JOBS + 2]
            link(dve.tensor_reduce(n_over, over[:, :], AX.X, ALU.add))
            link(dve.tensor_scalar(job_f[:, N_JOBS:N_JOBS + 1], n_over, 0.5, float(NE // 2), ALU.is_gt, ALU.add))
            link(dve.tensor_scalar(job_f[:, N_JOBS + 2:N_JOBS + 3], n_over, 2.5, None, ALU.is_gt))
            link(dve.tensor_tensor(job_f[:, N_JOBS:N_JOBS + 1], job_f[:, N_JOBS:N_JOBS + 1],
                                   job_f[:, N_JOBS + 2:N_JOBS + 3], ALU.add))
            dve.memset(merged_t[:, :], 0.0).then_inc(comb_done, 1)
            dve.wait_ge(comb_done, 1)
            dve.tensor_copy(job_i[0:1, :], job_f[0:1, :]).then_inc(jobs_ready, 1)
            dve.wait_ge(jobs_ready, 1)
            n_pairs = dve.value_load(job_i[0:1, N_JOBS:N_JOBS + 1], min_val=NE // 2, max_val=N_JOBS // 2)

            iota = cc(C_IOTA)
            with dve.Fori(0, n_pairs) as pair:
                for s in range(2):
                    for t in range(NT):
                        place = job_rank[:, ds(N_JOBS * t + s + 2 * pair, 1)]
                        weight = job_gate[:, ds(N_JOBS * t + s + 2 * pair, 1)]
                        dve.tensor_scalar(sel[:, 2 * s + t, :], iota, place, None, ALU.is_equal).then_inc(sel_ready, 1)
                        dve.tensor_scalar(sel_g[:, 2 * s + t, :], iota, place, weight, ALU.is_equal, ALU.mult
                                          ).then_inc(sel_ready, 1)
                dve.wait_ge(gather_ps, 3 * pair + 1)
                dve.tensor_copy(sel_t_t[:, :], bank(6)).then_inc(gather_d_ready, 1)
                dve.wait_ge(gather_ps, 3 * pair + 3)
                dve.tensor_copy(h_sel[:, KC:2 * KC, :], ps_t[:, 2048:3072]).then_inc(gather_d_ready, 1)
                with dve.Fori(0, N_EB) as b:
                    ff_block(N_FFB + pair * N_EB + b, EB)
                dve.wait_ge(down_ps[1], N_FFB + (pair + 1) * N_EB)
                dve.tensor_copy(y_slot[:, 1, :], ps_t[:, 3072:4096]).then_inc(y_ready, 1)
                dve.wait_ge(comb_ps, pair + 1)
                dve.tensor_tensor(merged_t[:, :], merged_t[:, :], ps_t[:, 0:2048], ALU.add).then_inc(comb_done, 1)
                dve.wait_ge(comb_done, pair + 2)
            for k in range(KC):
                dve.scalar_tensor_tensor(out=xT[:, k, :], in0=yT[:, k, :], scalar=mods[:, 3, 16 + k:17 + k],
                                         in1=xT[:, k, :], op0=ALU.mult, op1=ALU.add).then_inc(x_ready, 1)
            dve.wait_ge(x_ready, 5 * KC)
            normed(4)
            for k in range(KC):
                dve.tensor_scalar(hT[:, k, :], hT[:, k, :], par[:, P_FG + k:P_FG + k + 1], None, ALU.mult
                                  ).then_inc(h_ready, 1)

        @block.tensor
        def _(pe):
            za, zd, fill = [0], [0], [0]

            def mm(dst, lhs, rhs, start=True, stop=True, **kw):
                return pe.matmul(dst, lhs, rhs, start=start, stop=stop, **kw)

            def give_za(parts, rows=slice(0, P)):
                n = za[0]
                za[0] += 1
                if n >= 2:
                    pe.wait_ge(za_done, n - 1)
                for i, (lhs, rhs) in enumerate(parts):
                    last = mm(bank(n % 2, SEQ)[rows, :], lhs, rhs, i == 0, i == len(parts) - 1)
                last.then_inc(za_ready, 1)

            def give_zd(parts):
                n = zd[0]
                zd[0] += 1
                if n >= 2:
                    pe.wait_ge(zd_free, n - 1)
                for i, (lhs, rhs) in enumerate(parts):
                    last = mm(bank(2 + n % 2, SEQ), lhs, rhs, i == 0, i == len(parts) - 1)
                last.then_inc(zd_ready, 1)

            def landed(n):
                pe.wait_ge(ring_full[FILLS[n][0]], FULL[n])

            def mean_square(li):
                pe.wait_ge(xsq_ready, li + 1)
                for k in range(KC):
                    last = mm(bank(4, SEQ), ones, hT[:, k, :], k == 0, k == KC - 1)
                last.then_inc(ssum_ps, 1)

            def mod_sums(li):
                pe.wait_ge(ada_free, 3 + 24 * (li + 1))
                for c in range(24):
                    last = mm(bank(7, 24)[:, c:c + 1], ada_acc[:, P * c:P * c + P], cc(C_ONES, 1))
                last.then_inc(mod_ps, 1)

            def z_parts(w, c):
                return [(w[:, k, c:c + P], hT[:, k, :]) for k in range(KC)]

            def z_blocks(l, fills, give=None):
                for i, n_blocks in fills:
                    n = MIX_FILLS * l + i
                    landed(n)
                    w = fill_at(n, P * n_blocks, 0, KC)
                    for b in range(n_blocks):
                        give_za(z_parts(w, P * b))
                        if give is not None:
                            give()

            def mixer(l):
                mean_square(2 * l)
                pe.wait_ge(h_ready, KC * (2 * l + 1))
                f0 = MIX_FILLS * l
                z_blocks(l, [(0, 4), (1, 4), (2, 4), (3, 1)])
                if l > 0:
                    wv = fill_at(f0 + 3, 16, KC * P, KC)
                    give_za([(wv[:, k, :], hT[:, k, :]) for k in range(KC)], rows=VR)
                z_blocks(l, [(4, 4), (5, 2)])
                if l == 0:
                    mod_sums(1)
                pe.wait_ge(small_in, SMALL[l])
                pe.wait_ge(lora_ready, 2 * (l + 1))
                for t in range(NT):
                    tk = slice(P * t, P * t + P)
                    mm(bank(5 + t), cc(C_ONES, P, 0, 1), w0_sb[0:1, :], True, False)
                    last = mm(bank(5 + t), lora_in[0:32, tk], lora_w[0:32, :], False, True)
                last.then_inc(sigt_ps, 1)
                for b in range(4):
                    c = slice(P * b, P * b + P)
                    give_za([(lora_w[32:64, c], lora_in[32:64, :])])
                for b in range(4):
                    c = slice(P * b, P * b + P)
                    give_za([(lora_w[64:P, c], lora_in[64:P, :])])
                for b in range(4 * l):
                    c = slice(P * b, P * b + P)
                    pe.wait_ge(mix_done, ZMIX[l] + NB_RKV + 2)
                    give_za([(w0_sb[VR, c], vres_in[VR, :])])
                pe.wait_ge(kksq_ready, l + 1)
                for b in range(4):
                    give_zd([(bones, e1[:, b, :])])
                pe.wait_ge(sigt_ready, l + 1)
                for first, tri in ((4, C_TRI_I), (6, C_TRI_S)):
                    for b in range(4):
                        for t in range(NT):
                            o = 512 * first + SEQ * b + P * t
                            last = mm(ps_t[:, o:o + P], sig_tok[:, t, P * b:P * b + P], cc(tri))
                last.then_inc(cum_ps, 1)
                pe.wait_ge(rkk_ready, l + 1)
                for b in range(4):
                    give_zd([(bones, e2[:, b, :])])
                z_blocks(l, [(6, 4), (7, 4)])
                pe.wait_ge(pooled, 4 * (l + 1))
                pe.wait_ge(decay_ready, 3 * (l + 1))
                for b in range(2):
                    for q in range(2):
                        r = slice(64 * q, 64 * q + 64)
                        o = 512 * (4 + q) + SEQ * b
                        last = mm(ps_t[r, o:o + SEQ], pool_wsb[r, 64 * b:64 * b + 64], pl[r, b, :])
                last.then_inc(pool_ps, 1)
                landed(f0 + 9)
                wp, wc = fill_at(f0 + 9, D, 0, 2), fill_at(f0 + 9, D, 2048, 2)
                at = [0]

                def y_pool():
                    b = at[0]
                    at[0] += 1
                    pe.wait_ge(pool_y, 4 * (l + 1))
                    give_zd([(wp[:, k, P * b:P * b + P], pa3[:, k, PAD_P:]) for k in range(2)])

                z_blocks(l, [(8, 4), (10, 4)], y_pool)
                if l == 0:
                    mod_sums(2)
                pe.wait_ge(conv_u, 2 * (l + 1))
                for b in range(2):
                    last = mm(bank(4, SEQ), mean256, cy[:, b, :], b == 0, b == 1)
                last.then_inc(conv_mean, 1)
                pe.wait_ge(conv_sq, l + 1)
                for b in range(2):
                    last = mm(bank(5, SEQ), mean256, cb[:, b, :], b == 0, b == 1)
                last.then_inc(conv_var, 1)
                at[0] = 0

                def y_conv():
                    b = at[0]
                    at[0] += 1
                    pe.wait_ge(conv_y, l + 1)
                    give_zd([(wc[:, k, P * b:P * b + P], cy[:, k, :]) for k in range(2)])

                z_blocks(l, [(11, 4), (12, 4)], y_conv)
                if l == 0:
                    mod_sums(3)
                pe.wait_ge(tilde_ready, l + 1)
                for hf in range(NT):
                    wkv_half(l, hf)
                pe.wait_ge(o_ready, 2 * (l + 1))
                for b in range(4):
                    give_zd([(bones, o_all[:, b, :])])
                for b in range(4):
                    pe.wait_ge(o_sq, 4 * l + b + 1)
                    give_zd([(bones, e1[:, b, :])])
                pe.wait_ge(o_final, l + 1)
                landed(f0 + 13)
                w = fill_at(f0 + 13, D)
                for b in range(KC):
                    give_zd([(w[:, k, P * b:P * b + P], o_all[:, k, :]) for k in range(4)])
                landed(f0 + 14)
                landed(f0 + 15)
                pe.wait_ge(merged_ready, KC * (l + 1))
                w0_, w1_ = fill_at(f0 + 14, D), fill_at(f0 + 15, D)
                for b in range(KC):
                    give_zd([((w0_, w1_)[k // 4][:, k % 4, P * b:P * b + P], merged[:, k, :]) for k in range(KC)])

            def wkv_half(l, hf):
                k = 2 * l + hf
                tk = slice(P * hf, P * hf + P)
                base = k * T_INC
                at_, bt_, kt_, rt_, vt_ = kk_a, a_b, kkv, rr, vv
                pe.wait_ge(za_done, ZA[l, "end"])
                pe.wait_ge(zd_free, ZD[l, "mean"])
                pe.wait_ge(mods_ready, 4)
                if hf == 1:
                    pe.wait_ge(o_ready, k)
                    pe.wait_ge(s_ready, 5 * l + 3)
                for g in range(2):
                    r = slice(64 * g, 64 * g + 64)
                    for b in range(4):
                        o = P * b
                        mm(ps_t[:, 512 * g + o:512 * g + o + P], at_[r, b, tk], bt_[r, b, tk])
                        mm(ps_t[:, 512 * (2 + g) + o:512 * (2 + g) + o + P], bt_[r, b, tk], at_[r, b, tk])
                        last = mm(ps_t[:, 512 * (4 + g) + o:512 * (4 + g) + o + P], kt_[r, b, tk], at_[r, b, tk])
                    last.then_inc(amat_ps, 1)
                for i, src in enumerate((at_, vt_, bt_, kt_)):
                    if i >= 2:
                        pe.wait_ge((tok_a_ready, tok_d_ready)[i - 2], 2 * k + 1)
                    for b in range(4):
                        last = pe.transpose(ps_t[:, 512 * (6 + i % 2) + P * b:512 * (6 + i % 2) + P * b + P],
                                            src[:, b, tk], ident)
                    last.then_inc(tok_ps, 1)
                for m in range(1, LEVELS):
                    n = (k * (LEVELS - 1) + m - 1) * 2
                    for g in range(2):
                        pe.wait_ge(lvl_ready, n + g + 1)
                        pe.wait_ge(t_ready, base + 4 * (m - 1) + 2 * (g + 1))
                        for b in range(4):
                            h = 4 * g + b
                            last = mm(ps_t[:, 512 * g + P * b:512 * g + P * b + P], lvl_l[:, h, :], tinv[:, h, :])
                        last.then_inc(p_ps, 1)
                    if m == 1:
                        pe.wait_ge(amat_ready, 2 * k + 2)
                    for g in range(2):
                        pe.wait_ge(p_ready, n + g + 1)
                        for b in range(4):
                            h = 4 * g + b
                            if m < LEVELS - 1:
                                mm(ps_t[:, 512 * (2 + g) + P * b:512 * (2 + g) + P * b + P], tinv_t[:, h, :], p_sb[:, h, :])
                            last = mm(ps_t[:, 512 * (4 + g) + P * b:512 * (4 + g) + P * b + P], p_sb[:, h, :], tinv_t[:, h, :])
                        last.then_inc(dt_ps, 1)
                    if m == 2:
                        pe.wait_ge(tok_d_ready, 2 * (k + 1))
                        for h in range(8):
                            c = head_col(h)
                            last = mm(ps_t[:, 3584 + 64 * h:3584 + 64 * h + 64], ak_t[:, h, :], tok[:, 1, c:c + 64])
                        last.then_inc(akv_ps, 1)
                pe.wait_ge(t_ready, base + T_INC)
                pe.wait_ge(tok_a_ready, 2 * (k + 1))
                for h in range(8):
                    g, b, c = h // 4, h % 4, head_col(h)
                    last = mm(ps_t[64 * g:64 * g + 64, 3072 + P * b:3072 + P * b + P], tok[:, 0, c:c + 64], tinv_t[:, h, :])
                last.then_inc(ht_ps, 1)
                pe.wait_ge(akv_ready, k + 1)
                for h in range(8):
                    last = mm(ps_t[:, 3584 + 64 * h:3584 + 64 * h + 64], tinv_t[:, h, :], akv[:, h, :])
                last.then_inc(g_ps, 1)
                for g in range(2):
                    r = slice(64 * g, 64 * g + 64)
                    for b in range(4):
                        o = P * b
                        mm(ps_t[:, 512 * g + o:512 * g + o + P], bt_[r, b, tk], rt_[r, b, tk])
                        last = mm(ps_t[:, 512 * (2 + g) + o:512 * (2 + g) + o + P], kt_[r, b, tk], rt_[r, b, tk])
                    last.then_inc(rb_ps, 1)
                for c in range(2):
                    n = 2 * k + c
                    q = slice(64 * c, 64 * c + 64)
                    pe.wait_ge(ht_ready, k + 1)
                    pe.wait_ge(g_ready, k + 1)
                    pe.wait_ge(s_ready, 5 * l + 1 + 2 * hf + c)
                    if c == 1:
                        pe.wait_ge(o3_ready, 2 * n)
                    for g in range(2):
                        r = slice(64 * g, 64 * g + 64)
                        for b in range(4):
                            last = mm(ps_t[q, 512 * (4 + g) + 64 * b:512 * (4 + g) + 64 * b + 64], ht_sb[r, b, q], state[r, b, :])
                    last.then_inc(u_ps, 1)
                    t0 = P * hf + 64 * c
                    for g in range(2):
                        r = slice(64 * g, 64 * g + 64)
                        for b in range(4):
                            last = mm(ps_t[r, 512 * (6 + g) + 64 * b:512 * (6 + g) + 64 * b + 64], state[r, b, :], rt_[r, b, t0:t0 + 64])
                    last.then_inc(o3_ps, 1)
                    pe.wait_ge(u_ready, 2 * (n + 1))
                    pe.wait_ge(rb_ready, 4 * (k + 1))
                    for h in range(8):
                        g, b, hc = h // 4, h % 4, head_col(h)
                        dst = ps_t[64 * g:64 * g + 64, 64 * b:64 * b + 64]
                        mm(dst, tok[q, 2, hc:hc + 64], u_sb[q, h, :], True, False)
                        last = mm(dst, tok[q, 3, hc:hc + 64], tok[q, 1, hc:hc + 64], False, True)
                    last.then_inc(s_ps, 1)
                for h in range(8):
                    g, b, hc = h // 4, h % 4, head_col(h)
                    dst = ps_t[64 * g:64 * g + 64, 512 + P * b:512 + P * b + P]
                    mm(dst, u_sb[:, h, :], lvl_l[:, h, :], True, False)
                    last = mm(dst, tok[:, 1, hc:hc + 64], ak_t[:, h, :], False, True)
                last.then_inc(o_ps, 1)

            def up_products(n, s, t, lhs, w_of, width, full):
                pe.wait_ge(up_full[s], full)
                if not isinstance(n, int) or n >= 1:
                    pe.wait_ge(actt_ready[t], n)
                    pe.wait_ge(act_ready[t], n)
                for part, ps_sem in ((0, up_g_ps[t]), (1, up_u_ps[t])):
                    w = w_of(s, part)
                    for k in range(KC):
                        last = mm(bank(2 * t + part, width), lhs(t, k), w[:, k, 0:width], k == 0, k == KC - 1)
                    last.then_inc(ps_sem, 1)
                    if part == 0 and t == 1:
                        turn(n, 0, width)

            def turn(n, t, width):
                pe.wait_ge(act_ready[t], n + 1)
                for j in range(width // P):
                    last = pe.transpose(ps_t[:, 1024 * t + P * j:1024 * t + P * j + P], act_sb[:, t, P * j:P * j + P], ident)
                last.then_inc(actt_ps[t], 1)

            def down_products(n, s, t, w_of, width, full, start):
                pe.wait_ge(down_full[s], full)
                pe.wait_ge(actt_ready[t], n + 1)
                w = w_of(s, 2)
                for j in range(width // P):
                    for c in range(2):
                        last = mm(bank(4 + 2 * t + c), act_t[:, t, P * j:P * j + P], w[:, j, 512 * c:512 * c + 512],
                                  start and j == 0, True, skip_group_check=True)
                    if t == 0 and j == width // P - 1:
                        pass
                last.then_inc(down_ps[t], 1)

            def ffn_block(n, s, use):
                tile = lambda t, k: hT[:, k, P * t:P * t + P]
                up_products(n, s, 0, tile, ffn_set, FB, 32 * use)
                up_products(n, s, 1, tile, ffn_set, FB, 32 * use)
                first = isinstance(n, int) and n == 0
                down_products(n, s, 0, ffn_set, FB, 16 * use, first)
                turn(n, 1, FB)
                down_products(n, s, 1, ffn_set, FB, 16 * use, first)

            pe.wait_ge(cst_in, 16)
            pe.wait_ge(x_in_tok, 16)
            for t in range(NT):
                for k in range(KC):
                    last = pe.transpose(ps_t[:, 1024 * t + P * k:1024 * t + P * k + P], tokm[:, t, P * k:P * k + P], ident)
                last.then_inc(xt_ps, 1)
            mod_sums(0)
            mixer(0)

            mean_square(1)
            pe.wait_ge(h_ready, KC * 2)
            pe.wait_ge(zd_free, ZD[0, "end"])
            ffn_block(0, 0, 1)
            with pe.Fori(0, (N_FFB - 1) // 2) as it:
                ffn_block(2 * it + 1, 1, it + 1)
                ffn_block(2 * it + 2, 0, it + 2)
            pe.wait_ge(f_ytok, 2)
            for k in range(KC):
                for t in range(NT):
                    last = pe.transpose(ps_t[:, SEQ * k + P * t:SEQ * k + P * t + P], tokm[:, t, P * k:P * k + P], ident)
                last.then_inc(f_tr, 1)
            mixer(1)

            mean_square(3)
            pe.wait_ge(h_ready, KC * 4)
            pe.wait_ge(zd_free, ZD[1, "end"])
            for t in range(NT):
                for k in range(KC):
                    last = mm(bank(0, NT * NE)[:, NE * t:NE * t + NE], hT[:, k, P * t:P * t + P],
                              router_sb[:, NE * k:NE * k + NE], k == 0, k == KC - 1)
            last.then_inc(logits_ps, 1)
            for t in range(NT):
                for k in range(KC):
                    o = 2048 + 1024 * t + P * k
                    last = pe.transpose(ps_t[:, o:o + P], hT[:, k, P * t:P * t + P], ident)
            last.then_inc(htok_ps, 1)
            pe.wait_ge(r_sel_ready, 1)
            rank, half0, half1 = cc(C_RANK), r_sel[:, 0:NE], r_sel[:, NE:2 * NE]
            mm(ps_t[:, 512:512 + NE], rank, half0)
            mm(ps_t[:, 512 + NE:512 + 2 * NE], rank, half1, True, False)
            mm(ps_t[:, 512 + NE:512 + 2 * NE], ones, half0, False, True)
            mm(ps_t[:, 512 + 2 * NE:512 + 3 * NE], ones, half0, True, False)
            mm(ps_t[:, 512 + 2 * NE:512 + 3 * NE], ones, half1, False, True).then_inc(rank_ps, 1)

            pe.wait_ge(jobs_ready, 1)
            pe.wait_ge(htok_ready, 1)
            n_pairs = pe.value_load(job_i[0:1, N_JOBS:N_JOBS + 1], min_val=NE // 2, max_val=N_JOBS // 2)
            slots = lambda s, k: h_sel[:, KC * s + k, :]
            uses = ((N_FFB + 1) // 2, N_FFB // 2)
            with pe.Fori(0, n_pairs) as pair:
                pe.wait_ge(sel_ready, 8 * (pair + 1))
                pe.wait_ge(comb_done, pair + 1)
                for s in range(2):
                    for t in range(NT):
                        o = 3072 + SEQ * s + P * t
                        last = pe.transpose(ps_t[:, o:o + P], sel_g[:, 2 * s + t, :], ident)
                last.then_inc(gather_ps, 1)
                for s in range(2):
                    for k in range(KC):
                        o = 2048 * s + P * k
                        for t in range(NT):
                            last = mm(ps_t[:, o:o + P], tokm[:, t, P * k:P * k + P], sel[:, 2 * s + t, :], t == 0, t == 1)
                    last.then_inc(gather_ps, 1)
                pe.wait_ge(gather_ready, pair + 1)
                pe.wait_ge(gather_d_ready, 2 * (pair + 1))
                for c in range(4):
                    mm(bank(4 + c), zeros16[:, 0:P], zeros16[:, 0:512], True, True, skip_group_check=True)
                with pe.Fori(0, N_EB) as b:
                    m = pair * N_EB + b
                    n = N_FFB + m
                    up_products(n, 0, 0, slots, moe_set, EB, 32 * (uses[0] + 1) + 32 * m)
                    up_products(n, 1, 1, slots, moe_set, EB, 32 * (uses[1] + 1) + 32 * m)
                    down_products(n, 0, 0, moe_set, EB, 16 * (uses[0] + 1) + 16 * m, False)
                    turn(n, 1, EB)
                    down_products(n, 1, 1, moe_set, EB, 16 * (uses[1] + 1) + 16 * m, False)
                pe.wait_ge(y_ready, 2 * (pair + 1))
                for k in range(KC):
                    for s in range(2):
                        last = mm(ps_t[:, SEQ * k:SEQ * k + SEQ], y_slot[:, s, P * k:P * k + P], sel_t[:, s, :], s == 0, s == 1)
                last.then_inc(comb_ps, 1)

            mean_square(4)
            pe.wait_ge(h_ready, KC * 5)
            for t in range(NT):
                for k in range(KC):
                    o = 1024 * t + P * k
                    last = pe.transpose(ps_t[:, o:o + P], hT[:, k, P * t:P * t + P], ident)
                last.then_inc(out_ps, 1)


def kernel(**inputs):
    import numpy as _np
    import concourse.bacc as _bacc
    from concourse import mybir as _mybir
    from concourse.bass_utils import run_bass_kernel_spmd as _run

    a = {k: _np.ascontiguousarray(v) for k, v in inputs.items()}

    def columns(v):
        return v.reshape(-1, P).T

    params = _np.zeros((P, P_END), _np.float32)
    for l in range(DEPTH):
        parts = {"norm_g": a["norm_g"][l], "ada_b": a["ada_b"][l], "pool_scale": a["pool_scale"][l],
                 "conv_b": a["conv_b"][l], "ln_g": a["conv_ln_g"][l], "ln_b": a["conv_ln_b"][l],
                 "mu": a["rwkv_mu"][l], "a0": a["rwkv_a0"][l], "kk_scale": a["rwkv_kk_scale"][l],
                 "ka": a["rwkv_ka"][l], "rk": a["rwkv_rk"][l], "lnx_g": a["rwkv_lnx_g"][l],
                 "lnx_b": a["rwkv_lnx_b"][l]}
        for name, v in parts.items():
            c = columns(v)
            o = l * P_W + P_OFF[name]
            params[:, o:o + c.shape[1]] = c
        o = l * P_W + P_OFF["conv_w"]
        for b in range(2):
            params[:, o + b * CONV_K:o + (b + 1) * CONV_K] = a["conv_w"][l][:, P * b:P * b + P].T
        if l > 0:
            params[VR, l * P_W + P_OFF["vmu"]] = a["vres_mu"][l - 1]
            o = l * P_W + P_OFF["v0"]
            params[:, o:o + 4] = columns(a["vres_v0"][l - 1])
    params[:, P_C:P_C + KC] = columns(a["c"][0])
    params[:, P_FG:P_FG + KC] = columns(a["final_norm_g"])

    arrays = {
        "x": a["x"][0], "consts": shape_constants(), "params": params, "ada_w": a["ada_w"], "w_in": a["w_in"],
        "pool_w": a["pool_w"], "pool_proj": a["pool_proj"], "conv_proj": a["conv_proj"], "w0": a["rwkv_w0"],
        "w2": a["rwkv_w2"], "a2": a["rwkv_a2"], "g2": a["rwkv_g2"], "rwkv_proj": a["rwkv_proj"],
        "vres_down": a["vres_w_down"], "vres_v2": a["vres_v2"], "w_o": a["w_o"], "ffn_w1": a["ffn_w1"][0],
        "ffn_w3": a["ffn_w3"][0], "ffn_w2": a["ffn_w2"][0], "router": a["moe_router"][0],
        "moe_w1": a["moe_w1"][0], "moe_w3": a["moe_w3"][0], "moe_w2": a["moe_w2"][0],
    }
    nc = _bacc.Bacc("TRN2", target_bir_lowering=False, num_devices=1)
    f32 = _mybir.dt.float32
    args = [nc.dram_tensor(f"in_{n}", v.shape, f32, kind="ExternalInput").ap() for n, v in arrays.items()]
    y = nc.dram_tensor("out_y", (SEQ, D), f32, kind="ExternalOutput").ap()
    build_trunk(nc, *args, y)
    r = _run(nc, [{f"in_{n}": v for n, v in arrays.items()}], core_ids=[0])
    return r.results[0]["out_y"].reshape(1, SEQ, D)
```

```python
from contextlib import ExitStack

import numpy as np

import concourse.bass as bass
from concourse import mybir

P = 128
D = 1024
SEQ = 256
DEPTH = 2
KC = D // P
NT = SEQ // P
CONV_K = 31
NB_RKV = 12
COL_RWKV, COL_GATE = 768, 2432
GATE_R, GATE_P, GATE_C = COL_GATE + 2 * D, COL_GATE, COL_GATE + D
D_FF, D_FFE, NE = 2816, 3584, 8
FB = 256
EB = 512
N_FFB = D_FF // FB
N_EB = D_FFE // EB
N_JOBS = 12
N_RAW_P, N_SPLIT = 6, 3
FFN_PIECES, MOE_PIECES = 3, 12
CH = 64
VR = slice(64, 80)
N_RAW = 2
LEVELS = 6
DECAY = float(np.exp(-0.5))
PAD_P, PAD_C = 16, CONV_K - 1
MIX_FILLS = 16

C_ID, C_ONES, C_BONES, C_TRI_S, C_TRI_I, C_LOW0 = (P * i for i in range(6))
C_LVL = 6 * P
C_RANK = C_LVL + LEVELS * P
C_IOTA = C_RANK + P
C_CNT = C_IOTA + P
C_LOW8 = C_CNT + 2 * SEQ
C_EID = C_LOW8 + NE * NE
C_M256 = C_EID + NE
C_ZERO = C_M256 + P
C_END = C_ZERO + 256

PARAMS = [("norm_g", 16), ("ada_b", 48), ("pool_scale", 2), ("conv_w", 2 * CONV_K), ("conv_b", 2),
          ("ln_g", 2), ("ln_b", 2), ("mu", 13), ("a0", 4), ("kk_scale", 4), ("ka", 4),
          ("rk", 4), ("lnx_g", 4), ("lnx_b", 4), ("vmu", 1), ("v0", 4)]
P_OFF = {}
_at = 0
for _n, _w in PARAMS:
    P_OFF[_n] = _at
    _at += _w
P_W = _at
P_C = DEPTH * P_W
P_FG = P_C + KC
P_END = P_FG + KC


def shape_constants():
    i = np.arange(P)
    row, col = i[:, None], i[None, :]
    same = row // CH == col // CH
    c = np.zeros((P, C_END), np.float32)
    c[:, C_ID:C_ID + P] = row == col
    c[:, C_ONES:C_ONES + P] = 1
    c[:, C_BONES:C_BONES + P] = same
    c[:, C_TRI_S:C_TRI_S + P] = same & (row < col)
    c[:, C_TRI_I:C_TRI_I + P] = same & (row <= col)
    for m in range(LEVELS):
        n = 1 << m
        lvl = (row // (2 * n) == col // (2 * n)) & (row % (2 * n) < n) & (col % (2 * n) >= n)
        c[:, C_LVL + m * P:C_LVL + (m + 1) * P] = lvl
    c[:, C_LOW0:C_LOW0 + P] = c[:, C_LVL:C_LVL + P].T
    c[:, C_RANK:C_RANK + P] = row < col
    c[:, C_IOTA:C_IOTA + P] = col
    pos = np.arange(1, SEQ + 1)
    for b in range(2):
        for par in range(2):
            win = 2 ** (2 * b + par + 1)
            c[64 * par:64 * par + 64, C_CNT + b * SEQ:C_CNT + (b + 1) * SEQ] = \
                1.0 / np.minimum(pos, win).astype(np.float32)
    low = (np.arange(NE)[:, None] > np.arange(NE)[None, :]).astype(np.float32)
    c[:, C_LOW8:C_LOW8 + NE * NE] = low.reshape(1, -1)
    c[:, C_EID:C_EID + NE] = np.arange(NE)
    c[:, C_M256:C_M256 + P] = 1.0 / 256
    return c


def build_trunk(nc, x_in, consts, params, ada_w, w_in, pool_w, pool_proj, conv_proj, w0_row,
                w2, a2, g2, rwkv_proj, vres_down, vres_v2, w_o, ffn_w1, ffn_w3, ffn_w2,
                router, moe_w1, moe_w3, moe_w2, out):
    f32, i32 = mybir.dt.float32, mybir.dt.int32
    ALU, ACT, AX = mybir.AluOpType, mybir.ActivationFunctionType, mybir.AxisListType
    ds = bass.ds
    ctx = ExitStack()
    with ctx:
        def sb(name, cols, dt=f32):
            return ctx.enter_context(nc.sbuf_tensor(name, [P, cols], dt))

        def sem(name):
            return ctx.enter_context(nc.semaphore(name))

        def v3(t, a, n, w):
            return t[:, a:a + n * w].rearrange("p (n w) -> p n w", w=w)

        ring = sb("ring", 3 * 4096)
        scr_at = nc.sbuf_base
        scr = sb("scr", 3 * 4096)
        e1, e2, a_b, kk_a, gg, bon = (v3(scr, 1024 * i, 4, SEQ) for i in range(6))
        ltm, lvl_l, tinv, tinv_t, p_sb, ak_t = (v3(scr, 6144 + 1024 * i, 8, P) for i in range(6))
        sig_tok = v3(scr, 6144, NT, 512)
        o_state, o_all = e1, e2
        inv4_t = scr[:, 8192:9216]
        inv4 = v3(scr, 8192, 4, SEQ)
        rkv_at = nc.sbuf_base
        rkv_t = sb("rkv", NB_RKV * SEQ)
        rkv = v3(rkv_t, 0, NB_RKV, SEQ)
        rr, kkv, vv = rkv[:, 0:4, :], rkv[:, 4:8, :], rkv[:, 8:12, :]
        lora_in = sb("lora_in", SEQ)
        vres_in = sb("vres_in", SEQ)
        sg_t = sb("sg", 2 * SEQ)
        raw_t = sb("raw", N_RAW * (SEQ + 1))
        raw = v3(raw_t, 0, N_RAW, SEQ + 1)
        v_first = sb("v_first", 4 * SEQ)
        state_t = sb("state", 256)
        state = v3(state_t, 0, 4, 64)
        chunk_decay = sb("chunk_decay", 16)
        x_t = sb("x", KC * SEQ)
        xT = v3(x_t, 0, KC, SEQ)
        h_at = nc.sbuf_base
        h_t = sb("h", KC * SEQ)
        hT = v3(h_t, 0, KC, SEQ)
        merged_t = sb("merged", KC * SEQ)
        merged = v3(merged_t, 0, KC, SEQ)
        yT = merged
        gr_t = sb("gate_r", KC * SEQ)
        gate_r = v3(gr_t, 0, KC, SEQ)
        tokm = v3(gr_t, 0, NT, D)
        pu = sb("pool_u", 2 * (PAD_P + SEQ))
        pa = sb("pool_a", 2 * (PAD_P + SEQ))
        pbuf = sb("pool_b", 2 * (PAD_P + SEQ))
        pu3, pa3, pb3 = (v3(t, 0, 2, PAD_P + SEQ) for t in (pu, pa, pbuf))
        ca_t = sb("conv_a", 2 * (PAD_C + SEQ))
        ca = v3(ca_t, 0, 2, PAD_C + SEQ)
        cb_t = sb("conv_b_", 2 * SEQ)
        cb = v3(cb_t, 0, 2, SEQ)
        cy_t = sb("conv_y", 2 * SEQ)
        cy = v3(cy_t, 0, 2, SEQ)
        sg = v3(sg_t, 0, 2, SEQ)
        pl = sg
        tmp = sb("tmp", SEQ)
        rstd = sb("rstd", SEQ)
        wide_at = nc.sbuf_base
        wide = sb("wide", 6 * 1024)
        ada_ring = v3(wide, 0, 3, 1024)
        ada_acc = wide[:, 3072:6144]
        tok = v3(wide, 0, 4, 512)
        ht_sb = v3(wide, 2048, 4, P)
        akv, g_sb, u_sb = (v3(wide, 2560 + 512 * i, 8, 64) for i in range(3))
        act_sb = v3(wide, 0, 2, 512)
        sig_sb = v3(wide, 2048, 2, 512)
        y_slot = v3(wide, 3072, 2, D)
        sel = v3(wide, 5120, 4, P)
        sel_g = v3(wide, 5632, 4, P)
        lora_w = sb("lora_w", 512)
        w0_sb = sb("w0_sb", 512)
        pool_wsb = sb("pool_wsb", 2 * 64)
        sel_t_t = v_first[:, 0:2 * SEQ]
        sel_t = v3(v_first, 0, 2, SEQ)
        cst = sb("cst", C_END)
        par = sb("par", P_END)
        mods_t = sb("mods", 4 * 24)
        mods = v3(mods_t, 0, 4, 24)
        gain_t = sb("gain", 4 * 8)
        gain = v3(gain_t, 0, 4, 8)
        c_sig = sb("c_sig", KC)
        c_silu = sb("c_silu", KC)
        router_sb = sb("router_sb", KC * NE)

        f32r = mybir.dt.float32r

        def over_sb(name, at, n, w):
            t = nc.alloc_sbuf_tensor_at(name, [P, n * w], f32r, offset=at)
            return t[:, :].rearrange("p (n w) -> p n w", w=w)

        PW = 2048
        w_hi = over_sb("w_hi", scr_at, N_SPLIT, PW)
        w_lo = over_sb("w_lo", scr_at + 4 * N_SPLIT * PW, N_SPLIT, PW)
        f_hi = over_sb("f_hi", rkv_at, 2 * KC, P)
        f_lo = over_sb("f_lo", rkv_at + 4 * 2048, 2 * KC, P)
        act_hi = over_sb("act_hi", wide_at + 4096, 2, 512)
        act_lo = over_sb("act_lo", h_at, 2, 512)
        pieces = v3(ring, 0, N_RAW_P, PW)

        widths = [NT * NE] * 6 + [NT, NT] + [NE] * 3 + [4 * NE] + [NT * N_JOBS] * 2
        starts = [sum(widths[:i]) for i in range(len(widths))]
        (lg, r_cnt, r_sel, r_exp, r_gate, r_rank, r_max, r_den, n_tok, over, prev, onehot, job_rank,
         job_gate) = (pbuf[:, o:o + w] for o, w in zip(starts, widths))
        cmp_t = pu[:, 0:NT * NE * NE]
        cmp2_t = pu[:, NT * NE * NE:2 * NT * NE * NE]
        job_f = sb("job_f", N_JOBS + 4)
        job_i = sb("job_i", N_JOBS + 4, i32)

        ps_t = ctx.enter_context(nc.psum_tensor("ps", [P, 8 * 512], f32))
        ps = ps_t[:, :].rearrange("p (b n) -> p b n", b=8)

        def bank(b, n=512, p0=0, p1=P):
            return ps_t[p0:p1, 512 * b:512 * b + n]

        def cc(col, n=P, p0=0, p1=P):
            return cst[p0:p1, col:col + n]

        def pcol(l, name, i=0, p0=0, p1=P):
            o = l * P_W + P_OFF[name] + i
            return par[p0:p1, o:o + 1]

        ident, ones, bones, mean256 = cc(C_ID), cc(C_ONES), cc(C_BONES), cc(C_M256)
        zeros16 = cst[:, C_ZERO:C_ZERO + 256].bitcast(mybir.dt.bfloat16)


        def places(groups):
            at, first = 0, {}
            for l in range(DEPTH):
                for name, n in groups(l):
                    first[l, name] = at
                    at += n
                first[l, "end"] = at
            return first

        ZA = places(lambda l: [("z", NB_RKV + 1 + l), ("pc", 6), ("a", 4), ("g", 4), ("vres", 4 * l),
                               ("gate_r", KC), ("gate_p", KC), ("gate_c", KC)])
        ZD = places(lambda l: [("kk", 4), ("bonus", 4), ("y_pool", KC), ("y_conv", KC), ("mean", 4),
                               ("var", 4), ("y_rwkv", KC), ("w_o", KC)])

        ZMIX = (0, NB_RKV + 1)
        T_INC = 4 * LEVELS
        SMALL = (16 * 10, 16 * 18)

        def head_col(h):
            return P * (h % 4) + 64 * (h // 4)

        cst_in, par_in, x_in_tok, small_in = sem("cst_in"), sem("par_in"), sem("x_in_tok"), sem("small_in")
        ada_full = [sem(f"ada_full{i}") for i in range(3)]
        ada_free, ada_sum, mod_ps, mods_ready = sem("ada_free"), sem("ada_sum"), sem("mod_ps"), sem("mods_ready")
        ring_full = [sem(f"ring_full{i}") for i in range(3)]
        za_ready, za_done, zd_ready, zd_free = sem("za_ready"), sem("za_done"), sem("zd_ready"), sem("zd_free")
        mix_done, pads_ready = sem("mix_done"), sem("pads_ready")
        x_ready, xsq_ready, ssum_ps, h_ready, xt_ps = sem("x_ready"), sem("xsq_ready"), sem("ssum_ps"), sem("h_ready"), sem("xt_ps")
        c_sig_ready = sem("c_sig_ready")
        pooled, pool_ps, pool_y = sem("pooled"), sem("pool_ps"), sem("pool_y")
        conv_dev, gather_d_ready = sem("conv_dev"), sem("gather_d_ready")
        conv_u, conv_mean, conv_sq, conv_var, conv_un, conv_sg, conv_y = (
            sem(n) for n in ("conv_u", "conv_mean", "conv_sq", "conv_var", "conv_un", "conv_sg", "conv_y"))
        lora_ready, sigt_ps, sigt_ready = sem("lora_ready"), sem("sigt_ps"), sem("sigt_ready")
        kk_ready, kksq_ready, rkk_ready, cum_ps = sem("kk_ready"), sem("kksq_ready"), sem("rkk_ready"), sem("cum_ps")
        decay_ready, decay_used, tilde_ready = sem("decay_ready"), sem("decay_used"), sem("tilde_ready")
        amat_ps, amat_ready, tok_ps, tok_a_ready, tok_d_ready = (
            sem(n) for n in ("amat_ps", "amat_ready", "tok_ps", "tok_a_ready", "tok_d_ready"))
        lvl_ready, p_ps, p_ready, dt_ps, t_ready = (sem(n) for n in ("lvl_ready", "p_ps", "p_ready", "dt_ps", "t_ready"))
        ht_ps, ht_ready, akv_ps, akv_ready, g_ps, g_ready = (
            sem(n) for n in ("ht_ps", "ht_ready", "akv_ps", "akv_ready", "g_ps", "g_ready"))
        rb_ps, rb_ready, u_ps, u_ready, o3_ps, o3_ready, s_ps, s_ready = (
            sem(n) for n in ("rb_ps", "rb_ready", "u_ps", "u_ready", "o3_ps", "o3_ready", "s_ps", "s_ready"))
        o_ps, o_ready, o_dev, o_sq, o_final, merged_ready = (
            sem(n) for n in ("o_ps", "o_ready", "o_dev", "o_sq", "o_final", "merged_ready"))
        piece_full = [sem(f"piece_full{i}") for i in range(N_RAW_P)]
        hi_ready, split_ready, piece_used = sem("hi_ready"), sem("split_ready"), sem("piece_used")
        tile0_ps, f_hi_ready, f_lo_ready = sem("tile0_ps"), sem("f_hi_ready"), sem("f_lo_ready")
        sig_ready = [sem(f"sig_ready{i}") for i in range(2)]
        silu_ready = [sem(f"silu_ready{i}") for i in range(2)]
        act_ready = [sem(f"act_ready{i}") for i in range(2)]
        actt_ps = [sem(f"actt_ps{i}") for i in range(2)]
        act_hi_ready = [sem(f"act_hi_ready{i}") for i in range(2)]
        act_lo_ready = [sem(f"act_lo_ready{i}") for i in range(2)]
        f_ytok, f_tr = sem("f_ytok"), sem("f_tr")
        htok_ps, htok_ready = sem("htok_ps"), sem("htok_ready")
        logits_ps, r_maxed, r_exped, r_sel_ready, rank_ps, jobs_ready = (
            sem(n) for n in ("logits_ps", "r_maxed", "r_exped", "r_sel_ready", "rank_ps", "jobs_ready"))
        sel_ready, gather_ps, y_ready, comb_ps, comb_done = (
            sem(n) for n in ("sel_ready", "gather_ps", "y_ready", "comb_ps", "comb_done"))
        out_ps, out_rows, out_done = sem("out_ps"), sem("out_rows"), sem("out_done")
        dve_chain, pool_chain = sem("dve_chain"), sem("pool_chain")
        inv_in, rstd_ready = sem("inv_in"), sem("rstd_ready")

        def cols_of(l, c0, n):
            return w_in[l, :, c0:c0 + n].rearrange("(k p) c -> p k c", p=P)

        def rows_of(w, k0, n):
            return w[k0 * P:(k0 + n) * P, :].rearrange("(k p) c -> p k c", p=P)

        def mixer_fills(l):
            z, zd = lambda name, n: (za_ready, ZA[l, name] + n), lambda name, n: (zd_ready, ZD[l, name] + n)
            fills = [([(0, cols_of(l, COL_RWKV + 512 * i, 512))], z("z", 4 * i + 4)) for i in range(3)]
            last = [(0, cols_of(l, COL_RWKV + 1536, P))]
            if l > 0:
                last.append((KC * P, rows_of(vres_down[l - 1], 0, KC)))
            fills.append((last, z("z", NB_RKV + 1 + l)))
            fills.append(([(0, cols_of(l, 0, 512))], z("pc", 4)))
            fills.append(([(0, cols_of(l, 512, 256))], z("pc", 6)))
            fills += [([(0, cols_of(l, GATE_R + 512 * i, 512))], z("gate_r", 4 * i + 4)) for i in range(2)]
            fills.append(([(0, cols_of(l, GATE_P, 512))], z("gate_p", 4)))
            fills.append(([(0, rows_of(pool_proj[l], 0, 2)), (2048, rows_of(conv_proj[l], 0, 2))],
                          zd("y_conv", KC)))
            fills.append(([(0, cols_of(l, GATE_P + 512, 512))], z("gate_p", 8)))
            fills += [([(0, cols_of(l, GATE_C + 512 * i, 512))], z("gate_c", 4 * i + 4)) for i in range(2)]
            fills.append(([(0, rows_of(rwkv_proj[l], 0, 4))], zd("y_rwkv", KC)))
            fills += [([(0, rows_of(w_o[l], 4 * i, 4))], zd("w_o", KC)) for i in range(2)]
            return fills

        SLOT = [0, 1, 2, 0, 1, 2, 0, 1, 2, 0, 1, 2, 1, 2, 0, 1]
        FILLS, FULL, AFTER = [], [], []
        last_in, landed = {}, {}
        for l in range(DEPTH):
            for i, (dmas, free) in enumerate(mixer_fills(l)):
                s = SLOT[i]
                FILLS.append((s, dmas))
                AFTER.append(last_in.get(s))
                landed[s] = landed.get(s, 0) + 16 * len(dmas)
                FULL.append(landed[s])
                last_in[s] = free
            last_in = {}

        def fill_at(n, width, off=0, k=None):
            base = 4096 * FILLS[n][0] + off
            k = k or 4096 // width
            return ring[:, base:base + k * width].rearrange("p (k c) -> p k c", c=width)

        N_FFN_P = FFN_PIECES * N_FFB

        def piece_at(n):
            return N_FFN_P + MOE_PIECES * n

        FULL0 = [len(range(i, N_FFN_P, N_RAW_P)) for i in range(N_RAW_P)]

        block = ctx.enter_context(nc.Block())

        @block.sync
        def _(sp):
            sp.dma_start(tokm, x_in.rearrange("(t p) d -> p t d", p=P)).then_inc(x_in_tok, 16)
            sp.dma_start(cst[:, :], consts).then_inc(cst_in, 16)

            def mixer_weights(l):
                for i in range(MIX_FILLS):
                    n = MIX_FILLS * l + i
                    s, dmas = FILLS[n]
                    if AFTER[n] is not None:
                        sp.wait_ge(*AFTER[n])
                    for off, src in dmas:
                        k, w = src.shape[1], src.shape[2]
                        sp.dma_start(fill_at(n, w, off, k), src).then_inc(ring_full[s], 16)

            def ffn_weights(n, parity):
                for part, w in enumerate((ffn_w1, ffn_w3, ffn_w2)):
                    slot = 3 * parity + part
                    if not isinstance(n, int) or n >= 2:
                        sp.wait_ge(split_ready, 3 * n + part - N_RAW_P + 1)
                    src = w[:, ds(n * FB, FB)] if part < 2 else w[ds(n * FB, FB), :]
                    dst = pieces[:, slot, :].rearrange("p (k c) -> p k c", c=FB if part < 2 else D)
                    sp.dma_start(dst, src.rearrange("(k p) c -> p k c", p=P)).then_inc(piece_full[slot], 16)

            def moe_piece(m, b, e, i):
                s, part = (i // 4, i % 4 // 2) if i < 8 else ((i - 8) // 2, 2)
                half = i % 2
                if not isinstance(m, int) or m > 0 or i >= N_RAW_P:
                    sp.wait_ge(split_ready, piece_at(m) + i - N_RAW_P + 1)
                if part < 2:
                    src = (moe_w1, moe_w3)[part][ds(e[s], 1), 512 * half:512 * half + 512, ds(b * EB, EB)]
                else:
                    src = moe_w2[ds(e[s], 1), ds(b * EB + 256 * half, 256), :]
                dst = pieces[:, i % N_RAW_P, :].rearrange("p (k c) -> p k c", c=EB if part < 2 else D)
                sp.dma_start(dst, src.rearrange("o (k p) c -> p (o k) c", p=P)).then_inc(piece_full[i % N_RAW_P], 16)

            mixer_weights(0)
            sp.wait_ge(zd_ready, ZD[0, "end"])
            ffn_weights(0, 0)
            ffn_weights(1, 1)
            ffn_weights(2, 0)
            with sp.Fori(0, (N_FFB - 3) // 2) as it:
                ffn_weights(2 * it + 3, 1)
                ffn_weights(2 * it + 4, 0)
            sp.wait_ge(split_ready, N_FFN_P)
            mixer_weights(1)

            sp.wait_ge(zd_ready, ZD[1, "end"])
            for i in range(N_RAW_P):
                moe_piece(0, 0, (0, 1), i)
            sp.wait_ge(jobs_ready, 1)
            n_pairs = sp.value_load(job_i[0:1, N_JOBS:N_JOBS + 1], min_val=NE // 2, max_val=N_JOBS // 2)
            for i in range(N_RAW_P, MOE_PIECES):
                moe_piece(0, 0, (0, 1), i)
            with sp.Fori(1, N_EB) as b:
                for i in range(MOE_PIECES):
                    moe_piece(b, b, (0, 1), i)
            with sp.Fori(1, n_pairs) as pair:
                e = [sp.value_load(job_i[0:1, ds(2 * pair + s, 1)], min_val=0, max_val=NE - 1) for s in range(2)]
                with sp.Fori(0, N_EB) as b:
                    for i in range(MOE_PIECES):
                        moe_piece(pair * N_EB + b, b, e, i)
            for t in range(NT):
                sp.wait_ge(out_rows, t + 1)
                sp.dma_start(out.rearrange("(t p) d -> t p d", p=P)[t], tokm[:, t, :]).then_inc(out_done, 16)
            sp.wait_ge(out_done, 16 * NT)

        @block.gpsimd
        def _(pool):
            chain = [0]

            def link(ins):
                chain[0] += 1
                ins.then_inc(pool_chain, 1)
                pool.wait_ge(pool_chain, chain[0])
                return ins

            pool.dma_start(par[:, :], params).then_inc(par_in, 16)
            ada_rows = ada_w.rearrange("l i (k p) (t c) -> (l i k) t p c", p=P, c=1024)

            def ada_stream(first, last):
                with pool.Fori(first, last) as r:
                    for t in range(3):
                        pool.wait_ge(ada_free, 3 * r + t + 1)
                        pool.dma_start(ada_ring[:, t, :], ada_rows[ds(r, 1), t].rearrange("o p c -> (o p) c")
                                       ).then_inc(ada_full[t], 16)

            def small_weights(l):
                pool.dma_start(lora_w[0:32, :], w2[l]).then_inc(small_in, 16)
                pool.dma_start(lora_w[32:64, :], a2[l]).then_inc(small_in, 16)
                pool.dma_start(lora_w[64:P, :], g2[l]).then_inc(small_in, 16)
                pool.dma_start(w0_sb[0:1, :], w0_row[l:l + 1, :]).then_inc(small_in, 16)
                for g in range(4):
                    q = 64 * (g % 2)
                    pool.dma_start(pool_wsb[q:q + 64, 64 * (g // 2):64 * (g // 2) + 64],
                                   pool_w[l, g]).then_inc(small_in, 16)
                if l == 0:
                    pool.dma_start(w0_sb[VR, :], vres_v2[0]).then_inc(small_in, 16)
                    pool.dma_start(router_sb[:, :].rearrange("p (k e) -> p k e", e=NE),
                                   router.rearrange("(k p) e -> p k e", p=P)).then_inc(small_in, 16)

            def pooling(l):
                pool.wait_ge(za_done, ZA[l, "pc"] + 2)
                src = pu3
                for g, dst in enumerate((pa3, pb3, pa3, pb3)):
                    sh = 1 << g
                    lo = 2 * sh - 1
                    link(pool.tensor_tensor(dst[:, :, lo:], src[:, :, lo:],
                                            src[:, :, lo - sh:PAD_P + SEQ - sh], ALU.add))
                    q, b = slice(64 * (g % 2), 64 * (g % 2) + 64), g // 2
                    link(pool.tensor_tensor(pl[q, b, :], dst[q, b, PAD_P:],
                                            cst[q, C_CNT + b * SEQ:C_CNT + (b + 1) * SEQ], ALU.mult))
                    pool.tensor_tensor(pl[q, b, :], pl[q, b, :], pu3[q, b, PAD_P:], ALU.subtract
                                       ).then_inc(pooled, 1)
                    pool.wait_ge(pooled, 4 * l + g + 1)
                    src = dst

            def level_masks(l, hf):
                for m in range(1, LEVELS):
                    for g in range(2):
                        if m == 1:
                            pool.wait_ge(amat_ready, 2 * (2 * l + hf) + g + 1)
                        else:
                            pool.wait_ge(p_ps, ((2 * l + hf) * (LEVELS - 1) + m - 2) * 2 + g + 1)
                        pool.tensor_tensor(lvl_l[:, 4 * g:4 * g + 4, :], ltm[:, 4 * g:4 * g + 4, :],
                                           cc(C_LVL + m * P).unsqueeze(1).broadcast_to([P, 4, P]), ALU.mult
                                           ).then_inc(lvl_ready, 1)

            ada_stream(0, 8)
            small_weights(0)
            pool.wait_ge(cst_in, 16)
            pool.wait_ge(pads_ready, 1)
            ada_stream(8, 16)
            pooling(0)
            ada_stream(16, 32)
            level_masks(0, 0)
            level_masks(0, 1)
            pool.wait_ge(o_final, 1)
            small_weights(1)
            pooling(1)
            level_masks(1, 0)
            level_masks(1, 1)

        @block.scalar
        def _(act):
            za = [0]

            def evac(dst, func=ACT.Identity, rows=slice(0, P), **kw):
                n = za[0]
                za[0] += 1
                act.wait_ge(za_ready, n + 1)
                act.activation(dst, bank(n % 2, SEQ)[rows, :], func, **kw).then_inc(za_done, 1)

            roots = [0]

            def root(a):
                roots[0] += 1
                act.wait_ge(inv_in, roots[0])
                act.activation(a, a, ACT.Sqrt).then_inc(rstd_ready, 1)

            def square_x(li):
                act.wait_ge(x_ready, KC * (li + 1))
                act.activation(h_t[:, :], x_t[:, :], ACT.Square, scale=1.0 / 32).then_inc(xsq_ready, 1)
                root(rstd[:, :])

            def mixer(l):
                square_x(2 * l)
                for b in range(NB_RKV + 1 + l):
                    n = ZMIX[l] + b
                    if n >= N_RAW:
                        act.wait_ge(mix_done, n - N_RAW + 1)
                    rows = VR if b > NB_RKV else slice(0, P)
                    evac(raw[rows, n % N_RAW, 1:SEQ + 1], rows=rows)
                if l == 0:
                    act.wait_ge(pads_ready, 1)
                for b in range(2):
                    evac(pu3[:, b, PAD_P:])
                for b in range(2):
                    evac(ca[:, b, PAD_C:])
                for b in range(2):
                    evac(cb[:, b, :], ACT.Sigmoid)
                act.wait_ge(mix_done, ZMIX[l] + NB_RKV + 1)
                act.activation(lora_in[0:32, :], lora_in[0:32, :], ACT.Tanh).then_inc(lora_ready, 1)
                act.activation(lora_in[64:P, :], lora_in[64:P, :], ACT.Sigmoid).then_inc(lora_ready, 1)
                act.wait_ge(sigt_ps, l + 1)
                act.activation(scr[:, 6144:7168], ps_t[:, 5 * 512:7 * 512], ACT.Sigmoid).then_inc(sigt_ready, 1)
                for b in range(4):
                    evac(a_b[:, b, :], ACT.Sigmoid, bias=pcol(l, "a0", b))
                for b in range(4):
                    evac(gg[:, b, :])
                for b in range(4 * l):
                    evac(bon[:, b, :], ACT.Sigmoid, bias=pcol(l, "v0", b))
                act.wait_ge(kk_ready, 4 * (l + 1))
                act.activation(e1[:, :, :], kk_a[:, :, :], ACT.Square).then_inc(kksq_ready, 1)
                root(inv4_t)
                act.wait_ge(cum_ps, l + 1)
                act.wait_ge(zd_ready, ZD[l, "kk"] + 4)
                act.activation(scr[:, 0:1024], ps_t[:, 6 * 512:8 * 512], ACT.Exp, scale=-DECAY).then_inc(decay_ready, 1)
                act.wait_ge(zd_ready, ZD[l, "bonus"] + 4)
                act.activation(scr[:, 1024:2048], ps_t[:, 4 * 512:6 * 512], ACT.Exp, scale=DECAY).then_inc(decay_ready, 1)
                act.wait_ge(decay_used, l + 1)
                act.activation(scr[:, 0:1024], ps_t[:, 4 * 512:6 * 512], ACT.Exp, scale=-DECAY).then_inc(decay_ready, 1)
                for b in range(KC):
                    evac(gate_r[:, b, :], ACT.Sigmoid)
                act.wait_ge(pool_ps, l + 1)
                for b in range(2):
                    for q in range(2):
                        r = slice(64 * q, 64 * q + 64)
                        act.activation(pa3[r, b, PAD_P:], ps_t[r, 512 * (4 + q) + SEQ * b:512 * (4 + q) + SEQ * (b + 1)],
                                       ACT.Identity, scale=pcol(l, "pool_scale", b, 64 * q, 64 * q + 64)).then_inc(pool_y, 1)
                for b in range(KC):
                    if b >= 2:
                        act.wait_ge(zd_free, ZD[l, "y_pool"] + b - 1)
                    evac(sg[:, b % 2, :], ACT.Sigmoid)
                act.wait_ge(conv_dev, 2 * (l + 1))
                act.activation(cb_t[:, :], cy_t[:, :], ACT.Square).then_inc(conv_sq, 1)
                root(rstd[:, :])
                act.wait_ge(conv_un, 2 * (l + 1))
                act.activation(cb_t[:, :], cy_t[:, :], ACT.Sigmoid).then_inc(conv_sg, 1)
                for b in range(KC):
                    act.wait_ge(zd_free, ZD[l, "y_pool"] + KC + b - 1)
                    evac(sg[:, b % 2, :], ACT.Sigmoid)
                for hf in range(NT):
                    wkv_half(l, hf)
                for b in range(4):
                    act.wait_ge(o_dev, 4 * l + b + 1)
                    act.activation(e1[:, b, :], o_all[:, b, :], ACT.Square).then_inc(o_sq, 1)
                root(inv4_t)

            def wkv_half(l, hf):
                k = 2 * l + hf
                for i, kind in enumerate((0, 2)):
                    act.wait_ge(tok_ps, 4 * k + 2 * i + 1)
                    act.activation(tok[:, kind, :], bank(6), ACT.Identity).then_inc(tok_a_ready, 1)
                for m in range(1, LEVELS):
                    for g in range(2):
                        n = (k * (LEVELS - 1) + m - 1) * 2 + g
                        act.wait_ge(p_ps, n + 1)
                        act.activation(p_sb[:, 4 * g:4 * g + 4, :], bank(g), ACT.Identity).then_inc(p_ready, 1)
                    if m == 2:
                        act.wait_ge(akv_ps, k + 1)
                        act.activation(akv[:, :, :], bank(7), ACT.Identity).then_inc(akv_ready, 1)
                act.wait_ge(ht_ps, k + 1)
                act.activation(ht_sb[:, :, :], bank(6), ACT.Identity).then_inc(ht_ready, 1)
                act.wait_ge(g_ps, k + 1)
                act.activation(g_sb[:, :, :], bank(7), ACT.Identity).then_inc(g_ready, 1)
                for c in range(2):
                    act.wait_ge(o3_ps, 2 * k + c + 1)
                    for q in range(2):
                        r = slice(64 * q, 64 * q + 64)
                        act.activation(o_state[r, :, 128 * hf + 64 * c:128 * hf + 64 * c + 64],
                                       ps_t[r, 512 * (6 + q):512 * (6 + q) + 256], ACT.Identity).then_inc(o3_ready, 1)

            def hi(n, slot, full):
                act.wait_ge(piece_full[slot], full)
                if not isinstance(n, int) or n >= N_SPLIT:
                    act.wait_ge(piece_used, n - N_SPLIT + 1)
                act.activation(w_hi[:, slot % N_SPLIT, :], pieces[:, slot, :], ACT.Identity).then_inc(hi_ready, 1)

            def sigmoid_t(n, t, width):
                act.activation(sig_sb[:, t, 0:width], bank(2 * t, width), ACT.Sigmoid).then_inc(sig_ready[t], 1)

            def turned_t(n, t, width):
                act.wait_ge(actt_ps[t], n + 1)
                act.activation(act_hi[:, t, 0:width], bank(2 * t, width), ACT.Identity).then_inc(act_hi_ready[t], 1)

            def ffn_block(n, nxt, full):
                act.wait_ge(tile0_ps, 2 * n + 1)
                sigmoid_t(n, 0, FB)
                act.wait_ge(piece_used, 3 * n + 1)
                sigmoid_t(n, 1, FB)
                for part in range(3):
                    if nxt is not None:
                        hi(3 * n + 3 + part, nxt + part, full)
                    if part < 2:
                        turned_t(n, part, FB)

            def moe_block(m):
                n, p0 = N_FFB + m, piece_at(m)
                for i in range(MOE_PIECES):
                    hi(p0 + i, i % N_RAW_P, 16 * (FULL0[i % N_RAW_P] + i // N_RAW_P + 1) + 32 * m)
                    if i == 4:
                        sigmoid_t(n, 0, EB)
                    if i == 8:
                        sigmoid_t(n, 1, EB)
                        turned_t(n, 0, EB)
                turned_t(n, 1, EB)

            act.wait_ge(par_in, 16)
            act.activation(c_sig[:, :], par[:, P_C:P_C + KC], ACT.Sigmoid).then_inc(c_sig_ready, 1)
            mixer(0)
            square_x(1)
            for part in range(3):
                hi(part, part, 16)
            act.wait_ge(h_ready, 2 * KC)
            for t in range(NT):
                act.activation(f_hi[:, KC * t:KC * t + KC, :], hT[:, :, P * t:P * t + P], ACT.Identity).then_inc(f_hi_ready, 1)
            with act.Fori(0, N_FFB // 2) as it:
                ffn_block(2 * it, 3, 16 * (it + 1))
                ffn_block(2 * it + 1, 0, 16 * (it + 2))
            ffn_block(N_FFB - 1, None, None)
            act.wait_ge(piece_used, N_FFN_P)
            act.activation(tokm[:, 0, :], ps_t[:, 2048:3072], ACT.Identity).then_inc(f_ytok, 1)
            mixer(1)
            square_x(3)
            act.wait_ge(htok_ps, 1)
            act.activation(tokm[:, :, :], ps_t[:, 2048:4096], ACT.Identity).then_inc(htok_ready, 1)
            act.wait_ge(r_maxed, 2)
            act.activation(r_exp[:, :], r_exp[:, :], ACT.Exp).then_inc(r_exped, 1)
            act.wait_ge(jobs_ready, 1)
            n_pairs = act.value_load(job_i[0:1, N_JOBS:N_JOBS + 1], min_val=NE // 2, max_val=N_JOBS // 2)
            with act.Fori(0, n_pairs) as pair:
                act.wait_ge(gather_ps, 3 * pair + 2)
                act.activation(f_hi[:, 0:KC, :], ps_t[:, 0:1024], ACT.Identity).then_inc(f_hi_ready, 1)
                act.wait_ge(gather_ps, 3 * pair + 3)
                act.activation(f_hi[:, KC:2 * KC, :], ps_t[:, 2048:3072], ACT.Identity).then_inc(f_hi_ready, 1)
                with act.Fori(0, N_EB) as b:
                    moe_block(pair * N_EB + b)
                act.wait_ge(piece_used, piece_at((pair + 1) * N_EB))
                act.activation(y_slot[:, 0, :], ps_t[:, 2048:3072], ACT.Identity).then_inc(y_ready, 1)
            square_x(4)
            for t in range(NT):
                act.wait_ge(out_ps, t + 1)
                act.activation(tokm[:, t, :], ps_t[:, 1024 * t:1024 * (t + 1)], ACT.Identity).then_inc(out_rows, 1)

        @block.vector
        def _(dve):
            chain, zd, ada_n = [0], [0], [0]

            def link(ins):
                chain[0] += 1
                ins.then_inc(dve_chain, 1)
                dve.wait_ge(dve_chain, chain[0])

            def take():
                n = zd[0]
                zd[0] += 1
                dve.wait_ge(zd_ready, n + 1)
                return bank(2 + n % 2, SEQ)

            roots = [0]

            def inverse(a, last):
                if last is not None:
                    link(last)
                roots[0] += 1
                dve.reciprocal(a, a).then_inc(inv_in, 1)

            def ada_steps(count):
                for _ in range(count):
                    n = ada_n[0]
                    ada_n[0] += 1
                    k, t = n // 3 % KC, n % 3
                    acc = ada_acc[:, 1024 * t:1024 * (t + 1)]
                    dve.wait_ge(ada_full[t], 16 * (n // 3 + 1))
                    if n >= 3:
                        dve.wait_ge(ada_free, n + 1)
                    if k == 0:
                        if n >= 24:
                            dve.wait_ge(mod_ps, n // 24)
                        ins = dve.tensor_scalar(acc, ada_ring[:, t, :], c_silu[:, k:k + 1], None, ALU.mult)
                    else:
                        ins = dve.scalar_tensor_tensor(out=acc, in0=ada_ring[:, t, :], scalar=c_silu[:, k:k + 1],
                                                       in1=acc, op0=ALU.mult, op1=ALU.add)
                    ins.then_inc(ada_free, 1)

            def finish_mods(li):
                l, i = divmod(li, 2)
                dve.wait_ge(mod_ps, li + 1)
                o = l * P_W + P_OFF["ada_b"] + 24 * i
                link(dve.tensor_tensor(mods[:, li, :], bank(7, 24), par[:, o:o + 24], ALU.add))
                o = l * P_W + P_OFF["norm_g"] + 8 * i
                dve.scalar_tensor_tensor(out=gain[:, li, :], in0=mods[:, li, 8:16], scalar=1.0,
                                         in1=par[:, o:o + 8], op0=ALU.add, op1=ALU.mult).then_inc(mods_ready, 1)

            def normed(li):
                dve.wait_ge(ssum_ps, li + 1)
                inverse(rstd[:, :], dve.tensor_scalar(rstd[:, :], bank(4, SEQ), 1e-6, None, ALU.add))
                dve.wait_ge(rstd_ready, roots[0])
                link(dve.tensor_tensor(hT, xT, rstd[:, :].unsqueeze(1).broadcast_to([P, KC, SEQ]), ALU.mult))

            def norm_in(li):
                normed(li)
                dve.wait_ge(mods_ready, li + 1)
                for k in range(KC):
                    dve.tensor_scalar(hT[:, k, :], hT[:, k, :], gain[:, li, k:k + 1], mods[:, li, k:k + 1],
                                      ALU.mult, ALU.add).then_inc(h_ready, 1)

            def mix_shift(l):
                for b in range(NB_RKV + 1 + l):
                    n = ZMIX[l] + b
                    rows = VR if b > NB_RKV else slice(0, P)
                    dst = rkv[:, b, :] if b < NB_RKV else (lora_in, vres_in)[b - NB_RKV][rows, :]
                    mu = pcol(l, "mu", b) if b <= NB_RKV else pcol(l, "vmu", 0, 64, 80)
                    z = raw[rows, n % N_RAW, :]
                    dve.wait_ge(za_done, ZA[l, "z"] + b + 1)
                    link(dve.tensor_tensor(tmp[rows, :], z[:, 0:SEQ], z[:, 1:SEQ + 1], ALU.subtract))
                    dve.scalar_tensor_tensor(out=dst, in0=tmp[rows, :], scalar=mu, in1=z[:, 1:SEQ + 1],
                                             op0=ALU.mult, op1=ALU.add).then_inc(mix_done, 1)
                    dve.wait_ge(mix_done, n + 1)
                    if 4 <= b < 8:
                        dve.tensor_scalar(kk_a[:, b - 4, :], dst, pcol(l, "kk_scale", b - 4), None, ALU.mult
                                          ).then_inc(kk_ready, 1)
                    if l == 0 and b < NB_RKV:
                        ada_steps(2)

            def rwkv_inputs(l):
                dve.wait_ge(za_done, ZA[l, "a"] + 4)
                for b in range(4):
                    link(dve.tensor_scalar(tmp[:, :], a_b[:, b, :], 1.0, pcol(l, "ka", b), ALU.subtract, ALU.mult))
                    dve.wait_ge(kk_ready, 4 * (l + 1))
                    link(dve.scalar_tensor_tensor(out=kkv[:, b, :], in0=tmp[:, :], scalar=1.0, in1=kkv[:, b, :],
                                                  op0=ALU.add, op1=ALU.mult))
                for b in range(4):
                    link(dve.scalar_tensor_tensor(out=e2[:, b, :], in0=rr[:, b, :], scalar=pcol(l, "rk", b),
                                                  in1=kkv[:, b, :], op0=ALU.mult, op1=ALU.mult))
                dve.tensor_copy(tmp[:, 0:1], e2[:, 3, 0:1]).then_inc(rkk_ready, 1)
                if l == 0:
                    link(dve.tensor_copy(v_first[:, :], rkv_t[:, 8 * SEQ:12 * SEQ]))
                else:
                    dve.wait_ge(za_done, ZA[l, "vres"] + 4)
                    v1 = rkv_t[:, 8 * SEQ:12 * SEQ]
                    link(dve.tensor_tensor(v_first[:, :], v_first[:, :], v1, ALU.subtract))
                    link(dve.tensor_tensor(v_first[:, :], v_first[:, :], scr[:, 5120:6144], ALU.mult))
                    link(dve.tensor_tensor(v1, v1, v_first[:, :], ALU.add))
                for b in range(4):
                    dve.tensor_scalar(inv4[:, b, :], take(), 1e-24, None, ALU.max).then_inc(zd_free, 1)
                dve.wait_ge(zd_free, zd[0])
                inverse(inv4_t, None)
                for b in range(4):
                    dve.tensor_tensor(bon[:, b, :], take(), vv[:, b, :], ALU.mult).then_inc(zd_free, 1)
                dve.wait_ge(rstd_ready, roots[0])
                link(dve.tensor_tensor(kk_a, kk_a, inv4, ALU.mult))
                dve.wait_ge(decay_ready, 3 * l + 1)
                link(dve.tensor_tensor(a_b, a_b, kk_a, ALU.mult))
                dve.scalar_tensor_tensor(out=kk_a, in0=kk_a, scalar=-1.0, in1=e1, op0=ALU.mult, op1=ALU.mult
                                         ).then_inc(decay_used, 1)
                dve.wait_ge(decay_ready, 3 * l + 2)
                link(dve.tensor_tensor(a_b, a_b, e2, ALU.mult))
                link(dve.tensor_tensor(kkv, kkv, e2, ALU.mult))
                dve.wait_ge(decay_ready, 3 * l + 3)
                link(dve.tensor_copy(chunk_decay[:, :].rearrange("p (b c) -> p b c", b=4), e1[:, :, CH - 1:SEQ:CH]))
                dve.tensor_tensor(rr, rr, e1, ALU.mult).then_inc(tilde_ready, 1)

            def conv(l):
                dve.wait_ge(za_done, ZA[l, "pc"] + 6)
                link(dve.tensor_tensor(ca[:, :, PAD_C:], ca[:, :, PAD_C:], cb, ALU.mult))
                for b in range(2):
                    link(dve.tensor_scalar(cy[:, b, :], ca[:, b, 0:SEQ], pcol(l, "conv_w", b * CONV_K),
                                           pcol(l, "conv_b", b), ALU.mult, ALU.add))
                for j in range(1, CONV_K):
                    for b in range(2):
                        ins = dve.scalar_tensor_tensor(out=cy[:, b, :], in0=ca[:, b, j:j + SEQ],
                                                       scalar=pcol(l, "conv_w", b * CONV_K + j), in1=cy[:, b, :],
                                                       op0=ALU.mult, op1=ALU.add)
                        if j < CONV_K - 1:
                            link(ins)
                        else:
                            ins.then_inc(conv_u, 1)

            def conv_norm(l):
                dve.wait_ge(conv_mean, l + 1)
                dve.wait_ge(conv_u, 2 * (l + 1))
                for b in range(2):
                    dve.tensor_tensor(cy[:, b, :], cy[:, b, :], bank(4, SEQ), ALU.subtract).then_inc(conv_dev, 1)
                dve.wait_ge(conv_var, l + 1)
                inverse(rstd[:, :], dve.tensor_scalar(rstd[:, :], bank(5, SEQ), 1e-5, None, ALU.add))
                dve.wait_ge(rstd_ready, roots[0])
                dve.wait_ge(conv_dev, 2 * (l + 1))
                for b in range(2):
                    link(dve.tensor_tensor(cy[:, b, :], cy[:, b, :], rstd[:, :], ALU.mult))
                    dve.tensor_scalar(cy[:, b, :], cy[:, b, :], pcol(l, "ln_g", b), pcol(l, "ln_b", b),
                                      ALU.mult, ALU.add).then_inc(conv_un, 1)
                dve.wait_ge(conv_sg, l + 1)
                dve.wait_ge(conv_un, 2 * (l + 1))
                dve.tensor_tensor(cy, cy, cb, ALU.mult).then_inc(conv_y, 1)

            def wkv_half(l, hf):
                k = 2 * l + hf
                tri_s, tri_i = (cc(c).unsqueeze(1).broadcast_to([P, 4, P]) for c in (C_TRI_S, C_TRI_I))
                low0, lvl0, eye = (cc(c).unsqueeze(1).broadcast_to([P, 4, P]) for c in (C_LOW0, C_LVL, C_ID))

                def heads(b):
                    return bank(b).rearrange("p (n w) -> p n w", w=P)

                for g in range(2):
                    h4 = slice(4 * g, 4 * g + 4)
                    dve.wait_ge(amat_ps, 2 * k + g + 1)
                    link(dve.tensor_tensor(ltm[:, h4, :], heads(2 + g), tri_s, ALU.mult))
                    dve.tensor_tensor(ak_t[:, h4, :], heads(4 + g), tri_s, ALU.mult).then_inc(amat_ready, 1)
                    link(dve.tensor_tensor(tinv[:, h4, :], heads(g), low0, ALU.mult))
                    link(dve.tensor_tensor(tinv_t[:, h4, :], ltm[:, h4, :], lvl0, ALU.mult))
                    dve.tensor_tensor(tinv[:, h4, :], tinv[:, h4, :], eye, ALU.add).then_inc(t_ready, 1)
                    dve.tensor_tensor(tinv_t[:, h4, :], tinv_t[:, h4, :], eye, ALU.add).then_inc(t_ready, 1)
                base = k * T_INC
                for i, kind in enumerate((1, 3)):
                    dve.wait_ge(tok_ps, 4 * k + 2 * i + 2)
                    dve.tensor_copy(tok[:, kind, :], bank(7)).then_inc(tok_d_ready, 1)
                for m in range(1, LEVELS):
                    for g in range(2):
                        h4 = slice(4 * g, 4 * g + 4)
                        dve.wait_ge(dt_ps, (k * (LEVELS - 1) + m - 1) * 2 + g + 1)
                        dve.wait_ge(t_ready, base + 4 * m)
                        if m < LEVELS - 1:
                            dve.tensor_tensor(tinv[:, h4, :], tinv[:, h4, :], heads(2 + g), ALU.add).then_inc(t_ready, 1)
                        else:
                            dve.sem_inc(t_ready, 1)
                        dve.tensor_tensor(tinv_t[:, h4, :], tinv_t[:, h4, :], heads(4 + g), ALU.add).then_inc(t_ready, 1)
                for g in range(2):
                    h4 = slice(4 * g, 4 * g + 4)
                    dve.wait_ge(rb_ps, 2 * k + g + 1)
                    dve.tensor_tensor(lvl_l[:, h4, :], heads(g), tri_i, ALU.mult).then_inc(rb_ready, 1)
                    dve.tensor_tensor(ak_t[:, h4, :], heads(2 + g), tri_i, ALU.mult).then_inc(rb_ready, 1)
                for c in range(2):
                    n = 2 * k + c
                    r = slice(64 * c, 64 * c + 64)
                    dve.wait_ge(u_ps, n + 1)
                    dve.wait_ge(g_ready, k + 1)
                    for g in range(2):
                        dve.tensor_tensor(u_sb[r, 4 * g:4 * g + 4, :],
                                          ps_t[r, 512 * (4 + g):512 * (4 + g) + 256].rearrange("p (n w) -> p n w", w=64),
                                          g_sb[r, 4 * g:4 * g + 4, :], ALU.add).then_inc(u_ready, 1)
                    dve.wait_ge(s_ps, n + 1)
                    link(dve.tensor_tensor(state_t[:, :], state_t[:, :], bank(0, 256), ALU.add))
                    wc = chunk_decay[:, :].rearrange("p (b c) -> p b c", b=4)[:, :, 2 * hf + c:2 * hf + c + 1]
                    dve.tensor_tensor(state, state, wc.broadcast_to([P, 4, 64]), ALU.mult).then_inc(s_ready, 1)
                dve.wait_ge(o_ps, k + 1)
                dve.wait_ge(o3_ready, 4 * (k + 1))
                dve.tensor_tensor(o_all[:, :, P * hf:P * hf + P], bank(1).rearrange("p (n w) -> p n w", w=P),
                                  o_state[:, :, P * hf:P * hf + P], ALU.add).then_inc(o_ready, 1)

            def rwkv_out(l):
                dve.wait_ge(o_ready, 2 * (l + 1))
                for b in range(4):
                    dve.scalar_tensor_tensor(out=o_all[:, b, :], in0=take(), scalar=-1.0 / 64, in1=o_all[:, b, :],
                                             op0=ALU.mult, op1=ALU.add).then_inc(zd_free, 1)
                    dve.wait_ge(zd_free, zd[0])
                    dve.sem_inc(o_dev, 1)
                for b in range(4):
                    dve.tensor_scalar(inv4[:, b, :], take(), 1.0 / 64, 64e-5, ALU.mult, ALU.add).then_inc(zd_free, 1)
                dve.wait_ge(zd_free, zd[0])
                inverse(inv4_t, None)
                dve.wait_ge(rstd_ready, roots[0])
                link(dve.tensor_tensor(o_all, o_all, inv4, ALU.mult))
                for b in range(4):
                    link(dve.tensor_scalar(o_all[:, b, :], o_all[:, b, :], pcol(l, "lnx_g", b), pcol(l, "lnx_b", b),
                                           ALU.mult, ALU.add))
                link(dve.tensor_tensor(o_all, o_all, bon, ALU.add))
                dve.tensor_tensor(o_all, o_all, gg, ALU.mult).then_inc(o_final, 1)

            def mixer(l):
                norm_in(2 * l)
                mix_shift(l)
                if l == 0:
                    finish_mods(1)
                rwkv_inputs(l)
                conv(l)
                for b in range(KC):
                    src = take()
                    dve.wait_ge(za_done, ZA[l, "gate_p"] + b + 1)
                    dve.tensor_tensor(merged[:, b, :], src, sg[:, b % 2, :], ALU.mult).then_inc(zd_free, 1)
                    if l == 0:
                        ada_steps(3)
                if l == 0:
                    finish_mods(2)
                conv_norm(l)
                for b in range(KC):
                    src = take()
                    dve.wait_ge(za_done, ZA[l, "gate_c"] + b + 1)
                    dve.tensor_tensor(tmp[:, :], src, sg[:, b % 2, :], ALU.mult).then_inc(zd_free, 1)
                    dve.wait_ge(zd_free, zd[0])
                    link(dve.tensor_tensor(merged[:, b, :], merged[:, b, :], tmp[:, :], ALU.add))
                    if l == 0:
                        ada_steps(3)
                if l == 0:
                    finish_mods(3)
                dve.memset(state_t[:, :], 0.0).then_inc(s_ready, 1)
                dve.wait_ge(s_ready, 5 * l + 1)
                for hf in range(NT):
                    wkv_half(l, hf)
                rwkv_out(l)
                for b in range(KC):
                    if b >= 1:
                        dve.wait_ge(merged_ready, KC * l + b)
                    dve.tensor_tensor(tmp[:, :], take(), gate_r[:, b, :], ALU.mult).then_inc(zd_free, 1)
                    dve.wait_ge(zd_free, zd[0])
                    dve.tensor_tensor(merged[:, b, :], merged[:, b, :], tmp[:, :], ALU.add).then_inc(merged_ready, 1)
                for b in range(KC):
                    dve.scalar_tensor_tensor(out=xT[:, b, :], in0=take(), scalar=mods[:, 2 * l, 16 + b:17 + b],
                                             in1=xT[:, b, :], op0=ALU.mult, op1=ALU.add).then_inc(zd_free, 1)
                    dve.wait_ge(zd_free, zd[0])
                    dve.sem_inc(x_ready, 1)

            def lo(n, slot):
                dve.wait_ge(hi_ready, n + 1)
                dve.tensor_tensor(w_lo[:, slot % N_SPLIT, :], pieces[:, slot, :],
                                  w_hi[:, slot % N_SPLIT, :].bitcast(f32), ALU.subtract).then_inc(split_ready, 1)

            def silu_t(n, t, width):
                dve.wait_ge(sig_ready[t], n + 1)
                dve.tensor_tensor(sig_sb[:, t, 0:width], sig_sb[:, t, 0:width], bank(2 * t, width), ALU.mult
                                  ).then_inc(silu_ready[t], 1)

            def act_of(n, t, width):
                dve.wait_ge(silu_ready[t], n + 1)
                dve.tensor_tensor(act_sb[:, t, 0:width], sig_sb[:, t, 0:width], bank(2 * t + 1, width), ALU.mult
                                  ).then_inc(act_ready[t], 1)

            def turned_lo(n, t, width):
                dve.wait_ge(act_hi_ready[t], n + 1)
                dve.tensor_tensor(act_lo[:, t, 0:width], bank(2 * t, width), act_hi[:, t, 0:width].bitcast(f32),
                                  ALU.subtract).then_inc(act_lo_ready[t], 1)

            def ffn_block(n, nxt):
                silu_t(n, 0, FB)
                silu_t(n, 1, FB)
                dve.wait_ge(tile0_ps, 2 * n + 2)
                act_of(n, 0, FB)
                if nxt is not None:
                    lo(3 * n + 3, nxt)
                dve.wait_ge(piece_used, 3 * n + 2)
                act_of(n, 1, FB)
                turned_lo(n, 0, FB)
                if nxt is not None:
                    lo(3 * n + 4, nxt + 1)
                turned_lo(n, 1, FB)
                if nxt is not None:
                    lo(3 * n + 5, nxt + 2)

            def moe_block(m):
                n, p0 = N_FFB + m, piece_at(m)
                for i in range(MOE_PIECES):
                    lo(p0 + i, i % N_RAW_P)
                    if i == 5:
                        silu_t(n, 0, EB)
                        dve.wait_ge(piece_used, p0 + 4)
                        act_of(n, 0, EB)
                    if i == 8:
                        turned_lo(n, 0, EB)
                        silu_t(n, 1, EB)
                    if i == 9:
                        dve.wait_ge(piece_used, p0 + 8)
                        act_of(n, 1, EB)
                turned_lo(n, 1, EB)

            dve.memset(raw_t[:, :], 0.0)
            dve.memset(pu[:, :], 0.0)
            dve.memset(pa[:, :], 0.0)
            dve.memset(pbuf[:, :], 0.0)
            dve.memset(ca_t[:, :], 0.0).then_inc(pads_ready, 1)
            dve.sem_inc(ada_free, 3)
            ada_n_first = 0
            dve.wait_ge(c_sig_ready, 1)
            link(dve.tensor_tensor(c_silu[:, :], c_sig[:, :], par[:, P_C:P_C + KC], ALU.mult))
            for t in range(NT):
                dve.wait_ge(xt_ps, t + 1)
                src = ps_t[:, 1024 * t:1024 * (t + 1)].rearrange("p (k n) -> p k n", n=P)
                dve.tensor_copy(xT[:, :, P * t:P * t + P], src).then_inc(x_ready, KC // NT)
            ada_steps(3 * KC)
            finish_mods(0)
            mixer(0)
            norm_in(1)
            for part in range(3):
                lo(part, part)
            for t in range(NT):
                dve.wait_ge(f_hi_ready, t + 1)
                dve.tensor_tensor(f_lo[:, KC * t:KC * t + KC, :], hT[:, :, P * t:P * t + P],
                                  f_hi[:, KC * t:KC * t + KC, :].bitcast(f32), ALU.subtract).then_inc(f_lo_ready, 1)
            with dve.Fori(0, N_FFB // 2) as it:
                ffn_block(2 * it, 3)
                ffn_block(2 * it + 1, 0)
            ffn_block(N_FFB - 1, None)
            dve.wait_ge(piece_used, N_FFN_P)
            dve.tensor_copy(tokm[:, 1, :], ps_t[:, 3072:4096]).then_inc(f_ytok, 1)
            for k in range(KC):
                dve.wait_ge(f_tr, 2 * (k // 2) + 2)
                dve.scalar_tensor_tensor(out=xT[:, k, :], in0=ps_t[:, SEQ * k:SEQ * (k + 1)],
                                         scalar=mods[:, 1, 16 + k:17 + k], in1=xT[:, k, :],
                                         op0=ALU.mult, op1=ALU.add).then_inc(x_ready, 1)
            mixer(1)
            norm_in(3)

            lg3, sel3, gate3, rank3 = (t[:, :].rearrange("p (t e) -> p t e", e=NE) for t in (lg, r_sel, r_gate, r_rank))
            cmp3, cmq3 = (t[:, :].rearrange("p (t e f) -> p t e f", e=NE, f=NE) for t in (cmp_t, cmp2_t))
            low8 = cst[:, C_LOW8:C_LOW8 + NE * NE].rearrange("p (e f) -> p e f", f=NE)
            dve.wait_ge(logits_ps, 1)
            link(dve.tensor_copy(lg[:, :], bank(0, NT * NE)))
            link(dve.tensor_reduce(r_max[:, :], lg3, AX.X, ALU.max))
            for t in range(NT):
                dve.tensor_scalar(r_exp[:, NE * t:NE * t + NE], lg3[:, t, :], r_max[:, t:t + 1], None, ALU.subtract
                                  ).then_inc(r_maxed, 1)
            for t in range(NT):
                other = lg3[:, t, :].unsqueeze(1).broadcast_to([P, NE, NE])
                own = lg3[:, t, :].unsqueeze(2).broadcast_to([P, NE, NE])
                link(dve.tensor_tensor(cmp3[:, t], other, own, ALU.is_gt))
                link(dve.tensor_tensor(cmq3[:, t], other, own, ALU.is_equal))
                link(dve.tensor_tensor(cmq3[:, t], cmq3[:, t], low8, ALU.mult))
                link(dve.tensor_tensor(cmp3[:, t], cmp3[:, t], cmq3[:, t], ALU.add))
                link(dve.tensor_reduce(r_cnt[:, NE * t:NE * t + NE], cmp3[:, t], AX.X, ALU.add))
            dve.tensor_scalar(r_sel[:, :], r_cnt[:, :], 2.0, None, ALU.is_lt).then_inc(r_sel_ready, 1)
            dve.wait_ge(r_sel_ready, 1)
            dve.wait_ge(r_exped, 1)
            link(dve.tensor_tensor(r_gate[:, :], r_exp[:, :], r_sel[:, :], ALU.mult))
            link(dve.tensor_reduce(r_den[:, :], gate3, AX.X, ALU.add))
            link(dve.reciprocal(r_den[:, :], r_den[:, :]))
            link(dve.tensor_tensor(gate3, gate3, r_den[:, :].unsqueeze(2).broadcast_to([P, NT, NE]), ALU.mult))

            far = 1024.0
            dve.wait_ge(rank_ps, 1)
            link(dve.scalar_tensor_tensor(out=r_rank[:, :], in0=bank(1, NT * NE), scalar=far, in1=r_sel[:, :],
                                          op0=ALU.add, op1=ALU.mult))
            link(dve.tensor_scalar(r_rank[:, :], r_rank[:, :], far, None, ALU.subtract))
            link(dve.tensor_scalar(over[:, :], ps_t[:, 512 + NT * NE:512 + (NT + 1) * NE], float(P), None, ALU.is_gt))
            link(dve.tensor_tensor(cmp3[:, 0], low8, over[:, :].unsqueeze(1).broadcast_to([P, NE, NE]), ALU.mult))
            link(dve.tensor_reduce(prev[:, :], cmp3[:, 0], AX.X, ALU.add))
            jr = job_rank[:, :].rearrange("p (t j) -> p t j", j=N_JOBS)
            jg = job_gate[:, :].rearrange("p (t j) -> p t j", j=N_JOBS)
            link(dve.memset(job_rank[:, :], -far))
            link(dve.memset(job_gate[:, :], 0.0))
            link(dve.memset(job_f[:, :], 0.0))
            link(dve.tensor_copy(jr[:, :, 0:NE], rank3))
            link(dve.tensor_copy(jg[:, :, 0:NE], gate3))
            link(dve.tensor_copy(job_f[:, 0:NE], cc(C_EID, NE)))
            for q in range(3):
                oh = onehot[:, NE * q:NE * q + NE]
                w8 = cmp_t[:, NE * q:NE * q + NE]
                link(dve.tensor_scalar(oh, prev[:, :], float(q), None, ALU.is_equal))
                link(dve.tensor_tensor(oh, oh, over[:, :], ALU.mult))
                for t in range(NT):
                    link(dve.tensor_tensor(w8, oh, rank3[:, t, :], ALU.mult))
                    link(dve.tensor_reduce(jr[:, t, NE + q:NE + q + 1], w8, AX.X, ALU.add))
                    link(dve.tensor_tensor(w8, oh, gate3[:, t, :], ALU.mult))
                    link(dve.tensor_reduce(jg[:, t, NE + q:NE + q + 1], w8, AX.X, ALU.add))
                link(dve.tensor_tensor(w8, oh, cc(C_EID, NE), ALU.mult))
                link(dve.tensor_reduce(job_f[:, NE + q:NE + q + 1], w8, AX.X, ALU.add))
            link(dve.tensor_scalar(jr[:, :, NE:NE + 3], jr[:, :, NE:NE + 3], float(P), None, ALU.subtract))
            n_over = job_f[:, N_JOBS + 1:N_JOBS + 2]
            link(dve.tensor_reduce(n_over, over[:, :], AX.X, ALU.add))
            link(dve.tensor_scalar(job_f[:, N_JOBS:N_JOBS + 1], n_over, 0.5, float(NE // 2), ALU.is_gt, ALU.add))
            link(dve.tensor_scalar(job_f[:, N_JOBS + 2:N_JOBS + 3], n_over, 2.5, None, ALU.is_gt))
            link(dve.tensor_tensor(job_f[:, N_JOBS:N_JOBS + 1], job_f[:, N_JOBS:N_JOBS + 1],
                                   job_f[:, N_JOBS + 2:N_JOBS + 3], ALU.add))
            dve.memset(merged_t[:, :], 0.0).then_inc(comb_done, 1)
            dve.wait_ge(comb_done, 1)
            dve.tensor_copy(job_i[0:1, :], job_f[0:1, :]).then_inc(jobs_ready, 1)
            dve.wait_ge(jobs_ready, 1)
            n_pairs = dve.value_load(job_i[0:1, N_JOBS:N_JOBS + 1], min_val=NE // 2, max_val=N_JOBS // 2)

            iota = cc(C_IOTA)
            with dve.Fori(0, n_pairs) as pair:
                for s in range(2):
                    for t in range(NT):
                        place = job_rank[:, ds(N_JOBS * t + s + 2 * pair, 1)]
                        weight = job_gate[:, ds(N_JOBS * t + s + 2 * pair, 1)]
                        dve.tensor_scalar(sel[:, 2 * s + t, :], iota, place, None, ALU.is_equal).then_inc(sel_ready, 1)
                        dve.tensor_scalar(sel_g[:, 2 * s + t, :], iota, place, weight, ALU.is_equal, ALU.mult
                                          ).then_inc(sel_ready, 1)
                dve.wait_ge(gather_ps, 3 * pair + 1)
                dve.tensor_copy(sel_t_t[:, :], bank(6)).then_inc(gather_d_ready, 1)
                for s in range(2):
                    dve.wait_ge(f_hi_ready, 2 * pair + 3 + s)
                    src = ps_t[:, 2048 * s:2048 * s + 1024].rearrange("p (k n) -> p k n", n=P)
                    dve.tensor_tensor(f_lo[:, KC * s:KC * s + KC, :], src, f_hi[:, KC * s:KC * s + KC, :].bitcast(f32),
                                      ALU.subtract).then_inc(f_lo_ready, 1)
                with dve.Fori(0, N_EB) as b:
                    moe_block(pair * N_EB + b)
                dve.wait_ge(piece_used, piece_at((pair + 1) * N_EB))
                dve.tensor_copy(y_slot[:, 1, :], ps_t[:, 3072:4096]).then_inc(y_ready, 1)
                dve.wait_ge(comb_ps, pair + 1)
                dve.tensor_tensor(merged_t[:, :], merged_t[:, :], ps_t[:, 0:2048], ALU.add).then_inc(comb_done, 1)
                dve.wait_ge(comb_done, pair + 2)
            for k in range(KC):
                dve.scalar_tensor_tensor(out=xT[:, k, :], in0=yT[:, k, :], scalar=mods[:, 3, 16 + k:17 + k],
                                         in1=xT[:, k, :], op0=ALU.mult, op1=ALU.add).then_inc(x_ready, 1)
            dve.wait_ge(x_ready, 5 * KC)
            normed(4)
            for k in range(KC):
                dve.tensor_scalar(hT[:, k, :], hT[:, k, :], par[:, P_FG + k:P_FG + k + 1], None, ALU.mult
                                  ).then_inc(h_ready, 1)

        @block.tensor
        def _(pe):
            za, zd, fill = [0], [0], [0]

            def mm(dst, lhs, rhs, start=True, stop=True, **kw):
                return pe.matmul(dst, lhs, rhs, start=start, stop=stop, **kw)

            def give_za(parts, rows=slice(0, P)):
                n = za[0]
                za[0] += 1
                if n >= 2:
                    pe.wait_ge(za_done, n - 1)
                for i, (lhs, rhs) in enumerate(parts):
                    last = mm(bank(n % 2, SEQ)[rows, :], lhs, rhs, i == 0, i == len(parts) - 1)
                last.then_inc(za_ready, 1)

            def give_zd(parts):
                n = zd[0]
                zd[0] += 1
                if n >= 2:
                    pe.wait_ge(zd_free, n - 1)
                for i, (lhs, rhs) in enumerate(parts):
                    last = mm(bank(2 + n % 2, SEQ), lhs, rhs, i == 0, i == len(parts) - 1)
                last.then_inc(zd_ready, 1)

            def landed(n):
                pe.wait_ge(ring_full[FILLS[n][0]], FULL[n])

            def mean_square(li):
                pe.wait_ge(xsq_ready, li + 1)
                for k in range(KC):
                    last = mm(bank(4, SEQ), ones, hT[:, k, :], k == 0, k == KC - 1)
                last.then_inc(ssum_ps, 1)

            def mod_sums(li):
                pe.wait_ge(ada_free, 3 + 24 * (li + 1))
                for c in range(24):
                    last = mm(bank(7, 24)[:, c:c + 1], ada_acc[:, P * c:P * c + P], cc(C_ONES, 1))
                last.then_inc(mod_ps, 1)

            def z_parts(w, c):
                return [(w[:, k, c:c + P], hT[:, k, :]) for k in range(KC)]

            def z_blocks(l, fills, give=None):
                for i, n_blocks in fills:
                    n = MIX_FILLS * l + i
                    landed(n)
                    w = fill_at(n, P * n_blocks, 0, KC)
                    for b in range(n_blocks):
                        give_za(z_parts(w, P * b))
                        if give is not None:
                            give()

            def mixer(l):
                mean_square(2 * l)
                pe.wait_ge(h_ready, KC * (2 * l + 1))
                f0 = MIX_FILLS * l
                z_blocks(l, [(0, 4), (1, 4), (2, 4), (3, 1)])
                if l > 0:
                    wv = fill_at(f0 + 3, 16, KC * P, KC)
                    give_za([(wv[:, k, :], hT[:, k, :]) for k in range(KC)], rows=VR)
                z_blocks(l, [(4, 4), (5, 2)])
                if l == 0:
                    mod_sums(1)
                pe.wait_ge(small_in, SMALL[l])
                pe.wait_ge(lora_ready, 2 * (l + 1))
                for t in range(NT):
                    tk = slice(P * t, P * t + P)
                    mm(bank(5 + t), cc(C_ONES, P, 0, 1), w0_sb[0:1, :], True, False)
                    last = mm(bank(5 + t), lora_in[0:32, tk], lora_w[0:32, :], False, True)
                last.then_inc(sigt_ps, 1)
                for b in range(4):
                    c = slice(P * b, P * b + P)
                    give_za([(lora_w[32:64, c], lora_in[32:64, :])])
                for b in range(4):
                    c = slice(P * b, P * b + P)
                    give_za([(lora_w[64:P, c], lora_in[64:P, :])])
                for b in range(4 * l):
                    c = slice(P * b, P * b + P)
                    pe.wait_ge(mix_done, ZMIX[l] + NB_RKV + 2)
                    give_za([(w0_sb[VR, c], vres_in[VR, :])])
                pe.wait_ge(kksq_ready, l + 1)
                for b in range(4):
                    give_zd([(bones, e1[:, b, :])])
                pe.wait_ge(sigt_ready, l + 1)
                for first, tri in ((4, C_TRI_I), (6, C_TRI_S)):
                    for b in range(4):
                        for t in range(NT):
                            o = 512 * first + SEQ * b + P * t
                            last = mm(ps_t[:, o:o + P], sig_tok[:, t, P * b:P * b + P], cc(tri))
                last.then_inc(cum_ps, 1)
                pe.wait_ge(rkk_ready, l + 1)
                for b in range(4):
                    give_zd([(bones, e2[:, b, :])])
                z_blocks(l, [(6, 4), (7, 4)])
                pe.wait_ge(pooled, 4 * (l + 1))
                pe.wait_ge(decay_ready, 3 * (l + 1))
                for b in range(2):
                    for q in range(2):
                        r = slice(64 * q, 64 * q + 64)
                        o = 512 * (4 + q) + SEQ * b
                        last = mm(ps_t[r, o:o + SEQ], pool_wsb[r, 64 * b:64 * b + 64], pl[r, b, :])
                last.then_inc(pool_ps, 1)
                landed(f0 + 9)
                wp, wc = fill_at(f0 + 9, D, 0, 2), fill_at(f0 + 9, D, 2048, 2)
                at = [0]

                def y_pool():
                    b = at[0]
                    at[0] += 1
                    pe.wait_ge(pool_y, 4 * (l + 1))
                    give_zd([(wp[:, k, P * b:P * b + P], pa3[:, k, PAD_P:]) for k in range(2)])

                z_blocks(l, [(8, 4), (10, 4)], y_pool)
                if l == 0:
                    mod_sums(2)
                pe.wait_ge(conv_u, 2 * (l + 1))
                for b in range(2):
                    last = mm(bank(4, SEQ), mean256, cy[:, b, :], b == 0, b == 1)
                last.then_inc(conv_mean, 1)
                pe.wait_ge(conv_sq, l + 1)
                for b in range(2):
                    last = mm(bank(5, SEQ), mean256, cb[:, b, :], b == 0, b == 1)
                last.then_inc(conv_var, 1)
                at[0] = 0

                def y_conv():
                    b = at[0]
                    at[0] += 1
                    pe.wait_ge(conv_y, l + 1)
                    give_zd([(wc[:, k, P * b:P * b + P], cy[:, k, :]) for k in range(2)])

                z_blocks(l, [(11, 4), (12, 4)], y_conv)
                if l == 0:
                    mod_sums(3)
                pe.wait_ge(tilde_ready, l + 1)
                for hf in range(NT):
                    wkv_half(l, hf)
                pe.wait_ge(o_ready, 2 * (l + 1))
                for b in range(4):
                    give_zd([(bones, o_all[:, b, :])])
                for b in range(4):
                    pe.wait_ge(o_sq, 4 * l + b + 1)
                    give_zd([(bones, e1[:, b, :])])
                pe.wait_ge(o_final, l + 1)
                landed(f0 + 13)
                w = fill_at(f0 + 13, D)
                for b in range(KC):
                    give_zd([(w[:, k, P * b:P * b + P], o_all[:, k, :]) for k in range(4)])
                landed(f0 + 14)
                landed(f0 + 15)
                pe.wait_ge(merged_ready, KC * (l + 1))
                w0_, w1_ = fill_at(f0 + 14, D), fill_at(f0 + 15, D)
                for b in range(KC):
                    give_zd([((w0_, w1_)[k // 4][:, k % 4, P * b:P * b + P], merged[:, k, :]) for k in range(KC)])

            def wkv_half(l, hf):
                k = 2 * l + hf
                tk = slice(P * hf, P * hf + P)
                base = k * T_INC
                at_, bt_, kt_, rt_, vt_ = kk_a, a_b, kkv, rr, vv
                pe.wait_ge(za_done, ZA[l, "end"])
                pe.wait_ge(zd_free, ZD[l, "mean"])
                pe.wait_ge(mods_ready, 4)
                if hf == 1:
                    pe.wait_ge(o_ready, k)
                    pe.wait_ge(s_ready, 5 * l + 3)
                for g in range(2):
                    r = slice(64 * g, 64 * g + 64)
                    for b in range(4):
                        o = P * b
                        mm(ps_t[:, 512 * g + o:512 * g + o + P], at_[r, b, tk], bt_[r, b, tk])
                        mm(ps_t[:, 512 * (2 + g) + o:512 * (2 + g) + o + P], bt_[r, b, tk], at_[r, b, tk])
                        last = mm(ps_t[:, 512 * (4 + g) + o:512 * (4 + g) + o + P], kt_[r, b, tk], at_[r, b, tk])
                    last.then_inc(amat_ps, 1)
                for i, src in enumerate((at_, vt_, bt_, kt_)):
                    if i >= 2:
                        pe.wait_ge((tok_a_ready, tok_d_ready)[i - 2], 2 * k + 1)
                    for b in range(4):
                        last = pe.transpose(ps_t[:, 512 * (6 + i % 2) + P * b:512 * (6 + i % 2) + P * b + P],
                                            src[:, b, tk], ident)
                    last.then_inc(tok_ps, 1)
                for m in range(1, LEVELS):
                    n = (k * (LEVELS - 1) + m - 1) * 2
                    for g in range(2):
                        pe.wait_ge(lvl_ready, n + g + 1)
                        pe.wait_ge(t_ready, base + 4 * (m - 1) + 2 * (g + 1))
                        for b in range(4):
                            h = 4 * g + b
                            last = mm(ps_t[:, 512 * g + P * b:512 * g + P * b + P], lvl_l[:, h, :], tinv[:, h, :])
                        last.then_inc(p_ps, 1)
                    if m == 1:
                        pe.wait_ge(amat_ready, 2 * k + 2)
                    for g in range(2):
                        pe.wait_ge(p_ready, n + g + 1)
                        for b in range(4):
                            h = 4 * g + b
                            if m < LEVELS - 1:
                                mm(ps_t[:, 512 * (2 + g) + P * b:512 * (2 + g) + P * b + P], tinv_t[:, h, :], p_sb[:, h, :])
                            last = mm(ps_t[:, 512 * (4 + g) + P * b:512 * (4 + g) + P * b + P], p_sb[:, h, :], tinv_t[:, h, :])
                        last.then_inc(dt_ps, 1)
                    if m == 2:
                        pe.wait_ge(tok_d_ready, 2 * (k + 1))
                        for h in range(8):
                            c = head_col(h)
                            last = mm(ps_t[:, 3584 + 64 * h:3584 + 64 * h + 64], ak_t[:, h, :], tok[:, 1, c:c + 64])
                        last.then_inc(akv_ps, 1)
                pe.wait_ge(t_ready, base + T_INC)
                pe.wait_ge(tok_a_ready, 2 * (k + 1))
                for h in range(8):
                    g, b, c = h // 4, h % 4, head_col(h)
                    last = mm(ps_t[64 * g:64 * g + 64, 3072 + P * b:3072 + P * b + P], tok[:, 0, c:c + 64], tinv_t[:, h, :])
                last.then_inc(ht_ps, 1)
                pe.wait_ge(akv_ready, k + 1)
                for h in range(8):
                    last = mm(ps_t[:, 3584 + 64 * h:3584 + 64 * h + 64], tinv_t[:, h, :], akv[:, h, :])
                last.then_inc(g_ps, 1)
                for g in range(2):
                    r = slice(64 * g, 64 * g + 64)
                    for b in range(4):
                        o = P * b
                        mm(ps_t[:, 512 * g + o:512 * g + o + P], bt_[r, b, tk], rt_[r, b, tk])
                        last = mm(ps_t[:, 512 * (2 + g) + o:512 * (2 + g) + o + P], kt_[r, b, tk], rt_[r, b, tk])
                    last.then_inc(rb_ps, 1)
                for c in range(2):
                    n = 2 * k + c
                    q = slice(64 * c, 64 * c + 64)
                    pe.wait_ge(ht_ready, k + 1)
                    pe.wait_ge(g_ready, k + 1)
                    pe.wait_ge(s_ready, 5 * l + 1 + 2 * hf + c)
                    if c == 1:
                        pe.wait_ge(o3_ready, 2 * n)
                    for g in range(2):
                        r = slice(64 * g, 64 * g + 64)
                        for b in range(4):
                            last = mm(ps_t[q, 512 * (4 + g) + 64 * b:512 * (4 + g) + 64 * b + 64], ht_sb[r, b, q], state[r, b, :])
                    last.then_inc(u_ps, 1)
                    t0 = P * hf + 64 * c
                    for g in range(2):
                        r = slice(64 * g, 64 * g + 64)
                        for b in range(4):
                            last = mm(ps_t[r, 512 * (6 + g) + 64 * b:512 * (6 + g) + 64 * b + 64], state[r, b, :], rt_[r, b, t0:t0 + 64])
                    last.then_inc(o3_ps, 1)
                    pe.wait_ge(u_ready, 2 * (n + 1))
                    pe.wait_ge(rb_ready, 4 * (k + 1))
                    for h in range(8):
                        g, b, hc = h // 4, h % 4, head_col(h)
                        dst = ps_t[64 * g:64 * g + 64, 64 * b:64 * b + 64]
                        mm(dst, tok[q, 2, hc:hc + 64], u_sb[q, h, :], True, False)
                        last = mm(dst, tok[q, 3, hc:hc + 64], tok[q, 1, hc:hc + 64], False, True)
                    last.then_inc(s_ps, 1)
                for h in range(8):
                    g, b, hc = h // 4, h % 4, head_col(h)
                    dst = ps_t[64 * g:64 * g + 64, 512 + P * b:512 + P * b + P]
                    mm(dst, u_sb[:, h, :], lvl_l[:, h, :], True, False)
                    last = mm(dst, tok[:, 1, hc:hc + 64], ak_t[:, h, :], False, True)
                last.then_inc(o_ps, 1)

            def mm3(dst, lhs, rhs, first, last):
                (lh, ll), (rh, rl) = lhs, rhs
                pe.matmul(dst, lh, rh, start=first, stop=False, skip_group_check=True)
                pe.matmul(dst, lh, rl, start=False, stop=False, skip_group_check=True)
                return pe.matmul(dst, ll, rh, start=False, stop=last, skip_group_check=True)

            def tile_in(t, k):
                return f_hi[:, KC * t + k, :], f_lo[:, KC * t + k, :]

            def split_piece(slot, k, w, c=0, n=None):
                a = w * k + c
                return tuple(x[:, slot % N_SPLIT, a:a + (n or w)] for x in (w_hi, w_lo))

            def turn(n, t, width):
                pe.wait_ge(act_ready[t], n + 1)
                for j in range(width // P):
                    last = pe.transpose(ps_t[:, 1024 * t + P * j:1024 * t + P * j + P], act_sb[:, t, P * j:P * j + P], ident)
                last.then_inc(actt_ps[t], 1)

            def down_rows(t, slot, rows, j0, start=False):
                for j in rows:
                    lhs = tuple(x[:, t, P * (j0 + j):P * (j0 + j) + P] for x in (act_hi, act_lo))
                    for c in range(2):
                        last = mm3(bank(4 + 2 * t + c), lhs, split_piece(slot, j, D, 512 * c, 512), start and j == 0, True)
                return last

            def ffn_block(n):
                first = isinstance(n, int) and n == 0
                for part in range(2):
                    pe.wait_ge(split_ready, 3 * n + part + 1)
                    for t in range(NT):
                        if part == 0 and not first:
                            pe.wait_ge(act_lo_ready[t], n)
                            pe.wait_ge(act_ready[t], n)
                        for k in range(KC):
                            last = mm3(bank(2 * t + part, FB), tile_in(t, k), split_piece(part, k, FB), k == 0, k == KC - 1)
                            if part == 1 and t == 1 and k == KC - 3:
                                turn(n, 0, FB)
                        last.then_inc((tile0_ps, piece_used)[t], 1)
                pe.wait_ge(split_ready, 3 * n + 3)
                for t in range(NT):
                    pe.wait_ge(act_lo_ready[t], n + 1)
                    for j in range(FB // P):
                        last = down_rows(t, 2, [j], 0, first)
                        if t == 0 and j == 0:
                            turn(n, 1, FB)
                last.then_inc(piece_used, 1)

            def moe_block(m):
                n, p0 = N_FFB + m, piece_at(m)
                for i in range(MOE_PIECES):
                    pe.wait_ge(split_ready, p0 + i + 1)
                    if i < 8:
                        t, part, half = i // 4, i % 4 // 2, i % 2
                        if i % 4 == 0:
                            pe.wait_ge(act_lo_ready[t], n)
                            pe.wait_ge(act_ready[t], n)
                        for k in range(KC // 2):
                            last = mm3(bank(2 * t + part), tile_in(t, KC // 2 * half + k), split_piece(i, k, EB),
                                       half == 0 and k == 0, half == 1 and k == KC // 2 - 1)
                    else:
                        t, half = (i - 8) // 2, i % 2
                        if half == 0:
                            pe.wait_ge(act_lo_ready[t], n + 1)
                        last = down_rows(t, i, range(2), 2 * half)
                    last.then_inc(piece_used, 1)
                    if i == 5:
                        turn(n, 0, EB)
                    if i == 8:
                        turn(n, 1, EB)

            pe.wait_ge(cst_in, 16)
            pe.wait_ge(x_in_tok, 16)
            for t in range(NT):
                for k in range(KC):
                    last = pe.transpose(ps_t[:, 1024 * t + P * k:1024 * t + P * k + P], tokm[:, t, P * k:P * k + P], ident)
                last.then_inc(xt_ps, 1)
            mod_sums(0)
            mixer(0)

            mean_square(1)
            pe.wait_ge(h_ready, KC * 2)
            pe.wait_ge(zd_free, ZD[0, "end"])
            pe.wait_ge(f_lo_ready, NT)
            ffn_block(0)
            with pe.Fori(1, N_FFB) as n:
                ffn_block(n)
            pe.wait_ge(f_ytok, 2)
            for k in range(KC):
                for t in range(NT):
                    last = pe.transpose(ps_t[:, SEQ * k + P * t:SEQ * k + P * t + P], tokm[:, t, P * k:P * k + P], ident)
                last.then_inc(f_tr, 1)
            mixer(1)

            mean_square(3)
            pe.wait_ge(h_ready, KC * 4)
            pe.wait_ge(zd_free, ZD[1, "end"])
            for t in range(NT):
                for k in range(KC):
                    last = mm(bank(0, NT * NE)[:, NE * t:NE * t + NE], hT[:, k, P * t:P * t + P],
                              router_sb[:, NE * k:NE * k + NE], k == 0, k == KC - 1)
            last.then_inc(logits_ps, 1)
            for t in range(NT):
                for k in range(KC):
                    o = 2048 + 1024 * t + P * k
                    last = pe.transpose(ps_t[:, o:o + P], hT[:, k, P * t:P * t + P], ident)
            last.then_inc(htok_ps, 1)
            pe.wait_ge(r_sel_ready, 1)
            rank, half0, half1 = cc(C_RANK), r_sel[:, 0:NE], r_sel[:, NE:2 * NE]
            mm(ps_t[:, 512:512 + NE], rank, half0)
            mm(ps_t[:, 512 + NE:512 + 2 * NE], rank, half1, True, False)
            mm(ps_t[:, 512 + NE:512 + 2 * NE], ones, half0, False, True)
            mm(ps_t[:, 512 + 2 * NE:512 + 3 * NE], ones, half0, True, False)
            mm(ps_t[:, 512 + 2 * NE:512 + 3 * NE], ones, half1, False, True).then_inc(rank_ps, 1)

            pe.wait_ge(jobs_ready, 1)
            pe.wait_ge(htok_ready, 1)
            n_pairs = pe.value_load(job_i[0:1, N_JOBS:N_JOBS + 1], min_val=NE // 2, max_val=N_JOBS // 2)
            with pe.Fori(0, n_pairs) as pair:
                pe.wait_ge(sel_ready, 8 * (pair + 1))
                pe.wait_ge(comb_done, pair + 1)
                for s in range(2):
                    for t in range(NT):
                        o = 3072 + SEQ * s + P * t
                        last = pe.transpose(ps_t[:, o:o + P], sel_g[:, 2 * s + t, :], ident)
                last.then_inc(gather_ps, 1)
                for s in range(2):
                    for k in range(KC):
                        o = 2048 * s + P * k
                        for t in range(NT):
                            last = mm(ps_t[:, o:o + P], tokm[:, t, P * k:P * k + P], sel[:, 2 * s + t, :], t == 0, t == 1)
                    last.then_inc(gather_ps, 1)
                pe.wait_ge(gather_d_ready, pair + 1)
                pe.wait_ge(f_lo_ready, NT + 2 * (pair + 1))
                for c in range(4):
                    mm(bank(4 + c), zeros16[:, 0:P], zeros16[:, 0:512], True, True, skip_group_check=True)
                with pe.Fori(0, N_EB) as b:
                    moe_block(pair * N_EB + b)
                pe.wait_ge(y_ready, 2 * (pair + 1))
                for k in range(KC):
                    for s in range(2):
                        last = mm(ps_t[:, SEQ * k:SEQ * k + SEQ], y_slot[:, s, P * k:P * k + P], sel_t[:, s, :], s == 0, s == 1)
                last.then_inc(comb_ps, 1)

            mean_square(4)
            pe.wait_ge(h_ready, KC * 5)
            for t in range(NT):
                for k in range(KC):
                    o = 1024 * t + P * k
                    last = pe.transpose(ps_t[:, o:o + P], hT[:, k, P * t:P * t + P], ident)
                last.then_inc(out_ps, 1)


def kernel(**inputs):
    import numpy as _np
    import concourse.bacc as _bacc
    from concourse import mybir as _mybir
    from concourse.bass_utils import run_bass_kernel_spmd as _run

    a = {k: _np.ascontiguousarray(v) for k, v in inputs.items()}

    def columns(v):
        return v.reshape(-1, P).T

    params = _np.zeros((P, P_END), _np.float32)
    for l in range(DEPTH):
        parts = {"norm_g": a["norm_g"][l], "ada_b": a["ada_b"][l], "pool_scale": a["pool_scale"][l],
                 "conv_b": a["conv_b"][l], "ln_g": a["conv_ln_g"][l], "ln_b": a["conv_ln_b"][l],
                 "mu": a["rwkv_mu"][l], "a0": a["rwkv_a0"][l], "kk_scale": a["rwkv_kk_scale"][l],
                 "ka": a["rwkv_ka"][l], "rk": a["rwkv_rk"][l], "lnx_g": a["rwkv_lnx_g"][l],
                 "lnx_b": a["rwkv_lnx_b"][l]}
        for name, v in parts.items():
            c = columns(v)
            o = l * P_W + P_OFF[name]
            params[:, o:o + c.shape[1]] = c
        o = l * P_W + P_OFF["conv_w"]
        for b in range(2):
            params[:, o + b * CONV_K:o + (b + 1) * CONV_K] = a["conv_w"][l][:, P * b:P * b + P].T
        if l > 0:
            params[VR, l * P_W + P_OFF["vmu"]] = a["vres_mu"][l - 1]
            o = l * P_W + P_OFF["v0"]
            params[:, o:o + 4] = columns(a["vres_v0"][l - 1])
    params[:, P_C:P_C + KC] = columns(a["c"][0])
    params[:, P_FG:P_FG + KC] = columns(a["final_norm_g"])

    arrays = {
        "x": a["x"][0], "consts": shape_constants(), "params": params, "ada_w": a["ada_w"], "w_in": a["w_in"],
        "pool_w": a["pool_w"], "pool_proj": a["pool_proj"], "conv_proj": a["conv_proj"], "w0": a["rwkv_w0"],
        "w2": a["rwkv_w2"], "a2": a["rwkv_a2"], "g2": a["rwkv_g2"], "rwkv_proj": a["rwkv_proj"],
        "vres_down": a["vres_w_down"], "vres_v2": a["vres_v2"], "w_o": a["w_o"], "ffn_w1": a["ffn_w1"][0],
        "ffn_w3": a["ffn_w3"][0], "ffn_w2": a["ffn_w2"][0], "router": a["moe_router"][0],
        "moe_w1": a["moe_w1"][0], "moe_w3": a["moe_w3"][0], "moe_w2": a["moe_w2"][0],
    }
    nc = _bacc.Bacc("TRN2", target_bir_lowering=False, num_devices=1)
    f32 = _mybir.dt.float32
    args = [nc.dram_tensor(f"in_{n}", v.shape, f32, kind="ExternalInput").ap() for n, v in arrays.items()]
    y = nc.dram_tensor("out_y", (SEQ, D), f32, kind="ExternalOutput").ap()
    build_trunk(nc, *args, y)
    r = _run(nc, [{f"in_{n}": v for n, v in arrays.items()}], core_ids=[0])
    return r.results[0]["out_y"].reshape(1, SEQ, D)
```

```python
from contextlib import ExitStack

import numpy as np

import concourse.bass as bass
from concourse import mybir

P = 128
D = 1024
SEQ = 256
DEPTH = 2
KC = D // P
NT = SEQ // P
CONV_K = 31
NB_RKV = 12
COL_RWKV, COL_GATE = 768, 2432
GATE_R, GATE_P, GATE_C = COL_GATE + 2 * D, COL_GATE, COL_GATE + D
D_FF, D_FFE, NE = 2816, 3584, 8
FB = 256
EB = 512
N_FFB = D_FF // FB
N_EB = D_FFE // EB
N_JOBS = 12
N_RAW_P, N_SPLIT = 6, 3
FFN_PIECES, MOE_PIECES = 3, 12
CH = 64
VR = slice(64, 80)
N_RAW = 2
LEVELS = 6
ADA_Z = 1
TAPS = [list(range(NB_RKV + 1)), [(CONV_K - 1) * b // NB_RKV for b in range(NB_RKV + 1)]]
DECAY = float(np.exp(-0.5))
PAD_P, PAD_C = 16, CONV_K - 1
MIX_FILLS = 16
ADA_LEAD = 12

C_ID, C_ONES, C_BONES, C_TRI_S, C_TRI_I, C_LOW0 = (P * i for i in range(6))
C_LVL = 6 * P
C_RANK = C_LVL + LEVELS * P
C_IOTA = C_RANK + P
C_CNT = C_IOTA + P
C_LOW8 = C_CNT + 2 * SEQ
C_EID = C_LOW8 + NE * NE
C_M256 = C_EID + NE
C_ZERO = C_M256 + P
C_END = C_ZERO + 256

PARAMS = [("norm_g", 16), ("ada_b", 48), ("pool_scale", 2), ("conv_w", 2 * CONV_K), ("conv_b", 2),
          ("ln_g", 2), ("ln_b", 2), ("mu", 13), ("a0", 4), ("kk_scale", 4), ("ka", 4),
          ("rk", 4), ("lnx_g", 4), ("lnx_b", 4), ("vmu", 1), ("v0", 4)]
P_OFF = {}
_at = 0
for _n, _w in PARAMS:
    P_OFF[_n] = _at
    _at += _w
P_W = _at
P_C = DEPTH * P_W
P_FG = P_C + KC
P_END = P_FG + KC


def shape_constants():
    i = np.arange(P)
    row, col = i[:, None], i[None, :]
    same = row // CH == col // CH
    c = np.zeros((P, C_END), np.float32)
    c[:, C_ID:C_ID + P] = row == col
    c[:, C_ONES:C_ONES + P] = 1
    c[:, C_BONES:C_BONES + P] = same
    c[:, C_TRI_S:C_TRI_S + P] = same & (row < col)
    c[:, C_TRI_I:C_TRI_I + P] = same & (row <= col)
    for m in range(LEVELS):
        n = 1 << m
        lvl = (row // (2 * n) == col // (2 * n)) & (row % (2 * n) < n) & (col % (2 * n) >= n)
        c[:, C_LVL + m * P:C_LVL + (m + 1) * P] = lvl
    c[:, C_LOW0:C_LOW0 + P] = c[:, C_LVL:C_LVL + P].T
    c[:, C_RANK:C_RANK + P] = row < col
    c[:, C_IOTA:C_IOTA + P] = col
    pos = np.arange(1, SEQ + 1)
    for b in range(2):
        for par in range(2):
            win = 2 ** (2 * b + par + 1)
            c[64 * par:64 * par + 64, C_CNT + b * SEQ:C_CNT + (b + 1) * SEQ] = \
                1.0 / np.minimum(pos, win).astype(np.float32)
    low = (np.arange(NE)[:, None] > np.arange(NE)[None, :]).astype(np.float32)
    c[:, C_LOW8:C_LOW8 + NE * NE] = low.reshape(1, -1)
    c[:, C_EID:C_EID + NE] = np.arange(NE)
    c[:, C_M256:C_M256 + P] = 1.0 / 256
    return c


def build_trunk(nc, x_in, consts, params, ada_w, w_in, pool_w, pool_proj, conv_proj, w0_row,
                w2, a2, g2, rwkv_proj, vres_down, vres_v2, w_o, ffn_w1, ffn_w3, ffn_w2,
                router, moe_w1, moe_w3, moe_w2, out):
    f32, i32 = mybir.dt.float32, mybir.dt.int32
    ALU, ACT, AX = mybir.AluOpType, mybir.ActivationFunctionType, mybir.AxisListType
    ds = bass.ds
    ctx = ExitStack()
    with ctx:
        def sb(name, cols, dt=f32):
            return ctx.enter_context(nc.sbuf_tensor(name, [P, cols], dt))

        def sem(name):
            return ctx.enter_context(nc.semaphore(name))

        def v3(t, a, n, w):
            return t[:, a:a + n * w].rearrange("p (n w) -> p n w", w=w)

        ring = sb("ring", 3 * 4096)
        scr_at = nc.sbuf_base
        scr = sb("scr", 3 * 4096)
        e1, e2, a_b, kk_a, gg, bon = (v3(scr, 1024 * i, 4, SEQ) for i in range(6))
        ltm, lvl_l, tinv, tinv_t, p_sb, ak_t = (v3(scr, 6144 + 1024 * i, 8, P) for i in range(6))
        sig_tok = v3(scr, 6144, NT, 512)
        o_state, o_all = e1, e2
        inv4_t = scr[:, 8192:9216]
        inv4 = v3(scr, 8192, 4, SEQ)
        rkv_at = nc.sbuf_base
        rkv_t = sb("rkv", NB_RKV * SEQ)
        rkv = v3(rkv_t, 0, NB_RKV, SEQ)
        rr, kkv, vv = rkv[:, 0:4, :], rkv[:, 4:8, :], rkv[:, 8:12, :]
        lora_in = sb("lora_in", SEQ)
        vres_in = sb("vres_in", SEQ)
        sg_t = sb("sg", 2 * SEQ)
        v_first_at = nc.sbuf_base
        v_first = sb("v_first", 4 * SEQ)
        state_t = sb("state", 256)
        state = v3(state_t, 0, 4, 64)
        chunk_decay = sb("chunk_decay", 16)
        x_t = sb("x", KC * SEQ)
        xT = v3(x_t, 0, KC, SEQ)
        h_at = nc.sbuf_base
        h_t = sb("h", KC * SEQ)
        hT = v3(h_t, 0, KC, SEQ)
        merged_t = sb("merged", KC * SEQ)
        merged = v3(merged_t, 0, KC, SEQ)
        yT = merged
        gr_at = nc.sbuf_base
        gr_t = sb("gate_r", KC * SEQ)
        gate_r = v3(gr_t, 0, KC, SEQ)
        tokm = v3(gr_t, 0, NT, D)
        pu = sb("pool_u", 2 * (PAD_P + SEQ))
        pa_at = nc.sbuf_base
        pa = sb("pool_a", 2 * (PAD_P + SEQ))
        pbuf = sb("pool_b", 2 * (PAD_P + SEQ))
        pu3, pa3, pb3 = (v3(t, 0, 2, PAD_P + SEQ) for t in (pu, pa, pbuf))
        ca_at = nc.sbuf_base
        ca_t = sb("conv_a", 2 * (PAD_C + SEQ))
        ca = v3(ca_t, 0, 2, PAD_C + SEQ)
        cb_t = sb("conv_b_", 2 * SEQ)
        cb = v3(cb_t, 0, 2, SEQ)
        cy_t = sb("conv_y", 2 * SEQ)
        cy = v3(cy_t, 0, 2, SEQ)
        sg = v3(sg_t, 0, 2, SEQ)
        pl = sg
        tmp = sb("tmp", SEQ)
        rstd = sb("rstd", SEQ)
        wide_at = nc.sbuf_base
        wide = sb("wide", 6 * 1024)
        ada_ring = v3(wide, 0, 3, 1024)
        ada_acc = wide[:, 3072:6144]
        tok = v3(wide, 0, 4, 512)
        ht_sb = v3(wide, 2048, 4, P)
        akv, g_sb, u_sb = (v3(wide, 2560 + 512 * i, 8, 64) for i in range(3))
        act_sb = v3(wide, 0, 2, 512)
        sig_sb = v3(wide, 2048, 2, 512)
        sel_g = v3(wide, 5632, 4, P)
        slot_gate = state_t[:, 0:2]
        lora_w = sb("lora_w", 512)
        w0_sb = sb("w0_sb", 512)
        pool_wsb = sb("pool_wsb", 2 * 64)
        cst = sb("cst", C_END)
        par = sb("par", P_END)
        mods_t = sb("mods", 4 * 24)
        mods = v3(mods_t, 0, 4, 24)
        gain_t = sb("gain", 4 * 8)
        gain = v3(gain_t, 0, 4, 8)
        c_sig = sb("c_sig", KC)
        c_silu = sb("c_silu", KC)
        router_sb = sb("router_sb", KC * NE)

        f32r = mybir.dt.float32r

        def over_sb(name, at, n, w):
            t = nc.alloc_sbuf_tensor_at(name, [P, n * w], f32r, offset=at)
            return t[:, :].rearrange("p (n w) -> p n w", w=w)

        PW = 2048
        w_hi = over_sb("w_hi", scr_at, N_SPLIT, PW)
        w_lo = over_sb("w_lo", scr_at + 4 * N_SPLIT * PW, N_SPLIT, PW)
        f_hi = over_sb("f_hi", rkv_at, KC, SEQ)
        f_lo = over_sb("f_lo", rkv_at + 4 * 2048, KC, SEQ)
        act_hi = over_sb("act_hi", wide_at + 4096, 2, 512)
        act_lo = over_sb("act_lo", h_at, 2, 512)
        pieces = v3(ring, 0, N_RAW_P, PW)
        tok_hi = over_sb("tok_hi", gr_at, NT, D)
        tok_lo = [over_sb(f"tok_lo{t}", at, 1, D)[:, 0, :] for t, at in enumerate((h_at + 4096, v_first_at))]
        y_hi = over_sb("y_hi", wide_at + 4 * 3072, 2, D)
        y_lo = over_sb("y_lo", ca_at, 2, D)
        sel = over_sb("sel", wide_at + 4 * 5120, NT, 2 * P)
        sel_t = over_sb("sel_t", pa_at, 2, SEQ)

        widths = [NT * NE] * 6 + [NT, NT] + [NE] * 3 + [4 * NE] + [NT * N_JOBS] * 2
        starts = [sum(widths[:i]) for i in range(len(widths))]
        (lg, r_cnt, r_sel, r_exp, r_gate, r_rank, r_max, r_den, n_tok, over, prev, onehot, job_rank,
         job_gate) = (pbuf[:, o:o + w] for o, w in zip(starts, widths))
        cmp_t = pu[:, 0:NT * NE * NE]
        cmp2_t = pu[:, NT * NE * NE:2 * NT * NE * NE]
        raw_t = sb("raw", N_RAW * (SEQ + 1))
        raw = v3(raw_t, 0, N_RAW, SEQ + 1)
        job_f = sb("job_f", N_JOBS + 4)
        job_i = sb("job_i", N_JOBS + 4, i32)

        ps_t = ctx.enter_context(nc.psum_tensor("ps", [P, 8 * 512], f32))
        ps = ps_t[:, :].rearrange("p (b n) -> p b n", b=8)

        def bank(b, n=512, p0=0, p1=P):
            return ps_t[p0:p1, 512 * b:512 * b + n]

        def cc(col, n=P, p0=0, p1=P):
            return cst[p0:p1, col:col + n]

        def pcol(l, name, i=0, p0=0, p1=P):
            o = l * P_W + P_OFF[name] + i
            return par[p0:p1, o:o + 1]

        ident, ones, bones, mean256 = cc(C_ID), cc(C_ONES), cc(C_BONES), cc(C_M256)
        zeros16 = cst[:, C_ZERO:C_ZERO + 256].bitcast(mybir.dt.bfloat16)


        def places(groups):
            at, first = 0, {}
            for l in range(DEPTH):
                for name, n in groups(l):
                    first[l, name] = at
                    at += n
                first[l, "end"] = at
            return first

        ZA = places(lambda l: [("pc", 6), ("z", NB_RKV + 1 + l), ("a", 4), ("g", 4), ("vres", 4 * l),
                               ("gate_r", KC // 2), ("gate_p", KC), ("gate_c", KC), ("gate_r2", KC // 2)])
        ZD = places(lambda l: [("kk", 4), ("bonus", 4), ("y_pool", KC), ("y_conv", KC), ("mean", 4),
                               ("var", 4), ("y_rwkv", KC), ("w_o", KC)])

        ZMIX = (0, NB_RKV + 1)
        T_INC = 4 * LEVELS
        SMALL = (16 * 10, 16 * 18)

        def head_col(h):
            return P * (h % 4) + 64 * (h // 4)

        cst_in, par_in, x_in_tok, small_in = sem("cst_in"), sem("par_in"), sem("x_in_tok"), sem("small_in")
        ada_full = [sem(f"ada_full{i}") for i in range(3)]
        lead_full, lead_used = [sem(f"lead_full{i}") for i in range(ADA_LEAD // 4)], sem("lead_used")
        ada_free, mod_ps, mods_ready = sem("ada_free"), sem("mod_ps"), sem("mods_ready")
        ring_full = [sem(f"ring_full{i}") for i in range(3)]
        za_ready, za_done, zd_ready, zd_free = sem("za_ready"), sem("za_done"), sem("zd_ready"), sem("zd_free")
        mix_done, pads_ready = sem("mix_done"), sem("pads_ready")
        x_ready, xsq_ready, ssum_ps, hs_ready, h_ready, xt_ps = (
            sem(n) for n in ("x_ready", "xsq_ready", "ssum_ps", "hs_ready", "h_ready", "xt_ps"))
        c_sig_ready = sem("c_sig_ready")
        pooled, pool_ps, pool_y = sem("pooled"), sem("pool_ps"), sem("pool_y")
        conv_dev = sem("conv_dev")
        conv_u, conv_mean, conv_sq, conv_var, conv_un, conv_sg, conv_y = (
            sem(n) for n in ("conv_u", "conv_mean", "conv_sq", "conv_var", "conv_un", "conv_sg", "conv_y"))
        lora_ready, sigt_ps, sigt_ready = sem("lora_ready"), sem("sigt_ps"), sem("sigt_ready")
        kk_ready, kksq_ready, rkk_ready, cum_ps = sem("kk_ready"), sem("kksq_ready"), sem("rkk_ready"), sem("cum_ps")
        decay_ready, decay_used, tilde_ready = sem("decay_ready"), sem("decay_used"), sem("tilde_ready")
        amat_ps, amat_ready, tok_ps, tok_a_ready, tok_d_ready = (
            sem(n) for n in ("amat_ps", "amat_ready", "tok_ps", "tok_a_ready", "tok_d_ready"))
        lvl_ready, p_ps, p_ready, dt_ps, t_ready = (sem(n) for n in ("lvl_ready", "p_ps", "p_ready", "dt_ps", "t_ready"))
        ht_ps, ht_ready, akv_ps, akv_ready, g_ps, g_ready = (
            sem(n) for n in ("ht_ps", "ht_ready", "akv_ps", "akv_ready", "g_ps", "g_ready"))
        rb_ps, rb_ready, u_ps, u_ready, o3_ps, o3_ready, s_ps, s_ready = (
            sem(n) for n in ("rb_ps", "rb_ready", "u_ps", "u_ready", "o3_ps", "o3_ready", "s_ps", "s_ready"))
        o_ps, o_ready, o_dev, o_sq, o_final, merged_ready = (
            sem(n) for n in ("o_ps", "o_ready", "o_dev", "o_sq", "o_final", "merged_ready"))
        piece_full = [sem(f"piece_full{i}") for i in range(N_RAW_P)]
        hi_ready, split_ready, piece_used = sem("hi_ready"), sem("split_ready"), sem("piece_used")
        tile0_ps, f_hi_ready, f_lo_ready = sem("tile0_ps"), sem("f_hi_ready"), sem("f_lo_ready")
        sig_ready = [sem(f"sig_ready{i}") for i in range(2)]
        silu_ready = [sem(f"silu_ready{i}") for i in range(2)]
        act_ready = [sem(f"act_ready{i}") for i in range(2)]
        actt_ps = [sem(f"actt_ps{i}") for i in range(2)]
        act_hi_ready = [sem(f"act_hi_ready{i}") for i in range(2)]
        act_lo_ready = [sem(f"act_lo_ready{i}") for i in range(2)]
        f_ytok, f_tr = sem("f_ytok"), sem("f_tr")
        htok_ps, htok_ready = sem("htok_ps"), sem("htok_ready")
        logits_ps, r_maxed, r_exped, r_sel_ready, rank_ps, jobs_ready = (
            sem(n) for n in ("logits_ps", "r_maxed", "r_exped", "r_sel_ready", "rank_ps", "jobs_ready"))
        tok_lo_ready, sel_ready, gather_ps, selt_ps, selt_ready, y_hi_ready, y_lo_ready, comb_ps, comb_done = (
            sem(n) for n in ("tok_lo_ready", "sel_ready", "gather_ps", "selt_ps", "selt_ready", "y_hi_ready",
                             "y_lo_ready", "comb_ps", "comb_done"))
        out_ps, out_rows, out_done = sem("out_ps"), sem("out_rows"), sem("out_done")
        dve_chain, pool_chain = sem("dve_chain"), sem("pool_chain")
        inv_in, rstd_ready = sem("inv_in"), sem("rstd_ready")

        def cols_of(l, c0, n):
            return w_in[l, :, c0:c0 + n].rearrange("(k p) c -> p k c", p=P)

        def rows_of(w, k0, n):
            return w[k0 * P:(k0 + n) * P, :].rearrange("(k p) c -> p k c", p=P)

        def mixer_fills(l):
            z, zd = lambda name, n: (za_ready, ZA[l, name] + n), lambda name, n: (zd_ready, ZD[l, name] + n)
            fills = [([(0, cols_of(l, 0, 512))], z("pc", 4)), ([(0, cols_of(l, 512, 256))], z("pc", 6))]
            fills += [([(0, cols_of(l, COL_RWKV + 512 * i, 512))], z("z", 4 * i + 4)) for i in range(3)]
            last = [(0, cols_of(l, COL_RWKV + 1536, P))]
            if l > 0:
                last.append((KC * P, rows_of(vres_down[l - 1], 0, KC)))
            fills.append((last, z("z", NB_RKV + 1 + l)))
            fills.append(([(0, cols_of(l, GATE_R, 512))], z("gate_r", 4)))
            fills.append(([(0, cols_of(l, GATE_P, 512))], z("gate_p", 4)))
            fills.append(([(0, rows_of(pool_proj[l], 0, 2)), (2048, rows_of(conv_proj[l], 0, 2))],
                          zd("y_conv", KC)))
            fills.append(([(0, cols_of(l, GATE_P + 512, 512))], z("gate_p", 8)))
            fills += [([(0, cols_of(l, GATE_C + 512 * i, 512))], z("gate_c", 4 * i + 4)) for i in range(2)]
            fills.append(([(0, rows_of(rwkv_proj[l], 0, 4))], zd("y_rwkv", KC)))
            fills.append(([(0, cols_of(l, GATE_R + 512, 512))], z("gate_r2", 4)))
            fills += [([(0, rows_of(w_o[l], 4 * i, 4))], zd("w_o", KC)) for i in range(2)]
            return fills

        SLOT = [0, 1, 2, 0, 1, 2, 0, 1, 2, 0, 1, 0, 1, 2, 0, 2]
        FILLS, FULL, AFTER = [], [], []
        last_in, landed = {}, {}
        for l in range(DEPTH):
            for i, (dmas, free) in enumerate(mixer_fills(l)):
                s = SLOT[i]
                FILLS.append((s, dmas))
                AFTER.append(last_in.get(s))
                landed[s] = landed.get(s, 0) + 16 * len(dmas)
                FULL.append(landed[s])
                last_in[s] = free
            last_in = {}

        def fill_at(n, width, off=0, k=None):
            base = 4096 * FILLS[n][0] + off
            k = k or 4096 // width
            return ring[:, base:base + k * width].rearrange("p (k c) -> p k c", c=width)

        N_FFN_P = FFN_PIECES * N_FFB

        def piece_at(n):
            return N_FFN_P + MOE_PIECES * n

        FULL0 = [len(range(i, N_FFN_P, N_RAW_P)) for i in range(N_RAW_P)]

        block = ctx.enter_context(nc.Block())

        @block.sync
        def _(sp):
            sp.dma_start(tokm, x_in.rearrange("(t p) d -> p t d", p=P)).then_inc(x_in_tok, 16)
            sp.dma_start(cst[:, :], consts).then_inc(cst_in, 16)
            for i in range(ADA_LEAD // 4):
                rows, c0 = 4 * P * (i % 2), 1024 * (i // 2)
                sp.dma_start(v3(ring, 4096 * i, 4, 1024), ada_w[0, 0, rows:rows + 4 * P, c0:c0 + 1024]
                             .rearrange("(k p) c -> p k c", p=P)).then_inc(lead_full[i], 16)

            def mixer_weights(l):
                for i in range(MIX_FILLS):
                    n = MIX_FILLS * l + i
                    s, dmas = FILLS[n]
                    if n < 3:
                        sp.wait_ge(lead_used, 4 * (n + 1))
                    if AFTER[n] is not None:
                        sp.wait_ge(*AFTER[n])
                    for off, src in dmas:
                        k, w = src.shape[1], src.shape[2]
                        sp.dma_start(fill_at(n, w, off, k), src).then_inc(ring_full[s], 16)

            def ffn_weights(n, parity):
                for part, w in enumerate((ffn_w1, ffn_w3, ffn_w2)):
                    slot = 3 * parity + part
                    if not isinstance(n, int) or n >= 2:
                        sp.wait_ge(split_ready, 3 * n + part - N_RAW_P + 1)
                    src = w[:, ds(n * FB, FB)] if part < 2 else w[ds(n * FB, FB), :]
                    dst = pieces[:, slot, :].rearrange("p (k c) -> p k c", c=FB if part < 2 else D)
                    sp.dma_start(dst, src.rearrange("(k p) c -> p k c", p=P)).then_inc(piece_full[slot], 16)

            def moe_piece(m, b, e, i):
                s, part = (i // 4, i % 4 // 2) if i < 8 else ((i - 8) // 2, 2)
                half = i % 2
                if not isinstance(m, int) or m > 0 or i >= N_RAW_P:
                    sp.wait_ge(split_ready, piece_at(m) + i - N_RAW_P + 1)
                if part < 2:
                    src = (moe_w1, moe_w3)[part][ds(e[s], 1), 512 * half:512 * half + 512, ds(b * EB, EB)]
                else:
                    src = moe_w2[ds(e[s], 1), ds(b * EB + 256 * half, 256), :]
                dst = pieces[:, i % N_RAW_P, :].rearrange("p (k c) -> p k c", c=EB if part < 2 else D)
                sp.dma_start(dst, src.rearrange("o (k p) c -> p (o k) c", p=P)).then_inc(piece_full[i % N_RAW_P], 16)

            mixer_weights(0)
            sp.wait_ge(zd_ready, ZD[0, "end"])
            ffn_weights(0, 0)
            ffn_weights(1, 1)
            ffn_weights(2, 0)
            with sp.Fori(0, (N_FFB - 3) // 2) as it:
                ffn_weights(2 * it + 3, 1)
                ffn_weights(2 * it + 4, 0)
            sp.wait_ge(split_ready, N_FFN_P)
            mixer_weights(1)

            sp.wait_ge(zd_ready, ZD[1, "end"])
            for i in range(N_RAW_P):
                moe_piece(0, 0, (0, 1), i)
            sp.wait_ge(jobs_ready, 1)
            n_pairs = sp.value_load(job_i[0:1, N_JOBS:N_JOBS + 1], min_val=NE // 2, max_val=N_JOBS // 2)
            for i in range(N_RAW_P, MOE_PIECES):
                moe_piece(0, 0, (0, 1), i)
            with sp.Fori(1, N_EB) as b:
                for i in range(MOE_PIECES):
                    moe_piece(b, b, (0, 1), i)
            with sp.Fori(1, n_pairs) as pair:
                e = [sp.value_load(job_i[0:1, ds(2 * pair + s, 1)], min_val=0, max_val=NE - 1) for s in range(2)]
                with sp.Fori(0, N_EB) as b:
                    for i in range(MOE_PIECES):
                        moe_piece(pair * N_EB + b, b, e, i)
            for t in range(NT):
                sp.wait_ge(out_rows, t + 1)
                sp.dma_start(out.rearrange("(t p) d -> t p d", p=P)[t], tokm[:, t, :]).then_inc(out_done, 16)
            sp.wait_ge(out_done, 16 * NT)

        @block.gpsimd
        def _(pool):
            chain = [0]

            def link(ins):
                chain[0] += 1
                ins.then_inc(pool_chain, 1)
                pool.wait_ge(pool_chain, chain[0])
                return ins

            pool.dma_start(par[:, :], params).then_inc(par_in, 16)
            ada_cols = ada_w.rearrange("l i (k p) (t c) -> (l i) t k p c", p=P, c=1024)

            def ada_chunk(li, n):
                b = n % 3
                pool.wait_ge(ada_free, 24 * li + n - ADA_LEAD + 1)
                pool.dma_start(ada_ring[:, b, :], ada_cols[ds(li, 1), n // KC, n % KC].rearrange("o p c -> (o p) c")
                               ).then_inc(ada_full[b], 16)

            def ada_stream(first, last):
                with pool.Fori(first, last) as li:
                    for n in range(3 * KC):
                        ada_chunk(li, n)

            def small_weights(l):
                pool.dma_start(lora_w[0:32, :], w2[l]).then_inc(small_in, 16)
                pool.dma_start(lora_w[32:64, :], a2[l]).then_inc(small_in, 16)
                pool.dma_start(lora_w[64:P, :], g2[l]).then_inc(small_in, 16)
                pool.dma_start(w0_sb[0:1, :], w0_row[l:l + 1, :]).then_inc(small_in, 16)
                for g in range(4):
                    q = 64 * (g % 2)
                    pool.dma_start(pool_wsb[q:q + 64, 64 * (g // 2):64 * (g // 2) + 64],
                                   pool_w[l, g]).then_inc(small_in, 16)
                if l == 0:
                    pool.dma_start(w0_sb[VR, :], vres_v2[0]).then_inc(small_in, 16)
                    pool.dma_start(router_sb[:, :].rearrange("p (k e) -> p k e", e=NE),
                                   router.rearrange("(k p) e -> p k e", p=P)).then_inc(small_in, 16)

            def pooling(l):
                pool.wait_ge(za_done, ZA[l, "pc"] + 2)
                src = pu3
                for g, dst in enumerate((pa3, pb3, pa3, pb3)):
                    sh = 1 << g
                    lo = 2 * sh - 1
                    link(pool.tensor_tensor(dst[:, :, lo:], src[:, :, lo:],
                                            src[:, :, lo - sh:PAD_P + SEQ - sh], ALU.add))
                    q, b = slice(64 * (g % 2), 64 * (g % 2) + 64), g // 2
                    link(pool.tensor_tensor(pl[q, b, :], dst[q, b, PAD_P:],
                                            cst[q, C_CNT + b * SEQ:C_CNT + (b + 1) * SEQ], ALU.mult))
                    pool.tensor_tensor(pl[q, b, :], pl[q, b, :], pu3[q, b, PAD_P:], ALU.subtract
                                       ).then_inc(pooled, 1)
                    pool.wait_ge(pooled, 4 * l + g + 1)
                    src = dst

            def level_masks(l, hf):
                for m in range(1, LEVELS):
                    for g in range(2):
                        if m == 1:
                            pool.wait_ge(amat_ready, 2 * (2 * l + hf) + g + 1)
                        else:
                            pool.wait_ge(p_ps, ((2 * l + hf) * (LEVELS - 1) + m - 2) * 2 + g + 1)
                        pool.tensor_tensor(lvl_l[:, 4 * g:4 * g + 4, :], ltm[:, 4 * g:4 * g + 4, :],
                                           cc(C_LVL + m * P).unsqueeze(1).broadcast_to([P, 4, P]), ALU.mult
                                           ).then_inc(lvl_ready, 1)

            for n in range(ADA_LEAD, 3 * KC):
                ada_chunk(0, n)
            small_weights(0)
            pool.wait_ge(cst_in, 16)
            pool.wait_ge(pads_ready, 1)
            for n in range(2 * KC):
                ada_chunk(1, n)
            pooling(0)
            for n in range(2 * KC, 3 * KC):
                ada_chunk(1, n)
            ada_stream(2, 3)
            level_masks(0, 0)
            level_masks(0, 1)
            pool.wait_ge(o_final, 1)
            small_weights(1)
            pooling(1)
            ada_stream(3, 4)
            level_masks(1, 0)
            level_masks(1, 1)

        @block.scalar
        def _(act):
            za = [0]

            def evac(dst, func=ACT.Identity, rows=slice(0, P), **kw):
                n = za[0]
                za[0] += 1
                act.wait_ge(za_ready, n + 1)
                act.activation(dst, bank(n % 2, SEQ)[rows, :], func, **kw).then_inc(za_done, 1)

            roots = [0]

            def root(a):
                roots[0] += 1
                act.wait_ge(inv_in, roots[0])
                act.activation(a, a, ACT.Sqrt).then_inc(rstd_ready, 1)

            def square_x(li):
                act.wait_ge(x_ready, KC * (li + 1))
                act.activation(h_t[:, :], x_t[:, :], ACT.Square, scale=1.0 / 32).then_inc(xsq_ready, 1)

            def shifted(li, dst, done):
                for k in range(KC):
                    act.wait_ge(hs_ready, KC * li + k + 1)
                    act.activation(dst[:, k, :], hT[:, k, :], ACT.Identity, bias=mods[:, li, k:k + 1]).then_inc(done, 1)

            def norm_in(li):
                square_x(li)
                root(rstd[:, :])
                shifted(li, hT, h_ready)

            def mixer(l):
                norm_in(2 * l)
                if l == 0:
                    act.wait_ge(pads_ready, 1)
                for b in range(2):
                    evac(pu3[:, b, PAD_P:])
                for b in range(2):
                    evac(ca[:, b, PAD_C:])
                for b in range(2):
                    evac(cb[:, b, :], ACT.Sigmoid)
                for b in range(NB_RKV + 1 + l):
                    n = ZMIX[l] + b
                    if n >= N_RAW:
                        act.wait_ge(mix_done, n - N_RAW + 1)
                    rows = VR if b > NB_RKV else slice(0, P)
                    evac(raw[rows, n % N_RAW, 1:SEQ + 1], rows=rows)
                act.wait_ge(mix_done, ZMIX[l] + NB_RKV + 1)
                act.activation(lora_in[0:32, :], lora_in[0:32, :], ACT.Tanh).then_inc(lora_ready, 1)
                act.activation(lora_in[64:P, :], lora_in[64:P, :], ACT.Sigmoid).then_inc(lora_ready, 1)
                act.wait_ge(sigt_ps, l + 1)
                act.activation(scr[:, 6144:7168], ps_t[:, 5 * 512:7 * 512], ACT.Sigmoid).then_inc(sigt_ready, 1)
                for b in range(4):
                    evac(a_b[:, b, :], ACT.Sigmoid, bias=pcol(l, "a0", b))
                for b in range(4):
                    evac(gg[:, b, :])
                for b in range(4 * l):
                    evac(bon[:, b, :], ACT.Sigmoid, bias=pcol(l, "v0", b))
                act.wait_ge(kk_ready, 4 * (l + 1))
                act.activation(e1[:, :, :], kk_a[:, :, :], ACT.Square).then_inc(kksq_ready, 1)
                root(inv4_t)
                act.wait_ge(cum_ps, l + 1)
                act.wait_ge(zd_ready, ZD[l, "kk"] + 4)
                act.activation(scr[:, 0:1024], ps_t[:, 6 * 512:8 * 512], ACT.Exp, scale=-DECAY).then_inc(decay_ready, 1)
                act.wait_ge(zd_ready, ZD[l, "bonus"] + 4)
                act.activation(scr[:, 1024:2048], ps_t[:, 4 * 512:6 * 512], ACT.Exp, scale=DECAY).then_inc(decay_ready, 1)
                act.wait_ge(decay_used, l + 1)
                act.activation(scr[:, 0:1024], ps_t[:, 4 * 512:6 * 512], ACT.Exp, scale=-DECAY).then_inc(decay_ready, 1)
                for b in range(KC // 2):
                    evac(gate_r[:, b, :], ACT.Sigmoid)
                act.wait_ge(pool_ps, l + 1)
                for b in range(2):
                    for q in range(2):
                        r = slice(64 * q, 64 * q + 64)
                        act.activation(pa3[r, b, PAD_P:], ps_t[r, 512 * (6 + q) + SEQ * b:512 * (6 + q) + SEQ * (b + 1)],
                                       ACT.Identity, scale=pcol(l, "pool_scale", b, 64 * q, 64 * q + 64)).then_inc(pool_y, 1)
                for b in range(KC):
                    if b >= 2:
                        act.wait_ge(zd_free, ZD[l, "y_pool"] + b - 1)
                    evac(sg[:, b % 2, :], ACT.Sigmoid)
                    if b == 1:
                        act.wait_ge(conv_dev, 2 * (l + 1))
                        act.activation(cb_t[:, :], cy_t[:, :], ACT.Square).then_inc(conv_sq, 1)
                    if b == 3:
                        root(rstd[:, :])
                    if b == 5:
                        act.wait_ge(conv_un, 2 * (l + 1))
                        act.activation(cb_t[:, :], cy_t[:, :], ACT.Sigmoid).then_inc(conv_sg, 1)
                for b in range(KC):
                    act.wait_ge(zd_free, ZD[l, "y_pool"] + KC + b - 1)
                    evac(sg[:, b % 2, :], ACT.Sigmoid)
                for hf in range(NT):
                    wkv_half(l, hf)
                for b in range(4):
                    act.wait_ge(o_dev, 4 * l + b + 1)
                    act.activation(e1[:, b, :], o_all[:, b, :], ACT.Square).then_inc(o_sq, 1)
                evac(gate_r[:, KC // 2, :], ACT.Sigmoid)
                root(inv4_t)
                for b in range(KC // 2 + 1, KC):
                    evac(gate_r[:, b, :], ACT.Sigmoid)

            def wkv_half(l, hf):
                k = 2 * l + hf
                for i, kind in enumerate((0, 2)):
                    act.wait_ge(tok_ps, 4 * k + 2 * i + 1)
                    act.activation(tok[:, kind, :], bank(6), ACT.Identity).then_inc(tok_a_ready, 1)
                for m in range(1, LEVELS):
                    for g in range(2):
                        n = (k * (LEVELS - 1) + m - 1) * 2 + g
                        act.wait_ge(p_ps, n + 1)
                        act.activation(p_sb[:, 4 * g:4 * g + 4, :], bank(g), ACT.Identity).then_inc(p_ready, 1)
                    if m == 2:
                        act.wait_ge(akv_ps, k + 1)
                        act.activation(akv[:, :, :], bank(7), ACT.Identity).then_inc(akv_ready, 1)
                act.wait_ge(ht_ps, k + 1)
                act.activation(ht_sb[:, :, :], bank(6), ACT.Identity).then_inc(ht_ready, 1)
                act.wait_ge(g_ps, k + 1)
                act.activation(g_sb[:, :, :], bank(7), ACT.Identity).then_inc(g_ready, 1)
                for c in range(2):
                    act.wait_ge(o3_ps, 2 * k + c + 1)
                    for q in range(2):
                        r = slice(64 * q, 64 * q + 64)
                        act.activation(o_state[r, :, 128 * hf + 64 * c:128 * hf + 64 * c + 64],
                                       ps_t[r, 512 * (6 + q):512 * (6 + q) + 256], ACT.Identity).then_inc(o3_ready, 1)

            def hi(n, slot, full):
                act.wait_ge(piece_full[slot], full)
                if not isinstance(n, int) or n >= N_SPLIT:
                    act.wait_ge(piece_used, n - N_SPLIT + 1)
                act.activation(w_hi[:, slot % N_SPLIT, :], pieces[:, slot, :], ACT.Identity).then_inc(hi_ready, 1)

            def sigmoid_t(n, t, width):
                act.activation(sig_sb[:, t, 0:width], bank(2 * t, width), ACT.Sigmoid).then_inc(sig_ready[t], 1)

            def turned_t(n, t, width):
                act.wait_ge(actt_ps[t], n + 1)
                act.activation(act_hi[:, t, 0:width], bank(2 * t, width), ACT.Identity).then_inc(act_hi_ready[t], 1)

            def ffn_block(n, nxt, full):
                act.wait_ge(tile0_ps, 2 * n + 1)
                sigmoid_t(n, 0, FB)
                act.wait_ge(piece_used, 3 * n + 1)
                sigmoid_t(n, 1, FB)
                for part in range(3):
                    if nxt is not None:
                        hi(3 * n + 3 + part, nxt + part, full)
                    if part < 2:
                        turned_t(n, part, FB)

            def hi_of(m, i):
                hi(piece_at(m) + i, i % N_RAW_P, 16 * (FULL0[i % N_RAW_P] + i // N_RAW_P + 1) + 32 * m)

            def moe_block(m, first=0):
                n = N_FFB + m
                for i in range(first, MOE_PIECES):
                    hi_of(m, i)
                    if i == 4:
                        sigmoid_t(n, 0, EB)
                    if i == 8:
                        sigmoid_t(n, 1, EB)
                        turned_t(n, 0, EB)
                turned_t(n, 1, EB)

            act.wait_ge(par_in, 16)
            act.activation(c_sig[:, :], par[:, P_C:P_C + KC], ACT.Sigmoid).then_inc(c_sig_ready, 1)
            mixer(0)
            square_x(1)
            hi(0, 0, 16)
            root(rstd[:, :])
            shifted(1, f_hi, f_hi_ready)
            for part in range(1, 3):
                hi(part, part, 16)
            with act.Fori(0, N_FFB // 2) as it:
                ffn_block(2 * it, 3, 16 * (it + 1))
                ffn_block(2 * it + 1, 0, 16 * (it + 2))
            ffn_block(N_FFB - 1, None, None)
            act.wait_ge(piece_used, N_FFN_P)
            act.activation(tokm[:, 0, :], ps_t[:, 2048:3072], ACT.Identity).then_inc(f_ytok, 1)
            mixer(1)
            norm_in(3)
            hi_of(0, 0)
            act.wait_ge(htok_ps, 1)
            act.activation(tok_hi[:, :, :], ps_t[:, 2048:4096], ACT.Identity).then_inc(htok_ready, 1)
            act.wait_ge(r_maxed, 2)
            act.activation(r_exp[:, :], r_exp[:, :], ACT.Exp).then_inc(r_exped, 1)
            hi_of(0, 1)
            hi_of(0, 2)
            def tokens_hi(pair):
                for c in range(2):
                    act.wait_ge(gather_ps, 2 * pair + c + 1)
                    act.activation(f_hi[:, 4 * c:4 * c + 4, :], ps_t[:, 1024 * c:1024 + 1024 * c],
                                   ACT.Identity).then_inc(f_hi_ready, 1)

            tokens_hi(0)
            act.wait_ge(jobs_ready, 1)
            last_pair = act.value_load(job_i[0:1, N_JOBS + 3:N_JOBS + 4], min_val=NE // 2 - 1, max_val=N_JOBS // 2 - 1)

            def pair_of_jobs(pair, more):
                moe_block(pair * N_EB, N_SPLIT)
                with act.Fori(1, N_EB) as b:
                    moe_block(pair * N_EB + b)
                if more:
                    hi_of((pair + 1) * N_EB, 0)
                act.wait_ge(selt_ready, 2 * (pair + 1))
                for s in range(2):
                    act.wait_ge(piece_used, piece_at((pair + 1) * N_EB) - 2 * (1 - s))
                    act.activation(y_hi[:, s, :], ps_t[:, 2048 + 1024 * s:3072 + 1024 * s], ACT.Identity,
                                   scale=slot_gate[:, s:s + 1]).then_inc(y_hi_ready, 1)
                    if more:
                        hi_of((pair + 1) * N_EB, 1 + s)
                if more:
                    tokens_hi(pair + 1)

            with act.Fori(0, last_pair) as pair:
                pair_of_jobs(pair, True)
            pair_of_jobs(last_pair, False)
            square_x(4)
            root(rstd[:, :])
            for t in range(NT):
                act.wait_ge(out_ps, t + 1)
                act.activation(tokm[:, t, :], ps_t[:, 1024 * t:1024 * (t + 1)], ACT.Identity).then_inc(out_rows, 1)

        @block.vector
        def _(dve):
            chain, zd, ada_n = [0], [0], [0]

            def link(ins):
                chain[0] += 1
                ins.then_inc(dve_chain, 1)
                dve.wait_ge(dve_chain, chain[0])

            def take():
                n = zd[0]
                zd[0] += 1
                dve.wait_ge(zd_ready, n + 1)
                return bank(2 + n % 2, SEQ)

            roots = [0]

            def inverse(a, last):
                if last is not None:
                    link(last)
                roots[0] += 1
                dve.reciprocal(a, a).then_inc(inv_in, 1)

            def ada_steps(count):
                for _ in range(count):
                    n = ada_n[0]
                    ada_n[0] += 1
                    li, t, k = n // 24, n // KC % 3, n % KC
                    acc = ada_acc[:, 1024 * t:1024 * (t + 1)]
                    lead = n < ADA_LEAD
                    if lead:
                        dve.wait_ge(lead_full[n // 4], 16)
                        chunk, used = ring[:, 1024 * n:1024 * (n + 1)], lead_used
                    else:
                        dve.wait_ge(ada_full[n % 3], 16 * ((n - ADA_LEAD) // 3 + 1))
                        chunk, used = ada_ring[:, n % 3, :], ada_free
                    if k == 0:
                        if li > 0:
                            dve.wait_ge(mod_ps, 1 if li == 1 and t < 2 else li + 1)
                        ins = dve.tensor_scalar(acc, chunk, c_silu[:, k:k + 1], None, ALU.mult)
                    else:
                        dve.wait_ge(*((lead_used, n) if n <= ADA_LEAD else (ada_free, 3 + n - ADA_LEAD)))
                        ins = dve.scalar_tensor_tensor(out=acc, in0=chunk, scalar=c_silu[:, k:k + 1],
                                                       in1=acc, op0=ALU.mult, op1=ALU.add)
                    ins.then_inc(used, 1)

            def finish_mods(li, part=None):
                l, i = divmod(li, 2)
                c0, c1 = ((0, 16), (16, 24), (0, 24))[2 if part is None else part]
                dve.wait_ge(mod_ps, li + 2 if part is None else part + 1)
                o = l * P_W + P_OFF["ada_b"] + 24 * i
                ins = dve.tensor_tensor(mods[:, li, c0:c1], bank(7, 24)[:, c0:c1], par[:, o + c0:o + c1], ALU.add)
                if part == 1:
                    ins.then_inc(mods_ready, 1)
                    return
                link(ins)
                o = l * P_W + P_OFF["norm_g"] + 8 * i
                dve.scalar_tensor_tensor(out=gain[:, li, :], in0=mods[:, li, 8:16], scalar=1.0,
                                         in1=par[:, o:o + 8], op0=ALU.add, op1=ALU.mult).then_inc(mods_ready, 1)

            def norm_root(li):
                dve.wait_ge(ssum_ps, li + 1)
                inverse(rstd[:, :], dve.tensor_scalar(rstd[:, :], bank(4, SEQ), 1e-6, None, ALU.add))

            def norm_scale(gains, done):
                dve.wait_ge(rstd_ready, roots[0])
                for k in range(KC):
                    dve.scalar_tensor_tensor(out=hT[:, k, :], in0=xT[:, k, :], scalar=gains[:, k:k + 1],
                                             in1=rstd[:, :], op0=ALU.mult, op1=ALU.mult).then_inc(done, 1)

            def norm_in(li):
                if li > 0:
                    norm_root(li)
                if li == 1:
                    lo(0, 0)
                dve.wait_ge(mods_ready, li + 2 if li else 1)
                norm_scale(gain[:, li, :], hs_ready)

            def mix_shift(l):
                for b in range(NB_RKV + 1 + l):
                    n = ZMIX[l] + b
                    rows = VR if b > NB_RKV else slice(0, P)
                    dst = rkv[:, b, :] if b < NB_RKV else (lora_in, vres_in)[b - NB_RKV][rows, :]
                    mu = pcol(l, "mu", b) if b <= NB_RKV else pcol(l, "vmu", 0, 64, 80)
                    z = raw[rows, n % N_RAW, :]
                    dve.wait_ge(za_done, ZA[l, "z"] + b + 1)
                    link(dve.tensor_tensor(tmp[rows, :], z[:, 0:SEQ], z[:, 1:SEQ + 1], ALU.subtract))
                    dve.scalar_tensor_tensor(out=dst, in0=tmp[rows, :], scalar=mu, in1=z[:, 1:SEQ + 1],
                                             op0=ALU.mult, op1=ALU.add).then_inc(mix_done, 1)
                    dve.wait_ge(mix_done, n + 1)
                    if 4 <= b < 8:
                        dve.tensor_scalar(kk_a[:, b - 4, :], dst, pcol(l, "kk_scale", b - 4), None, ALU.mult
                                          ).then_inc(kk_ready, 1)
                    if l == 0 and b < NB_RKV:
                        ada_steps(2 if b < 4 else ADA_Z)
                    if b < NB_RKV:
                        conv_taps(l, 1 + TAPS[l][b], 1 + TAPS[l][b + 1])
                    if l == 0 and b == 9:
                        finish_mods(0, 1)

            def rwkv_inputs(l):
                dve.wait_ge(za_done, ZA[l, "a"] + 4)
                for b in range(4):
                    link(dve.tensor_scalar(tmp[:, :], a_b[:, b, :], 1.0, pcol(l, "ka", b), ALU.subtract, ALU.mult))
                    dve.wait_ge(kk_ready, 4 * (l + 1))
                    link(dve.scalar_tensor_tensor(out=kkv[:, b, :], in0=tmp[:, :], scalar=1.0, in1=kkv[:, b, :],
                                                  op0=ALU.add, op1=ALU.mult))
                for b in range(4):
                    link(dve.scalar_tensor_tensor(out=e2[:, b, :], in0=rr[:, b, :], scalar=pcol(l, "rk", b),
                                                  in1=kkv[:, b, :], op0=ALU.mult, op1=ALU.mult))
                dve.tensor_copy(tmp[:, 0:1], e2[:, 3, 0:1]).then_inc(rkk_ready, 1)
                if l == 0:
                    link(dve.tensor_copy(v_first[:, :], rkv_t[:, 8 * SEQ:12 * SEQ]))
                else:
                    dve.wait_ge(za_done, ZA[l, "vres"] + 4)
                    v1 = rkv_t[:, 8 * SEQ:12 * SEQ]
                    link(dve.tensor_tensor(v_first[:, :], v_first[:, :], v1, ALU.subtract))
                    link(dve.tensor_tensor(v_first[:, :], v_first[:, :], scr[:, 5120:6144], ALU.mult))
                    link(dve.tensor_tensor(v1, v1, v_first[:, :], ALU.add))
                for b in range(4):
                    dve.tensor_scalar(inv4[:, b, :], take(), 1e-24, None, ALU.max).then_inc(zd_free, 1)
                dve.wait_ge(zd_free, zd[0])
                inverse(inv4_t, None)
                for b in range(4):
                    dve.tensor_tensor(bon[:, b, :], take(), vv[:, b, :], ALU.mult).then_inc(zd_free, 1)
                dve.wait_ge(rstd_ready, roots[0])
                link(dve.tensor_tensor(kk_a, kk_a, inv4, ALU.mult))
                dve.wait_ge(decay_ready, 3 * l + 1)
                link(dve.tensor_tensor(a_b, a_b, kk_a, ALU.mult))
                dve.scalar_tensor_tensor(out=kk_a, in0=kk_a, scalar=-1.0, in1=e1, op0=ALU.mult, op1=ALU.mult
                                         ).then_inc(decay_used, 1)
                dve.wait_ge(decay_ready, 3 * l + 2)
                link(dve.tensor_tensor(a_b, a_b, e2, ALU.mult))
                link(dve.tensor_tensor(kkv, kkv, e2, ALU.mult))
                dve.wait_ge(decay_ready, 3 * l + 3)
                link(dve.tensor_copy(chunk_decay[:, :].rearrange("p (b c) -> p b c", b=4), e1[:, :, CH - 1:SEQ:CH]))
                dve.tensor_tensor(rr, rr, e1, ALU.mult).then_inc(tilde_ready, 1)

            def conv_start(l):
                dve.wait_ge(za_done, ZA[l, "pc"] + 6)
                link(dve.tensor_tensor(ca[:, :, PAD_C:], ca[:, :, PAD_C:], cb, ALU.mult))
                for b in range(2):
                    link(dve.tensor_scalar(cy[:, b, :], ca[:, b, 0:SEQ], pcol(l, "conv_w", b * CONV_K),
                                           pcol(l, "conv_b", b), ALU.mult, ALU.add))

            def conv_taps(l, first, last):
                for j in range(first, last):
                    for b in range(2):
                        ins = dve.scalar_tensor_tensor(out=cy[:, b, :], in0=ca[:, b, j:j + SEQ],
                                                       scalar=pcol(l, "conv_w", b * CONV_K + j), in1=cy[:, b, :],
                                                       op0=ALU.mult, op1=ALU.add)
                        if j < CONV_K - 1:
                            link(ins)
                        else:
                            ins.then_inc(conv_u, 1)

            def conv_norm(l, step):
                if step == 0:
                    dve.wait_ge(conv_mean, l + 1)
                    dve.wait_ge(conv_u, 2 * (l + 1))
                    for b in range(2):
                        dve.tensor_tensor(cy[:, b, :], cy[:, b, :], bank(4, SEQ), ALU.subtract).then_inc(conv_dev, 1)
                if step == 1:
                    dve.wait_ge(conv_var, l + 1)
                    inverse(rstd[:, :], dve.tensor_scalar(rstd[:, :], bank(5, SEQ), 1e-5, None, ALU.add))
                if step == 2:
                    dve.wait_ge(rstd_ready, roots[0])
                    dve.wait_ge(conv_dev, 2 * (l + 1))
                    for b in range(2):
                        link(dve.tensor_tensor(cy[:, b, :], cy[:, b, :], rstd[:, :], ALU.mult))
                        dve.tensor_scalar(cy[:, b, :], cy[:, b, :], pcol(l, "ln_g", b), pcol(l, "ln_b", b),
                                          ALU.mult, ALU.add).then_inc(conv_un, 1)
                if step == 3:
                    dve.wait_ge(conv_sg, l + 1)
                    dve.wait_ge(conv_un, 2 * (l + 1))
                    dve.tensor_tensor(cy, cy, cb, ALU.mult).then_inc(conv_y, 1)

            def wkv_half(l, hf):
                k = 2 * l + hf
                tri_s, tri_i = (cc(c).unsqueeze(1).broadcast_to([P, 4, P]) for c in (C_TRI_S, C_TRI_I))
                low0, lvl0, eye = (cc(c).unsqueeze(1).broadcast_to([P, 4, P]) for c in (C_LOW0, C_LVL, C_ID))

                def heads(b):
                    return bank(b).rearrange("p (n w) -> p n w", w=P)

                for g in range(2):
                    h4 = slice(4 * g, 4 * g + 4)
                    dve.wait_ge(amat_ps, 2 * k + g + 1)
                    link(dve.tensor_tensor(ltm[:, h4, :], heads(2 + g), tri_s, ALU.mult))
                    dve.tensor_tensor(ak_t[:, h4, :], heads(4 + g), tri_s, ALU.mult).then_inc(amat_ready, 1)
                    link(dve.tensor_tensor(tinv[:, h4, :], heads(g), low0, ALU.mult))
                    link(dve.tensor_tensor(tinv_t[:, h4, :], ltm[:, h4, :], lvl0, ALU.mult))
                    dve.tensor_tensor(tinv[:, h4, :], tinv[:, h4, :], eye, ALU.add).then_inc(t_ready, 1)
                    dve.tensor_tensor(tinv_t[:, h4, :], tinv_t[:, h4, :], eye, ALU.add).then_inc(t_ready, 1)
                base = k * T_INC
                for i, kind in enumerate((1, 3)):
                    dve.wait_ge(tok_ps, 4 * k + 2 * i + 2)
                    dve.tensor_copy(tok[:, kind, :], bank(7)).then_inc(tok_d_ready, 1)
                for m in range(1, LEVELS):
                    for g in range(2):
                        h4 = slice(4 * g, 4 * g + 4)
                        dve.wait_ge(dt_ps, (k * (LEVELS - 1) + m - 1) * 2 + g + 1)
                        dve.wait_ge(t_ready, base + 4 * m)
                        if m < LEVELS - 1:
                            dve.tensor_tensor(tinv[:, h4, :], tinv[:, h4, :], heads(2 + g), ALU.add).then_inc(t_ready, 1)
                        else:
                            dve.sem_inc(t_ready, 1)
                        dve.tensor_tensor(tinv_t[:, h4, :], tinv_t[:, h4, :], heads(4 + g), ALU.add).then_inc(t_ready, 1)
                for g in range(2):
                    h4 = slice(4 * g, 4 * g + 4)
                    dve.wait_ge(rb_ps, 2 * k + g + 1)
                    dve.tensor_tensor(lvl_l[:, h4, :], heads(g), tri_i, ALU.mult).then_inc(rb_ready, 1)
                    dve.tensor_tensor(ak_t[:, h4, :], heads(2 + g), tri_i, ALU.mult).then_inc(rb_ready, 1)
                for c in range(2):
                    n = 2 * k + c
                    r = slice(64 * c, 64 * c + 64)
                    dve.wait_ge(u_ps, n + 1)
                    dve.wait_ge(g_ready, k + 1)
                    for g in range(2):
                        dve.tensor_tensor(u_sb[r, 4 * g:4 * g + 4, :],
                                          ps_t[r, 512 * (4 + g):512 * (4 + g) + 256].rearrange("p (n w) -> p n w", w=64),
                                          g_sb[r, 4 * g:4 * g + 4, :], ALU.add).then_inc(u_ready, 1)
                    dve.wait_ge(s_ps, n + 1)
                    link(dve.tensor_tensor(state_t[:, :], state_t[:, :], bank(0, 256), ALU.add))
                    wc = chunk_decay[:, :].rearrange("p (b c) -> p b c", b=4)[:, :, 2 * hf + c:2 * hf + c + 1]
                    dve.tensor_tensor(state, state, wc.broadcast_to([P, 4, 64]), ALU.mult).then_inc(s_ready, 1)
                dve.wait_ge(o_ps, k + 1)
                dve.wait_ge(o3_ready, 4 * (k + 1))
                dve.tensor_tensor(o_all[:, :, P * hf:P * hf + P], bank(1).rearrange("p (n w) -> p n w", w=P),
                                  o_state[:, :, P * hf:P * hf + P], ALU.add).then_inc(o_ready, 1)

            def rwkv_out(l):
                dve.wait_ge(o_ready, 2 * (l + 1))
                for b in range(4):
                    dve.scalar_tensor_tensor(out=o_all[:, b, :], in0=take(), scalar=-1.0 / 64, in1=o_all[:, b, :],
                                             op0=ALU.mult, op1=ALU.add).then_inc(zd_free, 1)
                    dve.wait_ge(zd_free, zd[0])
                    dve.sem_inc(o_dev, 1)
                for b in range(4):
                    dve.tensor_scalar(inv4[:, b, :], take(), 1.0 / 64, 64e-5, ALU.mult, ALU.add).then_inc(zd_free, 1)
                dve.wait_ge(zd_free, zd[0])
                inverse(inv4_t, None)
                dve.wait_ge(rstd_ready, roots[0])
                link(dve.tensor_tensor(o_all, o_all, inv4, ALU.mult))
                for b in range(4):
                    link(dve.tensor_scalar(o_all[:, b, :], o_all[:, b, :], pcol(l, "lnx_g", b), pcol(l, "lnx_b", b),
                                           ALU.mult, ALU.add))
                link(dve.tensor_tensor(o_all, o_all, bon, ALU.add))
                dve.tensor_tensor(o_all, o_all, gg, ALU.mult).then_inc(o_final, 1)

            def mixer(l):
                norm_in(2 * l)
                conv_start(l)
                mix_shift(l)
                rwkv_inputs(l)
                if l == 0:
                    ada_steps(3 * KC - (NB_RKV - 4) * ADA_Z)
                    conv_taps(l, 1 + TAPS[l][NB_RKV], CONV_K)
                for b in range(KC):
                    src = take()
                    dve.wait_ge(za_done, ZA[l, "gate_p"] + b + 1)
                    dve.tensor_tensor(merged[:, b, :], src, sg[:, b % 2, :], ALU.mult).then_inc(zd_free, 1)
                    if b in (1, 3, 4, 6):
                        conv_norm(l, (1, 3, 4, 6).index(b))
                    if b == 0 and l == 0:
                        finish_mods(1)
                    if b > 0:
                        ada_steps(2)
                for b in range(KC):
                    src = take()
                    dve.wait_ge(za_done, ZA[l, "gate_c"] + b + 1)
                    dve.tensor_tensor(tmp[:, :], src, sg[:, b % 2, :], ALU.mult).then_inc(zd_free, 1)
                    dve.wait_ge(zd_free, zd[0])
                    link(dve.tensor_tensor(merged[:, b, :], merged[:, b, :], tmp[:, :], ALU.add))
                    ada_steps(2 if b < 2 else 1)
                finish_mods(2 + l)
                dve.memset(state_t[:, :], 0.0).then_inc(s_ready, 1)
                dve.wait_ge(s_ready, 5 * l + 1)
                for hf in range(NT):
                    wkv_half(l, hf)
                rwkv_out(l)
                for b in range(KC):
                    if b >= 1:
                        dve.wait_ge(merged_ready, KC * l + b)
                    src = take()
                    dve.wait_ge(za_done, ZA[l, "gate_r2"] + max(b + 1 - KC // 2, 0))
                    dve.tensor_tensor(tmp[:, :], src, gate_r[:, b, :], ALU.mult).then_inc(zd_free, 1)
                    dve.wait_ge(zd_free, zd[0])
                    dve.tensor_tensor(merged[:, b, :], merged[:, b, :], tmp[:, :], ALU.add).then_inc(merged_ready, 1)
                for b in range(KC):
                    dve.scalar_tensor_tensor(out=xT[:, b, :], in0=take(), scalar=mods[:, 2 * l, 16 + b:17 + b],
                                             in1=xT[:, b, :], op0=ALU.mult, op1=ALU.add).then_inc(zd_free, 1)
                    dve.wait_ge(zd_free, zd[0])
                    dve.sem_inc(x_ready, 1)

            def lo(n, slot):
                dve.wait_ge(hi_ready, n + 1)
                dve.tensor_tensor(w_lo[:, slot % N_SPLIT, :], pieces[:, slot, :],
                                  w_hi[:, slot % N_SPLIT, :].bitcast(f32), ALU.subtract).then_inc(split_ready, 1)

            def silu_t(n, t, width):
                dve.wait_ge(sig_ready[t], n + 1)
                dve.tensor_tensor(sig_sb[:, t, 0:width], sig_sb[:, t, 0:width], bank(2 * t, width), ALU.mult
                                  ).then_inc(silu_ready[t], 1)

            def act_of(n, t, width):
                dve.wait_ge(silu_ready[t], n + 1)
                dve.tensor_tensor(act_sb[:, t, 0:width], sig_sb[:, t, 0:width], bank(2 * t + 1, width), ALU.mult
                                  ).then_inc(act_ready[t], 1)

            def turned_lo(n, t, width):
                dve.wait_ge(act_hi_ready[t], n + 1)
                dve.tensor_tensor(act_lo[:, t, 0:width], bank(2 * t, width), act_hi[:, t, 0:width].bitcast(f32),
                                  ALU.subtract).then_inc(act_lo_ready[t], 1)

            def ffn_block(n, nxt):
                silu_t(n, 0, FB)
                silu_t(n, 1, FB)
                dve.wait_ge(tile0_ps, 2 * n + 2)
                act_of(n, 0, FB)
                if nxt is not None:
                    lo(3 * n + 3, nxt)
                dve.wait_ge(piece_used, 3 * n + 2)
                act_of(n, 1, FB)
                turned_lo(n, 0, FB)
                if nxt is not None:
                    lo(3 * n + 4, nxt + 1)
                turned_lo(n, 1, FB)
                if nxt is not None:
                    lo(3 * n + 5, nxt + 2)

            def moe_block(m, first=0):
                n, p0 = N_FFB + m, piece_at(m)
                for i in range(first, MOE_PIECES):
                    lo(p0 + i, i % N_RAW_P)
                    if i == 5:
                        silu_t(n, 0, EB)
                        dve.wait_ge(piece_used, p0 + 4)
                        act_of(n, 0, EB)
                    if i == 8:
                        turned_lo(n, 0, EB)
                        silu_t(n, 1, EB)
                    if i == 9:
                        dve.wait_ge(piece_used, p0 + 8)
                        act_of(n, 1, EB)
                turned_lo(n, 1, EB)

            dve.memset(raw_t[:, :], 0.0)
            dve.memset(pu[:, :], 0.0)
            dve.memset(pa[:, :], 0.0)
            dve.memset(pbuf[:, :], 0.0)
            dve.memset(ca_t[:, :], 0.0).then_inc(pads_ready, 1)
            dve.sem_inc(ada_free, 3)
            dve.wait_ge(c_sig_ready, 1)
            link(dve.tensor_tensor(c_silu[:, :], c_sig[:, :], par[:, P_C:P_C + KC], ALU.mult))
            for t in range(NT):
                dve.wait_ge(xt_ps, t + 1)
                src = ps_t[:, 1024 * t:1024 * (t + 1)].rearrange("p (k n) -> p k n", n=P)
                dve.tensor_copy(xT[:, :, P * t:P * t + P], src).then_inc(x_ready, KC // NT)
            ada_steps(2)
            norm_root(0)
            ada_steps(2 * KC - 2)
            finish_mods(0, 0)
            mixer(0)
            norm_in(1)
            for k in range(KC):
                dve.wait_ge(f_hi_ready, k + 1)
                dve.scalar_tensor_tensor(out=f_lo[:, k, :], in0=hT[:, k, :], scalar=mods[:, 1, k:k + 1],
                                         in1=f_hi[:, k, :].bitcast(f32), op0=ALU.add, op1=ALU.subtract
                                         ).then_inc(f_lo_ready, 1)
            for part in range(1, 3):
                lo(part, part)
            with dve.Fori(0, N_FFB // 2) as it:
                ffn_block(2 * it, 3)
                ffn_block(2 * it + 1, 0)
            ffn_block(N_FFB - 1, None)
            dve.wait_ge(piece_used, N_FFN_P)
            dve.tensor_copy(tokm[:, 1, :], ps_t[:, 3072:4096]).then_inc(f_ytok, 1)
            for k in range(KC):
                dve.wait_ge(f_tr, 2 * (k // 2) + 2)
                dve.scalar_tensor_tensor(out=xT[:, k, :], in0=ps_t[:, SEQ * k:SEQ * (k + 1)],
                                         scalar=mods[:, 1, 16 + k:17 + k], in1=xT[:, k, :],
                                         op0=ALU.mult, op1=ALU.add).then_inc(x_ready, 1)
            mixer(1)
            norm_in(3)

            lg3, sel3, gate3, rank3 = (t[:, :].rearrange("p (t e) -> p t e", e=NE) for t in (lg, r_sel, r_gate, r_rank))
            cmp3, cmq3 = (t[:, :].rearrange("p (t e f) -> p t e f", e=NE, f=NE) for t in (cmp_t, cmp2_t))
            low8 = cst[:, C_LOW8:C_LOW8 + NE * NE].rearrange("p (e f) -> p e f", f=NE)
            iota = cc(C_IOTA)

            def select(pair):
                for t in range(NT):
                    for s in range(2):
                        place = job_rank[:, ds(N_JOBS * t + s + 2 * pair, 1)]
                        weight = job_gate[:, ds(N_JOBS * t + s + 2 * pair, 1)]
                        dve.tensor_scalar(sel[:, t, P * s:P * s + P], iota, place, None, ALU.is_equal
                                          ).then_inc(sel_ready, 1)
                        dve.tensor_scalar(sel_g[:, 2 * t + s, :], iota, place, weight, ALU.is_equal, ALU.mult
                                          ).then_inc(sel_ready, 1)

            dve.memset(merged_t[:, :], 0.0).then_inc(comb_done, 1)
            dve.wait_ge(comb_done, 1)
            lo(piece_at(0), 0)
            dve.wait_ge(logits_ps, 1)
            link(dve.tensor_copy(lg[:, :], bank(0, NT * NE)))
            link(dve.tensor_reduce(r_max[:, :], lg3, AX.X, ALU.max))
            for t in range(NT):
                dve.tensor_scalar(r_exp[:, NE * t:NE * t + NE], lg3[:, t, :], r_max[:, t:t + 1], None, ALU.subtract
                                  ).then_inc(r_maxed, 1)
            for t in range(NT):
                other = lg3[:, t, :].unsqueeze(1).broadcast_to([P, NE, NE])
                own = lg3[:, t, :].unsqueeze(2).broadcast_to([P, NE, NE])
                link(dve.tensor_tensor(cmp3[:, t], other, own, ALU.is_gt))
                link(dve.tensor_tensor(cmq3[:, t], other, own, ALU.is_equal))
                link(dve.tensor_tensor(cmq3[:, t], cmq3[:, t], low8, ALU.mult))
                link(dve.tensor_tensor(cmp3[:, t], cmp3[:, t], cmq3[:, t], ALU.add))
                link(dve.tensor_reduce(r_cnt[:, NE * t:NE * t + NE], cmp3[:, t], AX.X, ALU.add))
            dve.tensor_scalar(r_sel[:, :], r_cnt[:, :], 2.0, None, ALU.is_lt).then_inc(r_sel_ready, 1)
            dve.wait_ge(r_sel_ready, 1)
            dve.wait_ge(r_exped, 1)
            link(dve.tensor_tensor(r_gate[:, :], r_exp[:, :], r_sel[:, :], ALU.mult))
            link(dve.tensor_reduce(r_den[:, :], gate3, AX.X, ALU.add))
            link(dve.reciprocal(r_den[:, :], r_den[:, :]))
            link(dve.tensor_tensor(gate3, gate3, r_den[:, :].unsqueeze(2).broadcast_to([P, NT, NE]), ALU.mult))

            dve.wait_ge(htok_ready, 1)
            for t in range(NT):
                dve.tensor_tensor(tok_lo[t], ps_t[:, 2048 + 1024 * t:3072 + 1024 * t], tok_hi[:, t, :].bitcast(f32),
                                  ALU.subtract).then_inc(tok_lo_ready, 1)

            far = 1024.0
            dve.wait_ge(rank_ps, 1)
            link(dve.scalar_tensor_tensor(out=r_rank[:, :], in0=bank(1, NT * NE), scalar=far, in1=r_sel[:, :],
                                          op0=ALU.add, op1=ALU.mult))
            link(dve.tensor_scalar(r_rank[:, :], r_rank[:, :], far, None, ALU.subtract))
            jr = job_rank[:, :].rearrange("p (t j) -> p t j", j=N_JOBS)
            jg = job_gate[:, :].rearrange("p (t j) -> p t j", j=N_JOBS)
            link(dve.memset(job_rank[:, :], -far))
            link(dve.memset(job_gate[:, :], 0.0))
            link(dve.tensor_copy(jr[:, :, 0:NE], rank3))
            link(dve.tensor_copy(jg[:, :, 0:NE], gate3))
            link(dve.tensor_scalar(over[:, :], ps_t[:, 512 + NT * NE:512 + (NT + 1) * NE], float(P), None, ALU.is_gt))
            select(0)
            link(dve.tensor_tensor(cmp3[:, 0], low8, over[:, :].unsqueeze(1).broadcast_to([P, NE, NE]), ALU.mult))
            link(dve.tensor_reduce(prev[:, :], cmp3[:, 0], AX.X, ALU.add))
            link(dve.memset(job_f[:, :], 0.0))
            link(dve.tensor_copy(job_f[:, 0:NE], cc(C_EID, NE)))
            for q in range(3):
                oh = onehot[:, NE * q:NE * q + NE]
                w8 = cmp_t[:, NE * q:NE * q + NE]
                link(dve.tensor_scalar(oh, prev[:, :], float(q), None, ALU.is_equal))
                link(dve.tensor_tensor(oh, oh, over[:, :], ALU.mult))
                for t in range(NT):
                    link(dve.tensor_tensor(w8, oh, rank3[:, t, :], ALU.mult))
                    link(dve.tensor_reduce(jr[:, t, NE + q:NE + q + 1], w8, AX.X, ALU.add))
                    link(dve.tensor_tensor(w8, oh, gate3[:, t, :], ALU.mult))
                    link(dve.tensor_reduce(jg[:, t, NE + q:NE + q + 1], w8, AX.X, ALU.add))
                link(dve.tensor_tensor(w8, oh, cc(C_EID, NE), ALU.mult))
                link(dve.tensor_reduce(job_f[:, NE + q:NE + q + 1], w8, AX.X, ALU.add))
            link(dve.tensor_scalar(jr[:, :, NE:NE + 3], jr[:, :, NE:NE + 3], float(P), None, ALU.subtract))
            n_over = job_f[:, N_JOBS + 1:N_JOBS + 2]
            link(dve.tensor_reduce(n_over, over[:, :], AX.X, ALU.add))
            link(dve.tensor_scalar(job_f[:, N_JOBS:N_JOBS + 1], n_over, 0.5, float(NE // 2), ALU.is_gt, ALU.add))
            link(dve.tensor_scalar(job_f[:, N_JOBS + 2:N_JOBS + 3], n_over, 2.5, None, ALU.is_gt))
            link(dve.tensor_tensor(job_f[:, N_JOBS:N_JOBS + 1], job_f[:, N_JOBS:N_JOBS + 1],
                                   job_f[:, N_JOBS + 2:N_JOBS + 3], ALU.add))
            link(dve.tensor_scalar(job_f[:, N_JOBS + 3:N_JOBS + 4], job_f[:, N_JOBS:N_JOBS + 1], 1.0, None, ALU.subtract))
            dve.tensor_copy(job_i[0:1, :], job_f[0:1, :]).then_inc(jobs_ready, 1)
            dve.wait_ge(jobs_ready, 1)
            last_pair = dve.value_load(job_i[0:1, N_JOBS + 3:N_JOBS + 4], min_val=NE // 2 - 1, max_val=N_JOBS // 2 - 1)

            def tokens_lo(pair):
                for c in range(2):
                    dve.wait_ge(f_hi_ready, KC + 2 * pair + c + 1)
                    dve.tensor_tensor(f_lo[:, 4 * c:4 * c + 4, :],
                                      ps_t[:, 1024 * c:1024 + 1024 * c].rearrange("p (k n) -> p k n", n=SEQ),
                                      f_hi[:, 4 * c:4 * c + 4, :].bitcast(f32), ALU.subtract).then_inc(f_lo_ready, 1)

            def pair_of_jobs(pair, more):
                dve.wait_ge(selt_ps, pair + 1)
                by_slot = bank(3).rearrange("p (s n) -> p s n", s=2)
                dve.tensor_reduce(slot_gate, by_slot, AX.X, ALU.add).then_inc(selt_ready, 1)
                dve.tensor_scalar(sel_t[:, :, :], by_slot, 0.0, None, ALU.is_gt).then_inc(selt_ready, 1)
                if more:
                    select(pair + 1)
                moe_block(pair * N_EB, N_SPLIT)
                with dve.Fori(1, N_EB) as b:
                    moe_block(pair * N_EB + b)
                nxt = piece_at((pair + 1) * N_EB)
                dve.wait_ge(selt_ready, 2 * (pair + 1))
                for s in range(2):
                    if more:
                        lo(nxt + s, s)
                    dve.wait_ge(y_hi_ready, 2 * pair + s + 1)
                    dve.scalar_tensor_tensor(out=y_lo[:, s, :], in0=ps_t[:, 2048 + 1024 * s:3072 + 1024 * s],
                                             scalar=slot_gate[:, s:s + 1], in1=y_hi[:, s, :].bitcast(f32),
                                             op0=ALU.mult, op1=ALU.subtract).then_inc(y_lo_ready, 1)
                if more:
                    tokens_lo(pair + 1)
                    lo(nxt + 2, 2)
                dve.wait_ge(comb_ps, pair + 1)
                dve.tensor_tensor(merged_t[:, :], merged_t[:, :], ps_t[:, 2048:4096], ALU.add).then_inc(comb_done, 1)
                dve.wait_ge(comb_done, pair + 2)

            tokens_lo(0)
            lo(piece_at(0) + 1, 1)
            lo(piece_at(0) + 2, 2)
            with dve.Fori(0, last_pair) as pair:
                pair_of_jobs(pair, True)
            pair_of_jobs(last_pair, False)
            for k in range(KC):
                dve.scalar_tensor_tensor(out=xT[:, k, :], in0=yT[:, k, :], scalar=mods[:, 3, 16 + k:17 + k],
                                         in1=xT[:, k, :], op0=ALU.mult, op1=ALU.add).then_inc(x_ready, 1)
            dve.wait_ge(x_ready, 5 * KC)
            norm_root(4)
            norm_scale(par[:, P_FG:P_FG + KC], h_ready)

        @block.tensor
        def _(pe):
            za, zd, fill = [0], [0], [0]

            def mm(dst, lhs, rhs, start=True, stop=True, **kw):
                return pe.matmul(dst, lhs, rhs, start=start, stop=stop, **kw)

            def give_za(parts, rows=slice(0, P)):
                n = za[0]
                za[0] += 1
                if n >= 2:
                    pe.wait_ge(za_done, n - 1)
                for i, (lhs, rhs) in enumerate(parts):
                    if n in (ZA[0, "pc"], ZA[1, "pc"]):
                        pe.wait_ge(h_ready, KC * (n > 0) + i + 1)
                    last = mm(bank(n % 2, SEQ)[rows, :], lhs, rhs, i == 0, i == len(parts) - 1)
                last.then_inc(za_ready, 1)

            def give_zd(parts):
                n = zd[0]
                zd[0] += 1
                if n >= 2:
                    pe.wait_ge(zd_free, n - 1)
                for i, (lhs, rhs) in enumerate(parts):
                    last = mm(bank(2 + n % 2, SEQ), lhs, rhs, i == 0, i == len(parts) - 1)
                last.then_inc(zd_ready, 1)

            def landed(n):
                pe.wait_ge(ring_full[FILLS[n][0]], FULL[n])

            def mean_square(li):
                pe.wait_ge(xsq_ready, li + 1)
                for k in range(KC):
                    last = mm(bank(4, SEQ), ones, hT[:, k, :], k == 0, k == KC - 1)
                last.then_inc(ssum_ps, 1)

            def mod_sums(li, part=None):
                c0, c1 = ((0, 16), (16, 24), (0, 24))[2 if part is None else part]
                if part == 0:
                    pe.wait_ge(lead_used, ADA_LEAD)
                if li > 0:
                    pe.wait_ge(mods_ready, li + 1)
                pe.wait_ge(ada_free, 3 + 24 * li + KC * c1 // 8 - ADA_LEAD)
                for c in range(c0, c1):
                    last = mm(bank(7, 24)[:, c:c + 1], ada_acc[:, P * c:P * c + P], cc(C_ONES, 1))
                last.then_inc(mod_ps, 1)

            def z_parts(w, c):
                return [(w[:, k, c:c + P], hT[:, k, :]) for k in range(KC)]

            def z_blocks(l, fills, give=None):
                for i, n_blocks in fills:
                    n = MIX_FILLS * l + i
                    landed(n)
                    w = fill_at(n, P * n_blocks, 0, KC)
                    for b in range(n_blocks):
                        give_za(z_parts(w, P * b))
                        if give is not None:
                            give()

            def mixer(l):
                if l > 0:
                    mean_square(2 * l)
                f0 = MIX_FILLS * l
                z_blocks(l, [(0, 4), (1, 2), (2, 4), (3, 4)])
                if l == 0:
                    mod_sums(0, 1)
                z_blocks(l, [(4, 4), (5, 1)])
                if l > 0:
                    wv = fill_at(f0 + 5, 16, KC * P, KC)
                    give_za([(wv[:, k, :], hT[:, k, :]) for k in range(KC)], rows=VR)
                pe.wait_ge(small_in, SMALL[l])
                pe.wait_ge(lora_ready, 2 * (l + 1))
                for t in range(NT):
                    tk = slice(P * t, P * t + P)
                    mm(bank(5 + t), cc(C_ONES, P, 0, 1), w0_sb[0:1, :], True, False)
                    last = mm(bank(5 + t), lora_in[0:32, tk], lora_w[0:32, :], False, True)
                last.then_inc(sigt_ps, 1)
                for b in range(4):
                    c = slice(P * b, P * b + P)
                    give_za([(lora_w[32:64, c], lora_in[32:64, :])])
                for b in range(4):
                    c = slice(P * b, P * b + P)
                    give_za([(lora_w[64:P, c], lora_in[64:P, :])])
                for b in range(4 * l):
                    c = slice(P * b, P * b + P)
                    pe.wait_ge(mix_done, ZMIX[l] + NB_RKV + 2)
                    give_za([(w0_sb[VR, c], vres_in[VR, :])])
                pe.wait_ge(kksq_ready, l + 1)
                for b in range(4):
                    give_zd([(bones, e1[:, b, :])])
                pe.wait_ge(sigt_ready, l + 1)
                for first, tri in ((4, C_TRI_I), (6, C_TRI_S)):
                    for b in range(4):
                        for t in range(NT):
                            o = 512 * first + SEQ * b + P * t
                            last = mm(ps_t[:, o:o + P], sig_tok[:, t, P * b:P * b + P], cc(tri))
                last.then_inc(cum_ps, 1)
                pe.wait_ge(rkk_ready, l + 1)
                for b in range(4):
                    give_zd([(bones, e2[:, b, :])])
                z_blocks(l, [(6, 4)])
                pe.wait_ge(pooled, 4 * (l + 1))
                pe.wait_ge(decay_ready, 3 * l + 1)
                for b in range(2):
                    for q in range(2):
                        r = slice(64 * q, 64 * q + 64)
                        o = 512 * (6 + q) + SEQ * b
                        last = mm(ps_t[r, o:o + SEQ], pool_wsb[r, 64 * b:64 * b + 64], pl[r, b, :])
                last.then_inc(pool_ps, 1)
                landed(f0 + 8)
                wp, wc = fill_at(f0 + 8, D, 0, 2), fill_at(f0 + 8, D, 2048, 2)
                at = [0]

                def y_pool():
                    b = at[0]
                    at[0] += 1
                    pe.wait_ge(pool_y, 4 * (l + 1))
                    give_zd([(wp[:, k, P * b:P * b + P], pa3[:, k, PAD_P:]) for k in range(2)])
                    if b == 0 and l == 0:
                        mod_sums(1)
                    if b == 1:
                        pe.wait_ge(conv_u, 2 * (l + 1))
                        pe.wait_ge(decay_ready, 3 * (l + 1))
                        for c in range(2):
                            last = mm(bank(4, SEQ), mean256, cy[:, c, :], c == 0, c == 1)
                        last.then_inc(conv_mean, 1)
                    if b == 3:
                        pe.wait_ge(conv_sq, l + 1)
                        for c in range(2):
                            last = mm(bank(5, SEQ), mean256, cb[:, c, :], c == 0, c == 1)
                        last.then_inc(conv_var, 1)

                z_blocks(l, [(7, 4), (9, 4)], y_pool)
                at[0] = 0

                def y_conv():
                    b = at[0]
                    at[0] += 1
                    pe.wait_ge(conv_y, l + 1)
                    give_zd([(wc[:, k, P * b:P * b + P], cy[:, k, :]) for k in range(2)])

                z_blocks(l, [(10, 4), (11, 4)], y_conv)
                mod_sums(2 + l)
                pe.wait_ge(tilde_ready, l + 1)
                for hf in range(NT):
                    wkv_half(l, hf)
                pe.wait_ge(o_ready, 2 * (l + 1))
                for b in range(4):
                    give_zd([(bones, o_all[:, b, :])])
                landed(f0 + 13)
                pe.wait_ge(s_ready, 5 * l + 5)
                wr = fill_at(f0 + 13, 512)
                give_za(z_parts(wr, 0))
                for b in range(4):
                    pe.wait_ge(o_sq, 4 * l + b + 1)
                    give_zd([(bones, e1[:, b, :])])
                for b in range(1, 4):
                    give_za(z_parts(wr, P * b))
                pe.wait_ge(o_final, l + 1)
                landed(f0 + 12)
                w = fill_at(f0 + 12, D)
                for b in range(KC):
                    give_zd([(w[:, k, P * b:P * b + P], o_all[:, k, :]) for k in range(4)])
                landed(f0 + 14)
                landed(f0 + 15)
                pe.wait_ge(merged_ready, KC * (l + 1))
                w0_, w1_ = fill_at(f0 + 14, D), fill_at(f0 + 15, D)
                for b in range(KC):
                    give_zd([((w0_, w1_)[k // 4][:, k % 4, P * b:P * b + P], merged[:, k, :]) for k in range(KC)])

            def wkv_half(l, hf):
                k = 2 * l + hf
                tk = slice(P * hf, P * hf + P)
                base = k * T_INC
                at_, bt_, kt_, rt_, vt_ = kk_a, a_b, kkv, rr, vv
                pe.wait_ge(za_done, ZA[l, "gate_r2"])
                pe.wait_ge(zd_free, ZD[l, "mean"])
                pe.wait_ge(mods_ready, 4 + l)
                if hf == 1:
                    pe.wait_ge(o_ready, k)
                    pe.wait_ge(s_ready, 5 * l + 3)
                for g in range(2):
                    r = slice(64 * g, 64 * g + 64)
                    for b in range(4):
                        o = P * b
                        mm(ps_t[:, 512 * g + o:512 * g + o + P], at_[r, b, tk], bt_[r, b, tk])
                        mm(ps_t[:, 512 * (2 + g) + o:512 * (2 + g) + o + P], bt_[r, b, tk], at_[r, b, tk])
                        last = mm(ps_t[:, 512 * (4 + g) + o:512 * (4 + g) + o + P], kt_[r, b, tk], at_[r, b, tk])
                    last.then_inc(amat_ps, 1)
                for i, src in enumerate((at_, vt_, bt_, kt_)):
                    if i >= 2:
                        pe.wait_ge((tok_a_ready, tok_d_ready)[i - 2], 2 * k + 1)
                    for b in range(4):
                        last = pe.transpose(ps_t[:, 512 * (6 + i % 2) + P * b:512 * (6 + i % 2) + P * b + P],
                                            src[:, b, tk], ident)
                    last.then_inc(tok_ps, 1)
                for m in range(1, LEVELS):
                    n = (k * (LEVELS - 1) + m - 1) * 2
                    for g in range(2):
                        pe.wait_ge(lvl_ready, n + g + 1)
                        pe.wait_ge(t_ready, base + 4 * (m - 1) + 2 * (g + 1))
                        for b in range(4):
                            h = 4 * g + b
                            last = mm(ps_t[:, 512 * g + P * b:512 * g + P * b + P], lvl_l[:, h, :], tinv[:, h, :])
                        last.then_inc(p_ps, 1)
                    if m == 1:
                        pe.wait_ge(amat_ready, 2 * k + 2)
                    for g in range(2):
                        pe.wait_ge(p_ready, n + g + 1)
                        for b in range(4):
                            h = 4 * g + b
                            if m < LEVELS - 1:
                                mm(ps_t[:, 512 * (2 + g) + P * b:512 * (2 + g) + P * b + P], tinv_t[:, h, :], p_sb[:, h, :])
                            last = mm(ps_t[:, 512 * (4 + g) + P * b:512 * (4 + g) + P * b + P], p_sb[:, h, :], tinv_t[:, h, :])
                        last.then_inc(dt_ps, 1)
                    if m == 2:
                        pe.wait_ge(tok_d_ready, 2 * (k + 1))
                        for h in range(8):
                            c = head_col(h)
                            last = mm(ps_t[:, 3584 + 64 * h:3584 + 64 * h + 64], ak_t[:, h, :], tok[:, 1, c:c + 64])
                        last.then_inc(akv_ps, 1)
                pe.wait_ge(t_ready, base + T_INC)
                pe.wait_ge(tok_a_ready, 2 * (k + 1))
                for h in range(8):
                    g, b, c = h // 4, h % 4, head_col(h)
                    last = mm(ps_t[64 * g:64 * g + 64, 3072 + P * b:3072 + P * b + P], tok[:, 0, c:c + 64], tinv_t[:, h, :])
                last.then_inc(ht_ps, 1)
                pe.wait_ge(akv_ready, k + 1)
                for h in range(8):
                    last = mm(ps_t[:, 3584 + 64 * h:3584 + 64 * h + 64], tinv_t[:, h, :], akv[:, h, :])
                last.then_inc(g_ps, 1)
                for g in range(2):
                    r = slice(64 * g, 64 * g + 64)
                    for b in range(4):
                        o = P * b
                        mm(ps_t[:, 512 * g + o:512 * g + o + P], bt_[r, b, tk], rt_[r, b, tk])
                        last = mm(ps_t[:, 512 * (2 + g) + o:512 * (2 + g) + o + P], kt_[r, b, tk], rt_[r, b, tk])
                    last.then_inc(rb_ps, 1)
                for c in range(2):
                    n = 2 * k + c
                    q = slice(64 * c, 64 * c + 64)
                    pe.wait_ge(ht_ready, k + 1)
                    pe.wait_ge(g_ready, k + 1)
                    pe.wait_ge(s_ready, 5 * l + 1 + 2 * hf + c)
                    if c == 1:
                        pe.wait_ge(o3_ready, 2 * n)
                    for g in range(2):
                        r = slice(64 * g, 64 * g + 64)
                        for b in range(4):
                            last = mm(ps_t[q, 512 * (4 + g) + 64 * b:512 * (4 + g) + 64 * b + 64], ht_sb[r, b, q], state[r, b, :])
                    last.then_inc(u_ps, 1)
                    t0 = P * hf + 64 * c
                    for g in range(2):
                        r = slice(64 * g, 64 * g + 64)
                        for b in range(4):
                            last = mm(ps_t[r, 512 * (6 + g) + 64 * b:512 * (6 + g) + 64 * b + 64], state[r, b, :], rt_[r, b, t0:t0 + 64])
                    last.then_inc(o3_ps, 1)
                    pe.wait_ge(u_ready, 2 * (n + 1))
                    pe.wait_ge(rb_ready, 4 * (k + 1))
                    for h in range(8):
                        g, b, hc = h // 4, h % 4, head_col(h)
                        dst = ps_t[64 * g:64 * g + 64, 64 * b:64 * b + 64]
                        mm(dst, tok[q, 2, hc:hc + 64], u_sb[q, h, :], True, False)
                        last = mm(dst, tok[q, 3, hc:hc + 64], tok[q, 1, hc:hc + 64], False, True)
                    last.then_inc(s_ps, 1)
                for h in range(8):
                    g, b, hc = h // 4, h % 4, head_col(h)
                    dst = ps_t[64 * g:64 * g + 64, 512 + P * b:512 + P * b + P]
                    mm(dst, u_sb[:, h, :], lvl_l[:, h, :], True, False)
                    last = mm(dst, tok[:, 1, hc:hc + 64], ak_t[:, h, :], False, True)
                last.then_inc(o_ps, 1)

            def mm3(dst, lhs, rhs, first, last):
                (lh, ll), (rh, rl) = lhs, rhs
                pe.matmul(dst, lh, rh, start=first, stop=False, skip_group_check=True)
                pe.matmul(dst, lh, rl, start=False, stop=False, skip_group_check=True)
                return pe.matmul(dst, ll, rh, start=False, stop=last, skip_group_check=True)

            def tile_in(t, k):
                return f_hi[:, k, P * t:P * t + P], f_lo[:, k, P * t:P * t + P]

            def split_piece(slot, k, w, c=0, n=None):
                a = w * k + c
                return tuple(x[:, slot % N_SPLIT, a:a + (n or w)] for x in (w_hi, w_lo))

            def turn(n, t, width):
                pe.wait_ge(act_ready[t], n + 1)
                for j in range(width // P):
                    last = pe.transpose(ps_t[:, 1024 * t + P * j:1024 * t + P * j + P], act_sb[:, t, P * j:P * j + P], ident)
                last.then_inc(actt_ps[t], 1)

            def down_rows(t, slot, rows, j0, start=False):
                for j in rows:
                    lhs = tuple(x[:, t, P * (j0 + j):P * (j0 + j) + P] for x in (act_hi, act_lo))
                    for c in range(2):
                        last = mm3(bank(4 + 2 * t + c), lhs, split_piece(slot, j, D, 512 * c, 512), start and j == 0, True)
                return last

            def ffn_block(n):
                first = isinstance(n, int) and n == 0
                for part in range(2):
                    pe.wait_ge(split_ready, 3 * n + part + 1)
                    for t in range(NT):
                        if part == 0 and not first:
                            pe.wait_ge(act_lo_ready[t], n)
                            pe.wait_ge(act_ready[t], n)
                        for k in range(KC):
                            if first and part == 0 and t == 0:
                                pe.wait_ge(f_lo_ready, k + 1)
                            last = mm3(bank(2 * t + part, FB), tile_in(t, k), split_piece(part, k, FB), k == 0, k == KC - 1)
                            if part == 1 and t == 1 and k == KC - 3:
                                turn(n, 0, FB)
                        last.then_inc((tile0_ps, piece_used)[t], 1)
                pe.wait_ge(split_ready, 3 * n + 3)
                for t in range(NT):
                    pe.wait_ge(act_lo_ready[t], n + 1)
                    for j in range(FB // P):
                        last = down_rows(t, 2, [j], 0, first)
                        if t == 0 and j == 0:
                            turn(n, 1, FB)
                last.then_inc(piece_used, 1)

            def moe_block(m, pair=None):
                n, p0 = N_FFB + m, piece_at(m)
                for i in range(MOE_PIECES):
                    pe.wait_ge(split_ready, p0 + i + 1)
                    if pair is not None and i == 6:
                        pe.wait_ge(selt_ready, 2 * (pair + 1))
                    if pair is not None and i == 8:
                        pe.wait_ge(comb_done, pair + 1)
                        for c in range(4):
                            mm(bank(4 + c), zeros16[:, 0:P], zeros16[:, 0:512], True, True, skip_group_check=True)
                    if i < 8:
                        t, part, half = i // 4, i % 4 // 2, i % 2
                        if i % 4 == 0:
                            pe.wait_ge(act_lo_ready[t], n)
                            pe.wait_ge(act_ready[t], n)
                        for k in range(KC // 2):
                            last = mm3(bank(2 * t + part), tile_in(t, KC // 2 * half + k), split_piece(i, k, EB),
                                       half == 0 and k == 0, half == 1 and k == KC // 2 - 1)
                    else:
                        t, half = (i - 8) // 2, i % 2
                        if half == 0:
                            pe.wait_ge(act_lo_ready[t], n + 1)
                        last = down_rows(t, i, range(2), 2 * half)
                    last.then_inc(piece_used, 1)
                    if i == 5:
                        turn(n, 0, EB)
                    if i == 8:
                        turn(n, 1, EB)

            pe.wait_ge(cst_in, 16)
            pe.wait_ge(x_in_tok, 16)
            for t in range(NT):
                for k in range(KC):
                    last = pe.transpose(ps_t[:, 1024 * t + P * k:1024 * t + P * k + P], tokm[:, t, P * k:P * k + P], ident)
                last.then_inc(xt_ps, 1)
            mean_square(0)
            mod_sums(0, 0)
            mixer(0)

            mean_square(1)
            pe.wait_ge(zd_free, ZD[0, "end"])
            ffn_block(0)
            with pe.Fori(1, N_FFB) as n:
                ffn_block(n)
            pe.wait_ge(f_ytok, 2)
            for k in range(KC):
                for t in range(NT):
                    last = pe.transpose(ps_t[:, SEQ * k + P * t:SEQ * k + P * t + P], tokm[:, t, P * k:P * k + P], ident)
                last.then_inc(f_tr, 1)
            mixer(1)

            mean_square(3)
            pe.wait_ge(h_ready, KC * 3)
            pe.wait_ge(zd_free, ZD[1, "end"])
            for t in range(NT):
                for k in range(KC):
                    last = mm(bank(0, NT * NE)[:, NE * t:NE * t + NE], hT[:, k, P * t:P * t + P],
                              router_sb[:, NE * k:NE * k + NE], k == 0, k == KC - 1)
            last.then_inc(logits_ps, 1)
            for t in range(NT):
                for k in range(KC):
                    o = 2048 + 1024 * t + P * k
                    last = pe.transpose(ps_t[:, o:o + P], hT[:, k, P * t:P * t + P], ident)
            last.then_inc(htok_ps, 1)
            pe.wait_ge(r_sel_ready, 1)
            rank, half0, half1 = cc(C_RANK), r_sel[:, 0:NE], r_sel[:, NE:2 * NE]
            mm(ps_t[:, 512:512 + NE], rank, half0)
            mm(ps_t[:, 512 + NE:512 + 2 * NE], rank, half1, True, False)
            mm(ps_t[:, 512 + NE:512 + 2 * NE], ones, half0, False, True)
            mm(ps_t[:, 512 + 2 * NE:512 + 3 * NE], ones, half0, True, False)
            mm(ps_t[:, 512 + 2 * NE:512 + 3 * NE], ones, half1, False, True).then_inc(rank_ps, 1)

            pe.wait_ge(tok_lo_ready, NT)

            def spread(dst, lhs):
                for i, (a, b) in enumerate(lhs):
                    last = pe.matmul(dst, a, b, start=i == 0, stop=i == len(lhs) - 1)
                return last

            def gather(pair):
                pe.wait_ge(sel_ready, 8 * (pair + 1))
                for k in range(KC):
                    c = slice(P * k, P * k + P)
                    last = spread(ps_t[:, SEQ * k:SEQ * (k + 1)],
                                  [(tok_hi[:, t, c], sel[:, t, :]) for t in range(NT)]
                                  + [(tok_lo[t][:, c], sel[:, t, :]) for t in range(NT)])
                    if k % 4 == 3:
                        last.then_inc(gather_ps, 1)

            def pair_of_jobs(pair, more):
                pe.wait_ge(f_lo_ready, KC + 2 * (pair + 1))
                for s in range(2):
                    for t in range(NT):
                        o = 1536 + SEQ * s + P * t
                        last = pe.transpose(ps_t[:, o:o + P], sel_g[:, 2 * t + s, :], ident)
                last.then_inc(selt_ps, 1)
                moe_block(pair * N_EB, pair)
                with pe.Fori(1, N_EB) as b:
                    moe_block(pair * N_EB + b)
                if more:
                    gather(pair + 1)
                pe.wait_ge(y_lo_ready, 2 * (pair + 1))
                for k in range(KC):
                    c = slice(P * k, P * k + P)
                    last = spread(ps_t[:, 2048 + SEQ * k:2048 + SEQ * (k + 1)],
                                  [(y[:, s, c], sel_t[:, s, :]) for y in (y_hi, y_lo) for s in range(2)])
                last.then_inc(comb_ps, 1)

            gather(0)
            pe.wait_ge(jobs_ready, 1)
            last_pair = pe.value_load(job_i[0:1, N_JOBS + 3:N_JOBS + 4], min_val=NE // 2 - 1, max_val=N_JOBS // 2 - 1)
            with pe.Fori(0, last_pair) as pair:
                pair_of_jobs(pair, True)
            pair_of_jobs(last_pair, False)

            mean_square(4)
            pe.wait_ge(h_ready, KC * 4)
            for t in range(NT):
                for k in range(KC):
                    o = 1024 * t + P * k
                    last = pe.transpose(ps_t[:, o:o + P], hT[:, k, P * t:P * t + P], ident)
                last.then_inc(out_ps, 1)


def kernel(**inputs):
    import numpy as _np
    import concourse.bacc as _bacc
    from concourse import mybir as _mybir
    from concourse.bass_utils import run_bass_kernel_spmd as _run

    a = {k: _np.ascontiguousarray(v) for k, v in inputs.items()}

    def columns(v):
        return v.reshape(-1, P).T

    params = _np.zeros((P, P_END), _np.float32)
    for l in range(DEPTH):
        parts = {"norm_g": a["norm_g"][l], "ada_b": a["ada_b"][l], "pool_scale": a["pool_scale"][l],
                 "conv_b": a["conv_b"][l], "ln_g": a["conv_ln_g"][l], "ln_b": a["conv_ln_b"][l],
                 "mu": a["rwkv_mu"][l], "a0": a["rwkv_a0"][l], "kk_scale": a["rwkv_kk_scale"][l],
                 "ka": a["rwkv_ka"][l], "rk": a["rwkv_rk"][l], "lnx_g": a["rwkv_lnx_g"][l],
                 "lnx_b": a["rwkv_lnx_b"][l]}
        for name, v in parts.items():
            c = columns(v)
            o = l * P_W + P_OFF[name]
            params[:, o:o + c.shape[1]] = c
        o = l * P_W + P_OFF["conv_w"]
        for b in range(2):
            params[:, o + b * CONV_K:o + (b + 1) * CONV_K] = a["conv_w"][l][:, P * b:P * b + P].T
        if l > 0:
            params[VR, l * P_W + P_OFF["vmu"]] = a["vres_mu"][l - 1]
            o = l * P_W + P_OFF["v0"]
            params[:, o:o + 4] = columns(a["vres_v0"][l - 1])
    params[:, P_C:P_C + KC] = columns(a["c"][0])
    params[:, P_FG:P_FG + KC] = columns(a["final_norm_g"])

    arrays = {
        "x": a["x"][0], "consts": shape_constants(), "params": params, "ada_w": a["ada_w"], "w_in": a["w_in"],
        "pool_w": a["pool_w"], "pool_proj": a["pool_proj"], "conv_proj": a["conv_proj"], "w0": a["rwkv_w0"],
        "w2": a["rwkv_w2"], "a2": a["rwkv_a2"], "g2": a["rwkv_g2"], "rwkv_proj": a["rwkv_proj"],
        "vres_down": a["vres_w_down"], "vres_v2": a["vres_v2"], "w_o": a["w_o"], "ffn_w1": a["ffn_w1"][0],
        "ffn_w3": a["ffn_w3"][0], "ffn_w2": a["ffn_w2"][0], "router": a["moe_router"][0],
        "moe_w1": a["moe_w1"][0], "moe_w3": a["moe_w3"][0], "moe_w2": a["moe_w2"][0],
    }
    nc = _bacc.Bacc("TRN2", target_bir_lowering=False, num_devices=1)
    f32 = _mybir.dt.float32
    args = [nc.dram_tensor(f"in_{n}", v.shape, f32, kind="ExternalInput").ap() for n, v in arrays.items()]
    y = nc.dram_tensor("out_y", (SEQ, D), f32, kind="ExternalOutput").ap()
    build_trunk(nc, *args, y)
    r = _run(nc, [{f"in_{n}": v for n, v in arrays.items()}], core_ids=[0])
    return r.results[0]["out_y"].reshape(1, SEQ, D)
```
